# Optimizing a Trainium2 kernel written in Bass

```python
import math
import jax, jax.numpy as jnp
from jax import lax
import numpy as np

D_MODEL = 1024
BATCH = 1
SEQ = 512
DEPTH = 1

MEM_LEN = 256
EPS = 1e-6
NEG_INF = -1e30
BIG = 1e30

NSA_HEADS = 16
NSA_GROUPS = 4
NSA_HPG = NSA_HEADS // NSA_GROUPS
NSA_DH = 64
NSA_SCALE = NSA_DH ** -0.5
CMP_BLOCK = 32
CMP_STRIDE = 16
CMP_HIDDEN = 128
SEL_BLOCK = 64
SEL_TOPK = 16
N_LOCAL_FORCED = 2
WINDOW = 512
SEL_QBLOCK = 32
WIN_QBLOCK = 128

ML_HEADS = 4
ML_DH = 128
ML_CHUNK = 64
CONV_WIDTH = 4

MEM_HEADS = 4
MEM_DH = 128
MEM_SCALE = MEM_DH ** -0.5

D_FF = -(-8 * D_MODEL // (3 * 256)) * 256

N_BRANCH = 3
NSA_Q = NSA_HEADS * NSA_DH
NSA_KV = NSA_GROUPS * NSA_DH
ML_W = ML_HEADS * ML_DH
MEM_W = MEM_HEADS * MEM_DH
IN_SPLITS = (NSA_Q, 6 * NSA_KV, 3 * NSA_HEADS, 3 * ML_W, 2 * ML_HEADS, ML_W, MEM_W, N_BRANCH * D_MODEL)
IN_WIDTH = NSA_Q + 6 * NSA_KV + 3 * NSA_HEADS + 3 * ML_W + 2 * ML_HEADS + ML_W + MEM_W + N_BRANCH * D_MODEL


def rmsnorm(x, g):
    xf = x.astype(jnp.float32)
    y = xf * lax.rsqrt(jnp.mean(xf * xf, axis=-1, keepdims=True) + EPS)
    return (y * g.astype(jnp.float32)).astype(x.dtype)

def masked_softmax(s, mask):
    s = jnp.where(mask, s.astype(jnp.float32), NEG_INF)
    return jax.nn.softmax(s, axis=-1) * mask

def compress_blocks(kv, pe, w1, w2):
    S = kv.shape[1]
    n_cmp = (S - CMP_BLOCK) // CMP_STRIDE + 1
    idx = jnp.arange(n_cmp)[:, None] * CMP_STRIDE + jnp.arange(CMP_BLOCK)[None, :]
    blocks = kv[:, idx] + pe[None, None, :, None, :]
    hid = jax.nn.silu(jnp.einsum('bnlgd,ldh->bngh', blocks, w1))
    return jnp.einsum('bngh,hd->bngd', hid, w2)

def nsa_compressed(q, k, v, pe_k, w1_k, w2_k, pe_v, w1_v, w2_v):
    S = q.shape[1]
    kc = compress_blocks(k, pe_k, w1_k, w2_k)
    vc = compress_blocks(v, pe_v, w1_v, w2_v)
    n_cmp = kc.shape[1]
    s = jnp.einsum('bsghd,bngd->bghsn', q, kc) * NSA_SCALE
    t = jnp.arange(S)
    end = jnp.arange(n_cmp) * CMP_STRIDE + CMP_BLOCK - 1
    p = masked_softmax(s, end[None, :] <= t[:, None])
    o = jnp.einsum('bghsn,bngd->bsghd', p.astype(vc.dtype), vc)
    return o, p

def cmp_to_sel_map(n_cmp, n_sel):
    c0 = jnp.arange(n_cmp) * CMP_STRIDE
    s0 = jnp.arange(n_sel) * SEL_BLOCK
    ov = jnp.minimum(c0[:, None] + CMP_BLOCK, s0[None, :] + SEL_BLOCK) - jnp.maximum(c0[:, None], s0[None, :])
    return jnp.clip(ov, 0, None).astype(jnp.float32) / CMP_BLOCK

def nsa_select(p_cmp, S):
    n_cmp = p_cmp.shape[-1]
    n_sel = S // SEL_BLOCK
    imp = jnp.einsum('bghsn,nj->bgsj', p_cmp, cmp_to_sel_map(n_cmp, n_sel))
    qblk = jnp.arange(S) // SEL_BLOCK
    j = jnp.arange(n_sel)
    rel = qblk[:, None] - j[None, :]
    causal = rel >= 0
    forced = causal & ((j[None, :] == 0) | (rel < N_LOCAL_FORCED))
    score = jnp.where(forced, BIG, jnp.where(causal, imp, NEG_INF))
    top_s, top_i = lax.top_k(score, min(SEL_TOPK, n_sel))
    return top_i, top_s > 0.5 * NEG_INF

def nsa_selected(q, k, v, top_i, top_ok):
    B, S, G, HPG, dh = q.shape
    n_sel = S // SEL_BLOCK
    nk = top_i.shape[-1]
    nq = S // SEL_QBLOCK
    kb = k.reshape(B, n_sel, SEL_BLOCK, G, dh).transpose(0, 3, 1, 2, 4)
    vb = v.reshape(B, n_sel, SEL_BLOCK, G, dh).transpose(0, 3, 1, 2, 4)
    qb = jnp.moveaxis(q.reshape(B, nq, SEL_QBLOCK, G, HPG, dh), 1, 0)
    ib = jnp.moveaxis(top_i.reshape(B, G, nq, SEL_QBLOCK, nk), 2, 0)
    mb = jnp.moveaxis(top_ok.reshape(B, G, nq, SEL_QBLOCK, nk), 2, 0)
    bi = jnp.arange(B)[:, None, None, None]
    gi = jnp.arange(G)[None, :, None, None]

    def body(args):
        qi, ii, mi, blk = args
        kg = kb[bi, gi, ii]
        vg = vb[bi, gi, ii]
        tpos = blk * SEL_QBLOCK + jnp.arange(SEL_QBLOCK)
        kpos = ii[..., None] * SEL_BLOCK + jnp.arange(SEL_BLOCK)
        mask = mi[..., None] & (kpos <= tpos[None, None, :, None, None])
        s = jnp.einsum('bqghd,bgqnld->bghqnl', qi, kg) * NSA_SCALE
        p = masked_softmax(s.reshape(B, G, HPG, SEL_QBLOCK, nk * SEL_BLOCK),
                           mask.reshape(B, G, 1, SEL_QBLOCK, nk * SEL_BLOCK))
        p = p.reshape(B, G, HPG, SEL_QBLOCK, nk, SEL_BLOCK).astype(vg.dtype)
        return jnp.einsum('bghqnl,bgqnld->bqghd', p, vg)

    out = lax.map(body, (qb, ib, mb, jnp.arange(nq)))
    return jnp.moveaxis(out, 0, 1).reshape(B, S, G, HPG, dh)

def nsa_window(q, k, v):
    B, S, G, HPG, dh = q.shape
    nq = S // WIN_QBLOCK
    span = WIN_QBLOCK + WINDOW
    kp = jnp.pad(k, ((0, 0), (WINDOW, 0), (0, 0), (0, 0)))
    vp = jnp.pad(v, ((0, 0), (WINDOW, 0), (0, 0), (0, 0)))
    qb = jnp.moveaxis(q.reshape(B, nq, WIN_QBLOCK, G, HPG, dh), 1, 0)

    def body(args):
        qi, blk = args
        start = blk * WIN_QBLOCK
        ks = lax.dynamic_slice_in_dim(kp, start, span, axis=1)
        vs = lax.dynamic_slice_in_dim(vp, start, span, axis=1)
        tpos = start + jnp.arange(WIN_QBLOCK)
        kpos = start - WINDOW + jnp.arange(span)
        d = tpos[:, None] - kpos[None, :]
        mask = (d >= 0) & (d < WINDOW) & (kpos[None, :] >= 0)
        s = jnp.einsum('bqghd,bkgd->bghqk', qi, ks) * NSA_SCALE
        p = masked_softmax(s, mask).astype(vs.dtype)
        return jnp.einsum('bghqk,bkgd->bqghd', p, vs)

    out = lax.map(body, (qb, jnp.arange(nq)))
    return jnp.moveaxis(out, 0, 1).reshape(B, S, G, HPG, dh)

def causal_conv(x, w, b):
    C = x.shape[-1]
    y = lax.conv_general_dilated(x, w[:, None, :], window_strides=(1,), padding=[(CONV_WIDTH - 1, 0)],
                                 dimension_numbers=('NWC', 'WIO', 'NWC'), feature_group_count=C)
    return y + b

def mlstm_chunkwise(q, k, v, i_pre, logf):
    B, S, H, dh = q.shape
    L = ML_CHUNK
    nc = S // L
    q = q.astype(jnp.float32)
    k = k.astype(jnp.float32) * (dh ** -0.5)
    v = v.astype(jnp.float32)

    def chunks(a):
        return jnp.moveaxis(a.reshape(B, nc, L, *a.shape[2:]), 1, 0)

    tril = jnp.tril(jnp.ones((L, L), dtype=bool))

    def step(carry, xs):
        C, n, m = carry
        qj, kj, vj, ij, fj = xs
        qh = qj.transpose(0, 2, 1, 3)
        kh = kj.transpose(0, 2, 1, 3)
        vh = vj.transpose(0, 2, 1, 3)
        b = jnp.cumsum(fj, axis=1).transpose(0, 2, 1)
        ih = ij.transpose(0, 2, 1)
        dlog = jnp.where(tril, b[..., :, None] - b[..., None, :] + ih[..., None, :], -jnp.inf)
        inter = b + m[..., None]
        m_t = jnp.maximum(inter, jnp.max(dlog, axis=-1))
        dw = jnp.exp(dlog - m_t[..., None])
        iw = jnp.exp(inter - m_t)
        sqk = jnp.einsum('bhld,bhsd->bhls', qh, kh) * dw
        num = jnp.einsum('bhls,bhsd->bhld', sqk, vh) + iw[..., None] * jnp.einsum('bhed,bhld->bhle', C, qh)
        den = jnp.sum(sqk, axis=-1) + iw * jnp.einsum('bhd,bhld->bhl', n, qh)
        h = num / jnp.maximum(jnp.abs(den), jnp.exp(-m_t))[..., None]
        b_end = b[..., -1]
        wlog = b_end[..., None] - b + ih
        m_new = jnp.maximum(b_end + m, jnp.max(wlog, axis=-1))
        ws = jnp.exp(wlog - m_new[..., None])
        decay = jnp.exp(b_end + m - m_new)
        C_new = decay[..., None, None] * C + jnp.einsum('bhs,bhse,bhsd->bhed', ws, vh, kh)
        n_new = decay[..., None] * n + jnp.einsum('bhs,bhsd->bhd', ws, kh)
        return (C_new, n_new, m_new), h

    init = (jnp.zeros((B, H, dh, dh), jnp.float32), jnp.zeros((B, H, dh), jnp.float32), jnp.zeros((B, H), jnp.float32))
    _, hs = lax.scan(step, init, (chunks(q), chunks(k), chunks(v), chunks(i_pre), chunks(logf)))
    return hs.transpose(1, 0, 3, 2, 4).reshape(B, S, H, dh)

def memory_xattn(q, mem, g, w_kv):
    B, S, _ = q.shape
    M = mem.shape[1]
    kv = rmsnorm(mem, g) @ w_kv
    k = kv[..., :MEM_W].reshape(B, M, MEM_HEADS, MEM_DH)
    v = kv[..., MEM_W:].reshape(B, M, MEM_HEADS, MEM_DH)
    qh = q.reshape(B, S, MEM_HEADS, MEM_DH)
    s = jnp.einsum('bshd,bmhd->bhsm', qh, k).astype(jnp.float32) * MEM_SCALE
    p = jax.nn.softmax(s, axis=-1).astype(v.dtype)
    return jnp.einsum('bhsm,bmhd->bshd', p, v).reshape(B, S, MEM_W)

def first_inputs(seed: int = 0) -> dict:
    key = jax.random.key(seed)
    ks = jax.random.split(key, 32)
    L = DEPTH

    def nrm(k, shape, scale):
        return jax.random.normal(k, shape, jnp.float32) * scale

    def gain(k, shape):
        return 1.0 + 0.05 * jax.random.normal(k, shape, jnp.float32)

    gate_b = jnp.concatenate([
        0.1 * jax.random.normal(ks[10], (L, ML_HEADS), jnp.float32),
        jnp.linspace(3.0, 6.0, ML_HEADS, dtype=jnp.float32)[None, :] + 0.1 * jax.random.normal(ks[11], (L, ML_HEADS), jnp.float32),
    ], axis=-1)
    return {
        "x": nrm(ks[0], (BATCH, SEQ, D_MODEL), 1.0),
        "mem": nrm(ks[1], (BATCH, MEM_LEN, D_MODEL), 1.0),
        "g_pre_mix": gain(ks[2], (L, D_MODEL)),
        "w_in": nrm(ks[3], (L, D_MODEL, IN_WIDTH), D_MODEL ** -0.5),
        "cmp_pe_k": nrm(ks[4], (L, CMP_BLOCK, NSA_DH), 0.1),
        "cmp_w1_k": nrm(ks[5], (L, CMP_BLOCK, NSA_DH, CMP_HIDDEN), (CMP_BLOCK * NSA_DH) ** -0.5),
        "cmp_w2_k": nrm(ks[6], (L, CMP_HIDDEN, NSA_DH), CMP_HIDDEN ** -0.5),
        "cmp_pe_v": nrm(ks[7], (L, CMP_BLOCK, NSA_DH), 0.1),
        "cmp_w1_v": nrm(ks[8], (L, CMP_BLOCK, NSA_DH, CMP_HIDDEN), (CMP_BLOCK * NSA_DH) ** -0.5),
        "cmp_w2_v": nrm(ks[9], (L, CMP_HIDDEN, NSA_DH), CMP_HIDDEN ** -0.5),
        "ml_conv_w": nrm(ks[12], (L, CONV_WIDTH, 2 * ML_W), CONV_WIDTH ** -0.5),
        "ml_conv_b": nrm(ks[13], (L, 2 * ML_W), 0.02),
        "ml_gate_b": gate_b,
        "ml_head_g": gain(ks[14], (L, ML_W)),
        "g_mem": gain(ks[15], (L, D_MODEL)),
        "w_mem_kv": nrm(ks[16], (L, D_MODEL, 2 * MEM_W), D_MODEL ** -0.5),
        "w_proj_nsa": nrm(ks[17], (L, NSA_Q, D_MODEL), NSA_Q ** -0.5),
        "w_proj_ml": nrm(ks[18], (L, ML_W, D_MODEL), ML_W ** -0.5),
        "w_proj_mem": nrm(ks[19], (L, MEM_W, D_MODEL), MEM_W ** -0.5),
        "w_out": nrm(ks[20], (L, D_MODEL, D_MODEL), D_MODEL ** -0.5),
        "g_post_mix": gain(ks[21], (L, D_MODEL)),
        "g_pre_ffn": gain(ks[22], (L, D_MODEL)),
        "w_ffn_in": nrm(ks[23], (L, D_MODEL, 2 * D_FF), D_MODEL ** -0.5),
        "w_ffn_down": nrm(ks[24], (L, D_FF, D_MODEL), D_FF ** -0.5),
        "g_post_ffn": gain(ks[25], (L, D_MODEL)),
    }

def first_block(x, mem, g_pre_mix, w_in, cmp_pe_k, cmp_w1_k, cmp_w2_k, cmp_pe_v, cmp_w1_v, cmp_w2_v,
              ml_conv_w, ml_conv_b, ml_gate_b, ml_head_g, g_mem, w_mem_kv, w_proj_nsa, w_proj_ml,
              w_proj_mem, w_out, g_post_mix, g_pre_ffn, w_ffn_in, w_ffn_down, g_post_ffn):
    B, S, _ = x.shape
    offsets = np.cumsum(IN_SPLITS)[:-1].tolist()
    for l in range(DEPTH):
        h = rmsnorm(x, g_pre_mix[l])
        z = h @ w_in[l]
        q_nsa, kv_nsa, g_nsa, qkv_ml, if_ml, o_ml, q_mem, g_merge = jnp.split(z, offsets, axis=-1)

        q = q_nsa.reshape(B, S, NSA_GROUPS, NSA_HPG, NSA_DH)
        kv = kv_nsa.reshape(B, S, 6, NSA_GROUPS, NSA_DH)
        o_cmp, p_cmp = nsa_compressed(q, kv[:, :, 0], kv[:, :, 1], cmp_pe_k[l], cmp_w1_k[l], cmp_w2_k[l],
                                      cmp_pe_v[l], cmp_w1_v[l], cmp_w2_v[l])
        top_i, top_ok = nsa_select(p_cmp, S)
        o_slc = nsa_selected(q, kv[:, :, 2], kv[:, :, 3], top_i, top_ok)
        o_win = nsa_window(q, kv[:, :, 4], kv[:, :, 5])
        gb = jax.nn.sigmoid(g_nsa.reshape(B, S, NSA_GROUPS, NSA_HPG, 3))
        y_nsa = (gb[..., 0:1] * o_cmp + gb[..., 1:2] * o_slc + gb[..., 2:3] * o_win).reshape(B, S, NSA_Q)

        qk = jax.nn.silu(causal_conv(qkv_ml[..., :2 * ML_W], ml_conv_w[l], ml_conv_b[l]))
        q_m = qk[..., :ML_W].reshape(B, S, ML_HEADS, ML_DH)
        k_m = qk[..., ML_W:].reshape(B, S, ML_HEADS, ML_DH)
        v_m = qkv_ml[..., 2 * ML_W:].reshape(B, S, ML_HEADS, ML_DH)
        gates = if_ml.astype(jnp.float32) + ml_gate_b[l].astype(jnp.float32)
        i_pre = gates[..., :ML_HEADS]
        logf = jax.nn.log_sigmoid(gates[..., ML_HEADS:])
        h_ml = mlstm_chunkwise(q_m, k_m, v_m, i_pre, logf)
        h_ml = h_ml * lax.rsqrt(jnp.mean(h_ml * h_ml, axis=-1, keepdims=True) + EPS)
        h_ml = h_ml.reshape(B, S, ML_W) * ml_head_g[l].astype(jnp.float32)
        y_ml = (jax.nn.sigmoid(o_ml.astype(jnp.float32)) * h_ml).astype(x.dtype)

        y_mem = memory_xattn(q_mem, mem, g_mem[l], w_mem_kv[l])

        gm = jax.nn.sigmoid(g_merge.reshape(B, S, N_BRANCH, D_MODEL))
        y = (gm[:, :, 0] * (y_nsa @ w_proj_nsa[l]) + gm[:, :, 1] * (y_ml @ w_proj_ml[l])
             + gm[:, :, 2] * (y_mem @ w_proj_mem[l]))
        x = x + rmsnorm(y @ w_out[l], g_post_mix[l])

        h = rmsnorm(x, g_pre_ffn[l])
        gu = h @ w_ffn_in[l]
        gate, up = gu[..., :D_FF], gu[..., D_FF:]
        x = x + rmsnorm((jax.nn.silu(gate) * up) @ w_ffn_down[l], g_post_ffn[l])
    return x


DEPTH_2 = 2

N_MIXERS = 2
POOL_WINDOWS = (2, 4, 8, 16)
N_POOL_GROUPS = len(POOL_WINDOWS)
POOL_GROUP_DIM = D_MODEL // N_POOL_GROUPS
CONV_KERNEL = 31
D_FF_2 = ((8 * D_MODEL // 3 + 255) // 256) * 256
RMS_EPS = 1e-6
LN_EPS = 1e-5
FFN_RESIDUAL_WEIGHT = 0.5
N_POOL_LAYERS = len(range(0, DEPTH_2, N_MIXERS))
N_CONV_LAYERS = len(range(1, DEPTH_2, N_MIXERS))


def rmsnorm_2(x, g):
    xf = x.astype(jnp.float32)
    y = xf * lax.rsqrt(jnp.mean(xf * xf, axis=-1, keepdims=True) + RMS_EPS)
    return (y * g.astype(jnp.float32)).astype(x.dtype)

def layernorm(x, g, b):
    xf = x.astype(jnp.float32)
    mu = jnp.mean(xf, axis=-1, keepdims=True)
    xc = xf - mu
    var = jnp.mean(xc * xc, axis=-1, keepdims=True)
    y = xc * lax.rsqrt(var + LN_EPS) * g.astype(jnp.float32) + b.astype(jnp.float32)
    return y.astype(x.dtype)

def swiglu_ffn(x, w_in, w_out):
    gate, up = jnp.split(x @ w_in, 2, axis=-1)
    return (jax.nn.silu(gate) * up) @ w_out

def pool_mixer(x, w_pool, b_pool, scale):
    B, S, D = x.shape
    xf = x.astype(jnp.float32)
    c = jnp.concatenate([jnp.zeros((B, 1, D), jnp.float32), jnp.cumsum(xf, axis=1)], axis=1)
    t = jnp.arange(S)
    parts = []
    for g, w in enumerate(POOL_WINDOWS):
        cg = c[..., g * POOL_GROUP_DIM:(g + 1) * POOL_GROUP_DIM]
        lo = jnp.clip(t - w // 2, 0, S)
        hi = jnp.clip(t - w // 2 + w, 0, S)
        cnt = (hi - lo).astype(jnp.float32)
        win_sum = jnp.take(cg, hi, axis=1) - jnp.take(cg, lo, axis=1)
        parts.append(win_sum / cnt[None, :, None])
    pooled = jnp.concatenate(parts, axis=-1) - xf
    pooled = pooled.astype(x.dtype).reshape(B, S, N_POOL_GROUPS, POOL_GROUP_DIM)
    y = jnp.einsum('bsgc,gcd->bsgd', pooled, w_pool).reshape(B, S, D) + b_pool
    return y * scale

def conformer_conv(x, w_pw1, b_pw1, w_dw, b_dw, ln_g, ln_b, w_pw2, b_pw2):
    D = x.shape[-1]
    a, gate = jnp.split(x @ w_pw1 + b_pw1, 2, axis=-1)
    h = a * jax.nn.sigmoid(gate)
    h = lax.conv_general_dilated(
        h, w_dw[:, None, :], window_strides=(1,),
        padding=[(CONV_KERNEL // 2, CONV_KERNEL // 2)],
        dimension_numbers=('NWC', 'WIO', 'NWC'),
        feature_group_count=D) + b_dw
    h = jax.nn.silu(layernorm(h, ln_g, ln_b))
    return h @ w_pw2 + b_pw2

def second_inputs(seed: int = 0) -> dict:
    key = jax.random.key(seed)
    ks = jax.random.split(key, 16)
    D, F, K = D_MODEL, D_FF_2, CONV_KERNEL
    nrm = lambda k, shape, s: jax.random.normal(k, shape, jnp.float32) * s
    return {
        "x": nrm(ks[0], (BATCH, SEQ, D), 1.0),
        "norm_g": 1.0 + nrm(ks[1], (DEPTH_2, 3, D), 0.05),
        "ffn_w_in": nrm(ks[2], (DEPTH_2, 2, D, 2 * F), D ** -0.5),
        "ffn_w_out": nrm(ks[3], (DEPTH_2, 2, F, D), F ** -0.5),
        "pool_w": nrm(ks[4], (N_POOL_LAYERS, N_POOL_GROUPS, POOL_GROUP_DIM, POOL_GROUP_DIM), POOL_GROUP_DIM ** -0.5),
        "pool_b": nrm(ks[5], (N_POOL_LAYERS, D), 0.02),
        "pool_scale": 1.0 + nrm(ks[6], (N_POOL_LAYERS, D), 0.1),
        "conv_w_pw1": nrm(ks[7], (N_CONV_LAYERS, D, 2 * D), D ** -0.5),
        "conv_b_pw1": nrm(ks[8], (N_CONV_LAYERS, 2 * D), 0.02),
        "conv_w_dw": nrm(ks[9], (N_CONV_LAYERS, K, D), K ** -0.5),
        "conv_b_dw": nrm(ks[10], (N_CONV_LAYERS, D), 0.02),
        "conv_ln_g": 1.0 + nrm(ks[11], (N_CONV_LAYERS, D), 0.05),
        "conv_ln_b": nrm(ks[12], (N_CONV_LAYERS, D), 0.02),
        "conv_w_pw2": nrm(ks[13], (N_CONV_LAYERS, D, D), D ** -0.5),
        "conv_b_pw2": nrm(ks[14], (N_CONV_LAYERS, D), 0.02),
        "final_g": 1.0 + nrm(ks[15], (D,), 0.05),
    }

def second_block(x, norm_g, ffn_w_in, ffn_w_out, pool_w, pool_b, pool_scale,
              conv_w_pw1, conv_b_pw1, conv_w_dw, conv_b_dw, conv_ln_g, conv_ln_b,
              conv_w_pw2, conv_b_pw2, final_g):
    for i in range(DEPTH_2):
        x = x + FFN_RESIDUAL_WEIGHT * swiglu_ffn(rmsnorm_2(x, norm_g[i, 0]), ffn_w_in[i, 0], ffn_w_out[i, 0])
        h = rmsnorm_2(x, norm_g[i, 1])
        j = i // N_MIXERS
        if i % N_MIXERS == 0:
            x = x + pool_mixer(h, pool_w[j], pool_b[j], pool_scale[j])
        else:
            x = x + conformer_conv(h, conv_w_pw1[j], conv_b_pw1[j], conv_w_dw[j], conv_b_dw[j],
                                   conv_ln_g[j], conv_ln_b[j], conv_w_pw2[j], conv_b_pw2[j])
        x = x + FFN_RESIDUAL_WEIGHT * swiglu_ffn(rmsnorm_2(x, norm_g[i, 2]), ffn_w_in[i, 1], ffn_w_out[i, 1])
    return rmsnorm_2(x, final_g)


def setup_inputs(seed=0):
    out = dict(first_inputs(seed))
    for name, value in second_inputs(seed + 1).items():
        if name != "x":
            out[name + "_2"] = value
    return out


def reference(
    x, mem, g_pre_mix, w_in, cmp_pe_k, cmp_w1_k, cmp_w2_k, cmp_pe_v, cmp_w1_v, cmp_w2_v,
    ml_conv_w, ml_conv_b, ml_gate_b, ml_head_g, g_mem, w_mem_kv, w_proj_nsa, w_proj_ml,
    w_proj_mem, w_out, g_post_mix, g_pre_ffn, w_ffn_in, w_ffn_down, g_post_ffn, norm_g_2,
    ffn_w_in_2, ffn_w_out_2, pool_w_2, pool_b_2, pool_scale_2, conv_w_pw1_2, conv_b_pw1_2,
    conv_w_dw_2, conv_b_dw_2, conv_ln_g_2, conv_ln_b_2, conv_w_pw2_2, conv_b_pw2_2, final_g_2,
):
    x = first_block(
        x, mem, g_pre_mix, w_in, cmp_pe_k, cmp_w1_k, cmp_w2_k, cmp_pe_v, cmp_w1_v, cmp_w2_v,
        ml_conv_w, ml_conv_b, ml_gate_b, ml_head_g, g_mem, w_mem_kv, w_proj_nsa, w_proj_ml,
        w_proj_mem, w_out, g_post_mix, g_pre_ffn, w_ffn_in, w_ffn_down, g_post_ffn,
    )
    return second_block(
        x, norm_g_2, ffn_w_in_2, ffn_w_out_2, pool_w_2, pool_b_2, pool_scale_2, conv_w_pw1_2,
        conv_b_pw1_2, conv_w_dw_2, conv_b_dw_2, conv_ln_g_2, conv_ln_b_2, conv_w_pw2_2,
        conv_b_pw2_2, final_g_2,
    )


_drawn_inputs = setup_inputs


def setup_inputs(seed=0):
    import zlib

    import numpy as np

    out = dict(_drawn_inputs(seed))
    spreads = {}
    factors = {'cmp_pe_k': 64.0,
     'ml_conv_b': 16.502,
     'g_mem': 4.814,
     'pool_b_2': 5.307,
     'conv_b_pw1_2': 8.0,
     'conv_b_dw_2': 4.986,
     'conv_ln_g_2': 3.067,
     'conv_ln_b_2': 8.0,
     'conv_b_pw2_2': 5.831,
     'cmp_w1_k': 3.752,
     'cmp_w2_k': 3.827,
     'cmp_pe_v': 8.0,
     'ml_head_g': 7.723}
    for name, (base, spread) in spreads.items():
        noise = np.random.default_rng([zlib.crc32(name.encode()), seed]).standard_normal(out[name].shape)
        drawn = base * np.exp(spread * noise) if base else spread * noise
        out[name] = __import__('jax').numpy.asarray(drawn.astype(out[name].dtype))
    for name, factor in factors.items():
        out[name] = (out[name] * factor).astype(out[name].dtype)
    return out
```

```python
from contextlib import ExitStack

import numpy as np

import concourse.bass as bass
from concourse import mybir

F32 = mybir.dt.float32
F32R = mybir.dt.float32r
ALU = mybir.AluOpType
ACT = mybir.ActivationFunctionType
AX_X = mybir.AxisListType.X

P = 128
T = 512
D = 1024
KT = D // P
TT = T // P
MEM = 256
MT = MEM // P
UC = 256
UNIT = KT * UC
FF = 2816
HT = FF // P
UP_STEPS = FF // UC
DOWN_K = (8, 8, 6)
GROUPS, HPG, DH = 4, 4, 64
NC = (T - 32) // 16 + 1
EPS = 1e-6
LN_EPS = 1e-5
TAPS = 31
PAD = TAPS // 2
POOL_PAD = 8
NEG = -1e30

C_KV, C_GATE, C_QK, C_V, C_IF, C_O, C_QMEM, C_MERGE = 1024, 2560, 2608, 3632, 4144, 4152, 4664, 5176

ROWS = [("g_pre_mix", 1), ("g_post_mix", 1), ("g_pre_ffn", 1), ("g_post_ffn", 1), ("g_mem", 1),
        ("norm_g_2", 6), ("pool_b_2", 1), ("pool_scale_2", 1), ("conv_b_pw1_2", 2), ("conv_b_dw_2", 1),
        ("conv_ln_g_2", 1), ("conv_ln_b_2", 1), ("conv_b_pw2_2", 1), ("ml_conv_w", 4), ("ml_conv_b", 1),
        ("conv_w_dw_2", TAPS)]
ROW, NROWS = {}, 0
for _name, _count in ROWS:
    ROW[_name] = NROWS
    NROWS += _count

UNITS = [("mem", 0, UC, "mem_k"), ("mem", 256, UC, "mem_k"), ("mem", 512, UC, "mem_v"), ("mem", 768, UC, "mem_v"),
         ("in", C_QMEM, UC, "q_mem"), ("in", C_QMEM + UC, UC, "q_mem"),
         ("in", C_KV, UC, "kc"), ("in", C_KV + 256, UC, "vc"), ("in", C_KV + 512, UC, "ks"), ("in", C_KV + 1024, UC, "kw"),
         ("in", C_KV + 768, UC, "vs"), ("in", C_KV + 1280, UC, "vw"), ("in", C_GATE, 48, "gate"), ("in", C_IF, 8, "if"),
         ("in", C_QK, UC, "qk"), ("in", C_QK + 256, UC, "qk"), ("in", C_QK + 512, UC, "qk"), ("in", C_QK + 768, UC, "qk"),
         ("in", C_V, UC, "v"), ("in", C_V + UC, UC, "v"), ("in", C_O, UC, "o"), ("in", C_O + UC, UC, "o")]
NFIX = len(UNITS)
FEATURE_MAJOR = ("mem_k", "q_mem", "kc", "vc", "ks", "kw", "qk")
ACT_ONLY = ("mem_v", "gate", "if", "o")
DVE_EVACS = [0]
for _u in UNITS:
    DVE_EVACS.append(DVE_EVACS[-1] + (_u[3] not in ACT_ONLY))

SCHEDULE = [("unit", u) for u in range(6)]
for _h in range(4):
    SCHEDULE += [("mem_scores", _h), ("unit", 6 + 2 * _h), ("mem_turn", _h), ("unit", 7 + 2 * _h), ("mem_out", _h)]
SCHEDULE += [("unit", 14), ("cmp_hidden", 0), ("unit", 15), ("cmp_out", 0), ("unit", 16), ("unit", 17),
             ("cmp_hidden", 1), ("unit", 18), ("cmp_out", 1), ("ml_gates", 0), ("unit", 19), ("ml_rows", 0),
             ("unit", 20), ("unit", 21)]
for _h in range(4):
    SCHEDULE += [("ml_scores", _h), ("ml_out", _h)]
SCHEDULE += [("ml_turn", 0)]

U_NSA = NFIX
U_MERGE = U_NSA + 2 * GROUPS
U_WOUT = U_MERGE + 6 * 4
PER_FFN = 2 * UP_STEPS + 12
U_FFN = [0] * 5
U_FFN[0] = U_WOUT + 4
U_FFN[1] = U_FFN[0] + PER_FFN
U_POOL = U_FFN[1] + PER_FFN
U_FFN[2] = U_POOL + 2
U_FFN[3] = U_FFN[2] + PER_FFN
U_PW1 = U_FFN[3] + PER_FFN
U_PW2 = U_PW1 + 8
U_FFN[4] = U_PW2 + 4
N_UNITS = U_FFN[4] + PER_FFN

STEPS = [(br, qb, hh) for br in range(2) for qb in range(TT) for hh in range(HPG)]
NS = len(STEPS)
OUT_BANK = (7, 1)
CMP_BANK = (2, 3, 4, 6)

K_ID, K_ONE, K_STRIP, K_TRI, K_CNEG, K_C01, K_SEL = 0, 128, 256, 768, 896, 1020, 1144
K_END = 1656


NSA_PER = 25


class Chain:

    def __init__(self, sem):
        self.sem, self.n, self.made = sem, 0, 0

    def link(self, eng, ins):
        self.step(ins)
        eng.wait_ge(self.sem, self.n)

    def step(self, ins):
        ins.then_inc(self.sem, 1)
        self.n = self.n + 1
        self.made += 1

    def enter(self, i, first, per):
        self.base, self.per, self.made = self.n, per, 0
        self.n = (i - first) * per + self.base

    def leave(self, turns):
        assert self.made == self.per, (self.made, self.per)
        self.n = self.base + turns * self.per


def constants():
    c = np.zeros((P, K_END), np.float32)
    p = np.arange(P)
    c[:, K_ID:K_ID + P] = np.eye(P)
    c[:, K_ONE:K_ONE + P] = 1
    c[:, K_STRIP + 384:K_STRIP + 512] = np.where(p[None, :] <= p[:, None], 0, NEG)
    c[:, K_TRI:K_TRI + P] = p[:, None] <= p[None, :]
    for qb in range(TT):
        seen = (16 * np.arange(NC) + 31)[None, :] <= (p + P * qb)[:, None]
        c[:, K_CNEG + NC * qb:K_CNEG + NC * (qb + 1)] = np.where(seen, 0, NEG)
        c[:, K_C01 + NC * qb:K_C01 + NC * (qb + 1)] = seen
    for h in range(4):
        c[h, K_SEL + P * h:K_SEL + P * (h + 1)] = 1
    t = np.arange(T)
    inv = np.zeros((4, T), np.float32)
    for g in range(4):
        w = 2 << g
        count = np.clip(t - w // 2 + w, 0, T) - np.clip(t - w // 2, 0, T)
        inv[g] = np.float32(1) / count.astype(np.float32)
    return c, inv


def build(nc, A, const_in, invcount_in, out):
    with ExitStack() as ctx:
        def sem(name):
            return ctx.enter_context(nc.semaphore(name))

        base = (nc.sbuf_base + 63) // 64 * 64
        limit = nc.sbuf_usable_end

        def at(name, shape, off, dt=F32):
            n = 4
            for s in shape[1:]:
                n *= s
            assert off + n <= limit, (name, off, n, limit)
            return nc.alloc_sbuf_tensor_at(name, shape, dt, offset=off)

        KB = 1024
        cid = at("identity_ones", [P, 256], base)
        vec = at("vectors", [P, 512], base + 1 * KB)
        stat = at("stat", [P, 128], base + 3 * KB)
        H0 = base + 3 * KB + 512
        h_hi = at("h_hi", [P, KT, T], H0, F32R)
        h_lo = at("h_lo", [P, KT, T], H0 + 16 * KB, F32R)
        W0 = H0 + 32 * KB
        raw = [at(f"w_raw{s}", [P, UNIT], W0 + 8 * KB * s) for s in range(2)]
        w_hi = [at(f"w_hi{s}", [P, UNIT], W0 + 8 * KB * (2 + s), F32R) for s in range(2)]
        w_lo = [at(f"w_lo{s}", [P, UNIT], W0 + 8 * KB * (4 + s), F32R) for s in range(2)]
        AR = W0 + 48 * KB

        ident = cid[:, 0:P]
        ones = cid[:, P:2 * P]

        def col(name, j, r=0):
            k = j * NROWS + ROW[name] + r
            return vec[:, k:k + 1]

        pe_cols = [vec[:, 448:480], vec[:, 480:512]]
        eps = stat[:, 0:1]
        ln_eps = stat[:, 1:2]
        ss = stat[:, 8:16]
        rs_tok = stat[:, 16:24]

        ymem = [at("ymem_hi", [P, 4, T], AR + 32 * KB, F32R), at("ymem_lo", [P, 4, T], AR + 40 * KB, F32R)]
        yml = [at("yml_hi", [P, 4, T], AR + 48 * KB, F32R), at("yml_lo", [P, 4, T], AR + 56 * KB, F32R)]
        ynsa = [at("ynsa_hi", [P, 8, T], AR, F32R), at("ynsa_lo", [P, 8, T], AR + 16 * KB, F32R)]
        PE0 = AR + 64 * KB
        v_sw = [at("v_sel", [P, TT, UC], PE0), at("v_win", [P, TT, UC], PE0 + 4 * KB)]
        gate = at("nsa_gate", [P, TT, 48], PE0 + 8 * KB)
        kcmp = at("k_cmp", [P, GROUPS, NC], PE0 + 8 * KB + 768)
        vcmp = at("v_cmp", [P, GROUPS, DH], PE0 + 9 * KB + 512)
        cms = at("const_masks", [P, 1144 - 256], PE0 + 10 * KB + 512)
        WK = PE0 + 14 * KB + 32
        strip = cms[:, 0:512]
        tri = cms[:, 512:640]
        cneg = cms[:, 640:640 + TT * NC]
        c01 = cms[:, 764:764 + TT * NC]

        x_tok = at("x_tok", [P, TT, D], AR)
        mem_tok = at("mem_tok", [P, MT, D], AR + 16 * KB)
        rows = at("vector_rows", [P, D], AR + 24 * KB)
        pe_rows = at("pe_rows", [P, 2, P], AR + 28 * KB)
        junk = at("junk", [P, D], AR + 30 * KB)
        m_hi = at("m_hi", [P, KT, MEM], WK, F32R)
        m_lo = at("m_lo", [P, KT, MEM], WK + 8 * KB, F32R)
        KM = WK + 17 * KB
        k_mem = at("k_mem", [P, 4, MEM], KM)
        v_mem = at("v_mem", [P, MT, T], KM + 4 * KB)
        q_mem = at("q_mem", [P, 4, T], KM + 8 * KB)
        p_mem = at("p_mem", [P, TT, MEM], AR + 48 * KB)
        pt_mem = at("pt_mem", [P, MT, T], AR + 52 * KB)
        kv_c = [at("k_c", [P, 2, T], AR), at("v_c", [P, 2, T], AR + 4 * KB)]
        cmp_a = at("cmp_a", [P, 2, T], AR + 8 * KB)
        cmp_b = at("cmp_b", [P, 2, T], AR + 12 * KB)
        cmp_w1 = at("cmp_w1", [P, 32, P], AR + 16 * KB)
        hid_c = at("cmp_hidden", [P, 2, 2, NC], WK + 45 * KB)
        w2k = at("cmp_w2k", [P, 2, DH], WK + 45 * KB + 512)
        w2v = at("cmp_w2v", [P, DH], WK + 46 * KB)
        k_stage = [at("k_sel_stage", [P, 2, T], WK + 33 * KB), at("k_win_stage", [P, 2, T], WK + 37 * KB)]
        qk_in = at("qk_in", [P, 8, T + 3], WK)
        v_ml = at("v_ml", [P, TT, 4, P + 1], WK + 16 * KB + 128)
        o_ml = at("o_ml", [P, TT, T], WK + 25 * KB)
        if_tok = at("if_tok", [P, TT, 8], WK + 44 * KB + 512)
        conv_acc = [at(f"conv_acc{i}", [P, T], AR + (58 + 2 * i) * KB) for i in range(2)]
        d_ml = [at(f"decay{i}", [P, T], WK + (41 + 2 * i) * KB - 512) for i in range(2)]
        head_g = at("head_g", [P, T], AR + 56 * KB)
        s_ml = at("s_ml", [P, TT, T], AR)
        h_mlt = at("h_ml", [P, TT, T], AR + 8 * KB)
        row4 = [at(f"gate_row{i}", [4, T], AR + (16 + 2 * i) * KB) for i in range(6)]
        sel4 = at("head_selector", [4, 4, P], AR + 28 * KB)
        gate_b = at("gate_bias", [4, 2], AR + 62 * KB)
        ones4 = at("ones_row", [4, T], AR + 30 * KB)
        g_col = stat[:, 32:48]
        emt = stat[:, 48:64]
        den = stat[:, 64:68]
        den2 = stat[:, 68:72]
        ss_ml = stat[:, 72:88]
        rr_ml = stat[:, 88:104]
        junk2 = at("ml_junk", [P, P], WK + 45 * KB)
        qT = at("q_group", [P, 2, T], WK)
        k_dup = [at("k_sel_group", [P, T], WK + 4 * KB), at("k_win_group", [P, T], WK + 6 * KB)]
        y_tok = at("y_tok", [P, TT, HPG * DH], WK + 8 * KB)
        prob = [at(f"prob{i}", [P, T], WK + (12 + 2 * i) * KB) for i in range(4)]
        probT = [at(f"probT{i}", [P, T], WK + (20 + 2 * i) * KB) for i in range(4)]
        p_c = at("p_cmp", [P, TT, HPG, NC], WK + 28 * KB)
        pT_c = at("pT_cmp", [NC, TT * HPG, P], WK + 30 * KB)
        y_br = at("y_branch", [P, HPG, DH], WK + 38 * KB)
        nst = at("nsa_stat", [P, 256], WK + 39 * KB)
        cmax = nst[:, 0:16]
        csum = nst[:, 16:32]
        crec = nst[:, 32:48]
        cg_c = nst[:, 48:64]
        nmax = nst[:, 64:96]
        psum_row = nst[:, 96:128]
        kc_g = nst[:, 192:192 + NC]
        prec = nst[:, 128:160]
        cg = nst[:, 160:192]
        ym = [at("merged_hi", [P, 8, T], WK, F32R), at("merged_lo", [P, 8, T], WK + 16 * KB, F32R)]
        mg = [at(f"merge_gate{t}", [P, T], WK + (32 + 2 * t) * KB) for t in range(2)]
        ma = [at(f"merge_acc{t}", [P, T], WK + (36 + 2 * t) * KB) for t in range(2)]
        mb = [at(f"merge_term{t}", [P, T], WK + (40 + 2 * t) * KB) for t in range(2)]
        X = at("x", [P, KT, T], AR)
        x_tok2 = at("x_tok_again", [P, TT, D], AR + 16 * KB)
        O = at("o", [P, KT, T], H0)
        hid = [at("hid_hi", [P, HT, T], AR + 16 * KB, F32R), at("hid_lo", [P, HT, T], AR + 60 * KB, F32R)]
        TL = AR + 104 * KB
        rb = at("rstd", [P, T], TL)
        tg = [at(f"gate_tmp{t}", [P, T], TL + (2 + 2 * t) * KB) for t in range(2)]
        sq = [at(f"square{t}", [P, T], TL + (6 + 2 * t) * KB + 64) for t in range(2)]
        ssq = at("sum_squares", [P, T], TL + 10 * KB + 64)
        W_HP = T + 2 * POOL_PAD
        hp = at("pool_h", [P, KT, W_HP], AR + 16 * KB)
        pool_s = [at(f"pool_sum{i}", [P, W_HP], AR + 33 * KB + 2176 * i) for i in range(2)]
        inv = at("inv_count", [P, 4, T], AR + 38 * KB)
        W_HC = T + 2 * PAD
        hc = at("conv_h", [P, KT, W_HC], AR + 16 * KB)
        hy = at("conv_y", [P, KT, T], AR + 34 * KB)
        cacc = [at(f"conv_sum{i}", [P, T], AR + (50 + 2 * i) * KB) for i in range(2)]
        mu = at("mean", [P, T], AR + 62 * KB)
        fg = at("final_gain", [P, D], AR + 16 * KB)
        junk3 = at("final_junk", [P, T], AR + 36 * KB)
        o_tok = at("out_tok", [P, TT, D], AR + 20 * KB)

        bank = [ctx.enter_context(nc.psum_tensor(f"bank{i}", [P, T], F32)) for i in range(8)]
        k_scratch = nc.dram_tensor("k_scratch", [2, 2 * P, T], F32, kind="Internal").ap()

        const_in_place = sem("const_in_place")
        mask_in_place = sem("mask_in_place")
        tok_in_place = sem("tok_in_place")
        rows_in_place = sem("rows_in_place")
        w_landed = [sem("w_landed0"), sem("w_landed1")]
        w_hi_ready = sem("w_hi_ready")
        w_lo_ready = sem("w_lo_ready")
        w_used = sem("w_used")
        act_chain_s = sem("act_chain")
        dve_chain_s = sem("dve_chain")
        pool_chain_s = sem("pool_chain")
        pe_done = sem("pe_done")
        stat_set = sem("stat_set")
        tok_root = sem("tok_root")
        tok_scaled = sem("tok_scaled")
        vec_turned = sem("vec_turned")
        vec_ready = sem("vec_ready")
        tok_turned = sem("tok_turned")
        start_hi = sem("start_hi")
        start_lo = sem("start_lo")
        evac_act = sem("evac_act")
        evac_dve = sem("evac_dve")
        mem_s = sem("mem_scores_ready")
        mem_m = sem("mem_max_ready")
        mem_e = sem("mem_exp_done")
        mem_p = sem("mem_prob_ready")
        mem_t = sem("mem_prob_turned")
        mem_ta = sem("mem_probT_act")
        mem_td = sem("mem_probT_dve")
        mem_o = sem("mem_out_ready")
        mem_yh = sem("mem_y_hi")
        mem_y = sem("mem_y_ready")
        w1_landed = sem("w1_landed")
        w2_landed = sem("w2_landed")
        cmp_ab = sem("cmp_ab_ready")
        cmp_h = sem("cmp_hidden_summed")
        cmp_hs = sem("cmp_hidden_ready")
        cmp_o = sem("cmp_out_ready")
        cmp_e = sem("cmp_kv_ready")
        k_stored = sem("k_stored")
        ml_const = sem("ml_const")
        if_turned = sem("if_turned")
        if_rows = sem("if_rows")
        f_min = sem("f_min")
        f_log = sem("f_log")
        g_rows = sem("g_rows")
        g_turned = sem("g_turned")
        g_cols = sem("g_cols")
        emt_ready = sem("emt_ready")
        conv_done = sem("ml_conv_done")
        qk_ready = sem("qk_ready")
        bc_ready = sem("ml_bcast_ready")
        sT_ready = sem("ml_scores_ready")
        d_arg = sem("decay_arg")
        d_exp = sem("decay_exp")
        s_used = sem("ml_scores_used")
        s_masked = sem("ml_scores_masked")
        mo_ready = sem("ml_out_ready")
        m_rec = sem("ml_den_ready")
        m_h = sem("ml_h_ready")
        m_root = sem("ml_root_ready")
        m_y = sem("ml_y_ready")
        m_turned = sem("ml_y_turned")
        m_hi_s = sem("ml_y_hi")
        m_lo_s = sem("ml_y_lo")
        kd_landed = sem("k_group_landed")
        q_act = sem("q_tile0_ready")
        q_dve = sem("q_tile1_ready")
        c_s = sem("c_scores_ready")
        c_sh = sem("c_shifted")
        c_e = sem("c_exp_done")
        c_p = sem("c_prob_ready")
        c_t = sem("c_prob_turned")
        c_ta = sem("c_probT_ready")
        c_o = sem("c_out_ready")
        s_s = sem("scores_ready")
        s_m = sem("scores_masked")
        s_open = sem("scores_open")
        s_e = sem("prob_ready")
        s_t = sem("prob_turned")
        s_pa = sem("probT_act")
        s_pd = sem("probT_dve")
        s_o = sem("attn_out_ready")
        s_or = sem("attn_out_read")
        y_done = sem("y_group_done")
        y_turned = sem("y_group_turned")
        y_split = sem("y_group_split")
        mg_gate = sem("merge_gate_ready")
        mg_used = sem("merge_gate_used")
        mg_split = sem("merged_ready")
        x_again = sem("x_tok_again_landed")
        x_turned = sem("x_turned")
        o_ready = sem("tile_evacuated")
        sq_ready = sem("square_ready")
        sq_added = sem("square_added")
        sumsq = sem("sum_squares_ready")
        root = sem("root_ready")
        rstd = sem("rstd_ready")
        x_new = sem("x_updated")
        ln_used = sem("ln_square_used")
        h_ready = sem("h_ready")
        g_scaled = sem("gate_scaled")
        silu_done = sem("silu_done")
        up_read = sem("up_read")
        hid_ready = sem("hidden_ready")
        inv_landed = sem("inv_count_landed")
        pooled = sem("pooled_ready")
        glu_arg = sem("glu_sigmoid_ready")
        glu = sem("glu_ready")
        conv_y = sem("conv_y_ready")
        mean_s = sem("mean_sum_ready")
        ln_x = sem("ln_centred")
        ln_sq = sem("ln_square_ready")
        ln_z = sem("ln_affine_ready")
        ln_act = sem("ln_silu_done")
        ln_h = sem("ln_h_ready")
        fin_turned = sem("final_turned")
        fin_sq = sem("final_squares")
        fin_sum = sem("final_sum")
        fin_root = sem("final_root")
        fin_y = sem("final_ready")
        fg_landed = sem("final_gain_landed")
        stored = sem("out_stored")

        w_in = A["w_in"][0]
        w_mem = A["w_mem_kv"][0]
        tiles_of = lambda w: w.rearrange("(k p) c -> p k c", p=P)
        w_in_t = tiles_of(w_in)
        src_fixed = {"mem": tiles_of(w_mem), "in": w_in_t}
        proj_t = [tiles_of(A["w_proj_nsa"][0]), tiles_of(A["w_proj_ml"][0]), tiles_of(A["w_proj_mem"][0])]
        wout_t = tiles_of(A["w_out"][0])
        ffn_in = [tiles_of(A["w_ffn_in"][0])] + [tiles_of(A["ffn_w_in_2"][i, j]) for i in range(2) for j in range(2)]
        ffn_dn = [tiles_of(A["w_ffn_down"][0])] + [tiles_of(A["ffn_w_out_2"][i, j]) for i in range(2) for j in range(2)]
        pool_t = A["pool_w_2"][0].rearrange("g (k p) c -> p (g k) c", p=P)
        pw1_t = tiles_of(A["conv_w_pw1_2"][0])
        pw2_t = tiles_of(A["conv_w_pw2_2"][0])
        x_rows = A["x"][0].rearrange("(t p) d -> p t d", p=P)

        NEXT = [("post", ("norm_g_2", 0)), ("half", None), ("half", ("norm_g_2", 3)), ("half", None), ("last", None)]
        H_EVENT = [0, 1, 2, 3, 5]
        R_EVENT = [2, 4, 6, 7, 10]
        X_BASE = [8, 16, 32, 40, 56]
        O_BASE = [8, 16, 24, 32, 40]
        SQ_BASE = [16, 32, 48, 56, None]

        block = ctx.enter_context(nc.Block())

        @block.sync
        def _(sp):
            def load(u2, s, src, k, n):
                if not isinstance(u2, int) or u2 > 0:
                    sp.wait_ge(w_landed[s], 16)
                    sp.wait_ge(w_lo_ready, u2 * 2 + (s - 1))
                sp.dma_start(raw[s][:, 0:k * n].rearrange("p (k c) -> p k c", c=n), src).then_inc(w_landed[s], 16)

            sp.dma_start(cid[:, :], const_in[:, 0:256]).then_inc(const_in_place, 16)
            for m in range(MT):
                sp.dma_start(mem_tok[:, m, :], A["mem"][0][m * P:(m + 1) * P, :]).then_inc(tok_in_place, 16)
            for t in range(TT):
                sp.dma_start(x_tok[:, t, :], x_rows[:, t, :]).then_inc(tok_in_place, 16)
            for u, (w, c, n, kind) in enumerate(UNITS):
                load(u // 2, u % 2, src_fixed[w][:, :, c:c + n], KT, n)
                if u == 4:
                    sp.wait_ge(tok_turned, 16)
                    for half in range(2):
                        sp.dma_start(cmp_w1[DH * half:DH * (half + 1), :, :],
                                     A["cmp_w1_k"][0].rearrange("l d h -> d l h")).then_inc(w1_landed, 16)
                if u == 12:
                    sp.wait_ge(evac_act, 10)
                    sp.wait_ge(evac_dve, DVE_EVACS[10])
                    for b in range(2):
                        sp.dma_start(k_scratch[b].rearrange("(t p) n -> p t n", p=P), k_stage[b][:, :, :]).then_inc(k_stored, 16)
                if u == 16:
                    sp.wait_ge(cmp_h, 1)
                    for half in range(2):
                        sp.dma_start(cmp_w1[DH * half:DH * (half + 1), :, :],
                                     A["cmp_w1_v"][0].rearrange("l d h -> d l h")).then_inc(w1_landed, 16)
            sp.wait_ge(k_stored, 32)
            with sp.Fori(0, GROUPS) as g:
                for s in range(2):
                    load(g + U_NSA // 2, s, w_in_t[:, :, bass.ds(g * 256 + s * P, P)], KT, P)
                sp.wait_ge(k_stored, 32)
                sp.wait_ge(w_used, g * 2 + (U_NSA + 1))
                for b in range(2):
                    for half in range(2):
                        sp.dma_start(k_dup[b][DH * half:DH * (half + 1), :],
                                     k_scratch[b, bass.ds(g * DH, DH), :]).then_inc(kd_landed, 16)

            def merge_loads(c):
                for b in range(3):
                    h2 = c * 3 + (U_MERGE // 2 + b)
                    load(h2, 0, w_in_t[:, :, bass.ds(c * UC + (C_MERGE + b * D), UC)], KT, UC)
                    load(h2, 1, proj_t[b][:, :, bass.ds(c * UC, UC)], KT if b == 0 else 4, UC)

            with sp.Fori(0, 4) as c:
                merge_loads(c)
            for n in range(4):
                load((U_WOUT + n) // 2, n % 2, wout_t[:, :, n * UC:(n + 1) * UC], KT, UC)
                if n == 1:
                    sp.wait_ge(w_used, U_WOUT)
                    sp.dma_start(x_tok2[:, :, :], x_rows).then_inc(x_again, 16)
            for f in range(5):
                with sp.Fori(0, UP_STEPS) as i:
                    load(i + U_FFN[f] // 2, 0, ffn_in[f][:, :, bass.ds(i * UC, UC)], KT, UC)
                    load(i + U_FFN[f] // 2, 1, ffn_in[f][:, :, bass.ds(i * UC + FF, UC)], KT, UC)
                u = U_FFN[f] + 2 * UP_STEPS
                for c in range(4):
                    k0 = 0
                    for k in DOWN_K:
                        load(u // 2, u % 2, ffn_dn[f][:, k0:k0 + k, c * UC:(c + 1) * UC], k, UC)
                        k0 += k
                        u += 1
                if f == 1:
                    for n in range(2):
                        load((U_POOL + n) // 2, n, pool_t[:, 4 * n:4 * n + 4, :], 4, UC)
                    sp.wait_ge(w_used, U_POOL)
                    sp.dma_start(inv[:, :, :], invcount_in.rearrange("(o g) t -> o g t", o=1).to_broadcast([P, 4, T])
                                 ).then_inc(inv_landed, 16)
                if f == 3:
                    for n in range(4):
                        load(U_PW1 // 2 + n, 0, pw1_t[:, :, D + n * UC:D + (n + 1) * UC], KT, UC)
                        load(U_PW1 // 2 + n, 1, pw1_t[:, :, n * UC:(n + 1) * UC], KT, UC)
                    for n in range(4):
                        load((U_PW2 + n) // 2, n % 2, pw2_t[:, :, n * UC:(n + 1) * UC], KT, UC)
            sp.wait_ge(w_used, N_UNITS)
            sp.dma_start(fg[:, :], A["final_g_2"].rearrange("(o d) -> o d", o=1).to_broadcast([P, D])).then_inc(fg_landed, 16)
            for t in range(TT):
                sp.wait_ge(fin_y, t + 1)
                sp.dma_start(out[0].rearrange("(t p) d -> p t d", p=P)[:, t, :], o_tok[:, t, :]).then_inc(stored, 16)
            sp.wait_ge(stored, 16 * TT)

        @block.scalar
        def _(act):
            chain = Chain(act_chain_s)

            def high(u2, s):
                act.wait_ge(w_landed[s], u2 * 16 + 16)
                if not isinstance(u2, int) or u2 > 0:
                    act.wait_ge(w_used, u2 * 2 + (s - 1))
                nc.scalar.activation(w_hi[s][:, :], raw[s][:, :], ACT.Copy).then_inc(w_hi_ready, 1)

            def high_next(u):
                if u + 1 < N_UNITS:
                    high((u + 1) // 2, (u + 1) % 2)

            def root_of_sum(n):
                act.wait_ge(sumsq, n)
                nc.scalar.activation(rb[:, :], bank[4][:, :], ACT.Sqrt, bias=eps, scale=1.0 / D).then_inc(root, 1)

            r = 0
            for name, count in ROWS:
                src = A[name]
                src = src.rearrange("a b d -> (a b) d") if len(src.shape) == 3 else src.rearrange("a (r d) -> (a r) d", d=D)
                act.dma_start(rows[r:r + count, :], src).then_inc(rows_in_place, 16)
                r += count
            for b, name in enumerate(("cmp_pe_k", "cmp_pe_v")):
                for half in range(2):
                    act.dma_start(pe_rows[0:32, b, DH * half:DH * (half + 1)], A[name][0]).then_inc(rows_in_place, 16)
            act.dma_start(cms[:, :], const_in[:, K_STRIP:K_SEL]).then_inc(mask_in_place, 16)
            for half in range(2):
                act.dma_start(w2k[:, half, :], A["cmp_w2_k"][0]).then_inc(w2_landed, 16)
            act.dma_start(w2v[:, :], A["cmp_w2_v"][0]).then_inc(w2_landed, 16)

            act.wait_ge(tok_in_place, 16 * 6)
            act.wait_ge(stat_set, 1)
            for t in range(6):
                src = mem_tok[:, t, :] if t < MT else x_tok[:, t - MT, :]
                chain.link(act, nc.scalar.activation(junk[:, :], src, ACT.Square, accum_out=ss[:, t:t + 1]))
            nc.scalar.activation(rs_tok[:, 0:6], ss[:, 0:6], ACT.Sqrt, bias=eps, scale=1.0 / D).then_inc(tok_root, 1)
            high(0, 0)
            act.wait_ge(vec_ready, 1)
            for n in range(16):
                act.wait_ge(tok_turned, n + 1)
                if n < 8:
                    nc.scalar.activation(m_hi[:, n, :], bank[n][:, 0:MEM], ACT.Copy, scale=col("g_mem", n)).then_inc(start_hi, 1)
                else:
                    j = n - 8
                    nc.scalar.activation(h_hi[:, j, :], bank[j][:, :], ACT.Copy, scale=col("g_pre_mix", j)).then_inc(start_hi, 1)

            def evacuate(u):
                w, c, n, kind = UNITS[u]
                b0, b1 = bank[2 * (u % 2)], bank[2 * (u % 2) + 1]
                act.wait_ge(w_used, u + 1)
                v0 = b0[:, :].rearrange("p (t c) -> p t c", c=UC)
                v1 = b1[:, :].rearrange("p (t c) -> p t c", c=UC)
                cp = ACT.Copy
                if kind == "mem_k":
                    ins = nc.scalar.activation(k_mem[:, 2 * u, :], b0[:, 0:MEM], cp)
                elif kind == "mem_v":
                    ins = nc.scalar.activation(v_mem[:, :, c - 512:c - 512 + UC], v0, cp)
                elif kind == "q_mem":
                    ins = nc.scalar.activation(q_mem[:, 2 * (u - 4), :], b0[:, :], cp)
                elif kind in ("kc", "vc"):
                    ins = nc.scalar.activation(kv_c[u - 6][:, 0, :], b0[:, :], cp)
                elif kind in ("ks", "kw"):
                    ins = nc.scalar.activation(k_stage[u - 8][:, 0, :], b0[:, :], cp)
                elif kind in ("vs", "vw"):
                    ins = nc.scalar.activation(v_sw[u - 10][:, 0:2, :], v0, cp)
                elif kind == "gate":
                    nc.scalar.activation(gate[:, 0:2, :], v0[:, :, 0:48], ACT.Sigmoid)
                    ins = nc.scalar.activation(gate[:, 2:4, :], v1[:, :, 0:48], ACT.Sigmoid)
                elif kind == "if":
                    nc.scalar.activation(if_tok[:, 0:2, :], v0[:, :, 0:8], cp)
                    ins = nc.scalar.activation(if_tok[:, 2:4, :], v1[:, :, 0:8], cp)
                elif kind == "qk":
                    ins = nc.scalar.activation(qk_in[:, 2 * (u - 14), 3:3 + T], b0[:, :], cp)
                elif kind == "v":
                    h0 = 2 * (u - 18)
                    for t in range(2):
                        ins = nc.scalar.activation(v_ml[:, t, h0:h0 + 2, 0:P], v0[:, t, :].rearrange("p (h d) -> p h d", d=P), cp)
                else:
                    c0 = UC * (u - 20)
                    nc.scalar.activation(o_ml[:, 0:2, c0:c0 + UC], v0, ACT.Sigmoid)
                    ins = nc.scalar.activation(o_ml[:, 2:4, c0:c0 + UC], v1, ACT.Sigmoid)
                ins.then_inc(evac_act, 1)
                if kind == "qk":
                    for j in range(2 * (u - 14), 2 * (u - 14) + 2):
                        act.wait_ge(conv_done, j + 1)
                        nc.scalar.activation(qk_in[:, j, 3:3 + T], conv_acc[j % 2][:, :], ACT.Silu).then_inc(qk_ready, 1)

            def mem_scores(h):
                act.wait_ge(mem_m, h + 1)
                for qb in range(TT):
                    src = bank[4 + qb // 2][:, 256 * (qb % 2):256 * (qb % 2) + 256]
                    ins = nc.scalar.activation(p_mem[:, qb, :], src, ACT.Exp, bias=stat[:, 32 + qb:33 + qb], scale=P ** -0.5,
                                               accum_out=stat[:, 36 + qb:37 + qb])
                ins.then_inc(mem_e, 1)

            def mem_turn(h):
                act.wait_ge(mem_t, h + 1)
                nc.scalar.activation(pt_mem[:, 0, :], bank[6][:, :], ACT.Copy).then_inc(mem_ta, 1)

            def mem_out(h):
                act.wait_ge(mem_o, h + 1)
                nc.scalar.activation(ymem[0][:, h, :], bank[4][:, :], ACT.Copy).then_inc(mem_yh, 1)

            def cmp_hidden(b):
                act.wait_ge(cmp_h, b + 1)
                for par in range(2):
                    ins = nc.scalar.activation(hid_c[:, par, :, :], bank[4 + par][:, 0:2 * NC].rearrange("p (t n) -> p t n", n=NC),
                                               ACT.Silu)
                ins.then_inc(cmp_hs, 1)

            def ml_gates(_):
                for half in range(2):
                    act.dma_start(gate_b[0:4, half:half + 1],
                                  A["ml_gate_b"][0][4 * half:4 * half + 4].rearrange("(a b) -> a b", b=1)).then_inc(ml_const, 16)
                act.dma_start(sel4[:, :, :], const_in[0:4, K_SEL:K_END].rearrange("p (h c) -> p h c", c=P)).then_inc(ml_const, 16)
                act.dma_start(head_g[:, :], A["ml_head_g"].to_broadcast([P, T])).then_inc(ml_const, 16)

            def ml_rows(_):
                act.wait_ge(ml_const, 64)
                act.wait_ge(if_turned, 1)
                nc.scalar.activation(row4[0][:, :], bank[6][0:4, :], ACT.Identity, bias=gate_b[0:4, 0:1])
                nc.scalar.activation(row4[1][:, :], bank[7][0:4, :], ACT.Identity, bias=gate_b[0:4, 1:2]).then_inc(if_rows, 1)
                act.wait_ge(f_min, 1)
                chain.link(act, nc.scalar.activation(row4[2][:, :], row4[2][:, :], ACT.Exp))
                nc.scalar.activation(row4[2][:, :], row4[2][:, :], ACT.Ln, bias=1.0).then_inc(f_log, 1)
                act.wait_ge(g_turned, 1)
                nc.scalar.activation(emt, bank[7][:, 16:32], ACT.Exp, scale=-1.0).then_inc(emt_ready, 1)

            def ml_scores(h):
                for sb in range(TT):
                    n = TT * h + sb
                    act.wait_ge(d_arg, n + 1)
                    d = d_ml[n % 2][:, 0:T - P * sb]
                    nc.scalar.activation(d, d, ACT.Exp).then_inc(d_exp, 1)

            def ml_out(h):
                act.wait_ge(m_rec, h + 1)
                for tb in range(TT):
                    src = bank[7 if tb < 2 else 4][:, (P + 1) * (tb % 2):(P + 1) * (tb % 2) + P]
                    chain.link(act, nc.scalar.activation(h_mlt[:, tb, P * h:P * (h + 1)], src, ACT.Copy, scale=den[:, tb:tb + 1]))
                for tb in range(TT):
                    ins = nc.scalar.activation(junk2[:, :], h_mlt[:, tb, P * h:P * (h + 1)], ACT.Square,
                                               accum_out=ss_ml[:, 4 * tb + h:4 * tb + h + 1])
                    chain.link(act, ins)
                act.sem_inc(m_h, 1)
                if h == 3:
                    nc.scalar.activation(rr_ml, ss_ml, ACT.Sqrt, bias=eps, scale=1.0 / P).then_inc(m_root, 1)

            def ml_turn(_):
                for h in range(4):
                    act.wait_ge(m_turned, h + 1)
                    nc.scalar.activation(yml[0][:, h, :], bank[4 + h][:, :], ACT.Copy).then_inc(m_hi_s, 1)

            steps = {"mem_scores": mem_scores, "mem_turn": mem_turn, "mem_out": mem_out, "cmp_hidden": cmp_hidden,
                     "ml_gates": ml_gates, "ml_rows": ml_rows, "ml_scores": ml_scores, "ml_out": ml_out, "ml_turn": ml_turn}
            for what, n in SCHEDULE:
                if what == "unit":
                    high_next(n)
                    evacuate(n)
                elif what in steps:
                    steps[what](n)

            with act.Fori(0, GROUPS) as g:
                high(g + U_NSA // 2, 1)
                act.wait_ge(w_used, g * 2 + (U_NSA + 1))
                nc.scalar.activation(qT[:, 0, :], bank[0][:, :], ACT.Copy).then_inc(q_act, 1)
                high(g + (U_NSA // 2 + 1), 0)
                act.wait_ge(c_sh, g + 1)
                nc.scalar.activation(p_c[:, :, :, :], p_c[:, :, :, :], ACT.Exp, scale=DH ** -0.5).then_inc(c_e, 1)

                def exp_step(i):
                    br, qb, hh = STEPS[i]
                    n = P * (qb + 1)
                    act.wait_ge(s_m, g * NS + (i + 1))
                    nc.scalar.activation(prob[i % 4][:, 0:n], prob[i % 4][:, 0:n], ACT.Exp, bias=nmax[:, i:i + 1], scale=-1.0,
                                         accum_out=psum_row[:, i:i + 1]).then_inc(s_e, 1)

                def turn_step(i):
                    if i % 2 == 0:
                        br, qb, hh = STEPS[i]
                        n = P * (qb + 1)
                        act.wait_ge(s_t, g * NS + (i + 1))
                        nc.scalar.activation(probT[i % 4][:, 0:n], bank[5 + i % 2][:, 0:n], ACT.Copy).then_inc(s_pa, 1)

                for i in range(NS + 2):
                    if i < NS:
                        exp_step(i)
                    if i >= 2:
                        turn_step(i - 2)
                act.wait_ge(c_t, g + 1)
                for qb in range(TT):
                    ins = nc.scalar.activation(pT_c[:, HPG * qb:HPG * (qb + 1), :],
                                               bank[CMP_BANK[qb]][0:NC, :].rearrange("p (h q) -> p h q", q=P), ACT.Copy)
                ins.then_inc(c_ta, 1)

            def merge(c):
                for b in range(3):
                    n3 = c * 3 + b
                    h2 = c * 3 + (U_MERGE // 2 + b)
                    high(h2, 1)
                    act.wait_ge(w_used, h2 * 2 + 1)
                    for t in range(2):
                        if not isinstance(n3, int) or n3 > 0:
                            act.wait_ge(mg_used, n3 * 2)
                        nc.scalar.activation(mg[t][:, :], bank[t][:, :], ACT.Sigmoid).then_inc(mg_gate, 1)
                    high(h2 + 1, 0)

            merge(0)
            with act.Fori(1, 4) as c:
                merge(c)
            for n in range(4):
                high_next(U_WOUT + n)
            root_of_sum(1)

            for f in range(5):
                def up(i, first=False):
                    u2 = i + U_FFN[f] // 2
                    n = i * 2 + 2 * UP_STEPS * f
                    high(u2, 1)
                    if first:
                        root_of_sum(R_EVENT[f] if f < 4 else 9)
                    for t in range(2):
                        act.wait_ge(g_scaled, n + (t + 1))
                        nc.scalar.activation(tg[t][:, :], tg[t][:, :], ACT.Silu).then_inc(silu_done, 1)
                    high(u2 + 1, 0)

                up(0, True)
                with act.Fori(1, UP_STEPS) as i:
                    up(i)
                for n in range(12):
                    high_next(U_FFN[f] + 2 * UP_STEPS + n)
                if f == 0:
                    root_of_sum(3)
                if f == 1:
                    root_of_sum(5)
                    for n in range(2):
                        high_next(U_POOL + n)
                if f == 3:
                    root_of_sum(8)
                    for n in range(4):
                        u = U_PW1 + 2 * n
                        high_next(u)
                        for t in range(2):
                            act.wait_ge(w_used, u + 1)
                            if n > 0:
                                act.wait_ge(glu, 2 * n)
                            nc.scalar.activation(tg[t][:, :], bank[t][:, :], ACT.Sigmoid,
                                                 bias=col("conv_b_pw1_2", 2 * n + t, 1)).then_inc(glu_arg, 1)
                        high_next(u + 1)
                    act.wait_ge(ln_used, KT)
                    nc.scalar.activation(rb[:, :], bank[5][:, :], ACT.Sqrt, bias=ln_eps, scale=1.0 / D).then_inc(root, 1)
                    for j in range(KT):
                        act.wait_ge(ln_z, j + 1)
                        nc.scalar.activation(hy[:, j, :], hy[:, j, :], ACT.Silu, bias=col("conv_ln_b_2", j)).then_inc(ln_act, 1)
                    for n in range(4):
                        high_next(U_PW2 + n)

            act.wait_ge(fin_turned, 1)
            for t in range(TT):
                for b in range(2):
                    chain.link(act, nc.scalar.activation(junk3[:, :], bank[2 * t + b][:, :], ACT.Square,
                                                         accum_out=stat[:, 32 + 2 * t + b:33 + 2 * t + b]))
            act.sem_inc(fin_sq, 1)
            act.wait_ge(fin_sum, 1)
            nc.scalar.activation(stat[:, 44:48], stat[:, 40:44], ACT.Sqrt, bias=eps, scale=1.0 / D).then_inc(fin_root, 1)

        @block.gpsimd
        def _(pool):
            def low_part(u, s):
                pool.wait_ge(w_hi_ready, u + 1)
                nc.gpsimd.tensor_tensor(w_lo[s][:, :], raw[s][:, :], w_hi[s][:, :].bitcast(F32), ALU.subtract).then_inc(w_lo_ready, 1)

            def low_next(u):
                if u + 1 < N_UNITS:
                    low_part(u + 1, (u + 1) % 2)

            def clear():
                nc.gpsimd.memset(ssq[:, :], 0.0).then_inc(sq_added, 1)
                tally[0] += 1
                pool.wait_ge(sq_added, tally[0])

            def add_square(k):
                pool.wait_ge(sq_ready, k + 1)
                nc.gpsimd.tensor_tensor(ssq[:, :], ssq[:, :], sq[k % 2][:, :], ALU.add).then_inc(sq_added, 1)
                tally[0] += 1
                pool.wait_ge(sq_added, tally[0])

            def clear_after(n):
                pool.wait_ge(sumsq, n)
                clear()

            tally = [0]
            low_part(0, 0)
            for u in range(NFIX):
                low_next(u)
            with pool.Fori(0, GROUPS) as g:
                low_part(g * 2 + (U_NSA + 1), 1)
                low_part(g * 2 + (U_NSA + 2), 0)
            with pool.Fori(0, 12) as i:
                low_part(i * 2 + (U_MERGE + 1), 1)
                low_part(i * 2 + (U_MERGE + 2), 0)
            pool.wait_ge(mg_split, 8)
            clear()
            for n in range(4):
                low_next(U_WOUT + n)
                for t in range(2):
                    add_square(2 * n + t)
            clear_after(1)
            for j in range(KT):
                add_square(8 + j)
            for f in range(5):
                low_part(U_FFN[f] + 1, 1)
                clear_after(R_EVENT[f] if f < 4 else 9)
                low_part(U_FFN[f] + 2, 0)
                with pool.Fori(1, UP_STEPS) as i:
                    low_part(i * 2 + (U_FFN[f] + 1), 1)
                    low_part(i * 2 + (U_FFN[f] + 2), 0)
                for c in range(4):
                    for n in range(3):
                        low_next(U_FFN[f] + 2 * UP_STEPS + 3 * c + n)
                    if f < 4:
                        for t in range(2):
                            add_square(SQ_BASE[f] + 2 * c + t)
                if f == 0:
                    clear_after(3)
                    for j in range(KT):
                        add_square(24 + j)
                if f == 1:
                    clear_after(5)
                    for n in range(2):
                        low_next(U_POOL + n)
                    for j in range(KT):
                        add_square(40 + j)
                if f == 3:
                    clear_after(8)
                    for n in range(8):
                        low_next(U_PW1 + n)
                    for n in range(4):
                        low_next(U_PW2 + n)
                        for t in range(2):
                            add_square(64 + 2 * n + t)

        @block.tensor
        def _(pe):
            def products(s, kt, cols, x, banks, n=T, k0=0, k_all=None, ready=None):
                k_all = kt if k_all is None else k_all
                for k in range(kt):
                    if ready is not None:
                        ready(k)
                    for t, b in enumerate(banks):
                        c = k * cols + t * P
                        wh, wl = w_hi[s][:, c:c + P], w_lo[s][:, c:c + P]
                        xh, xl = x[0][:, k0 + k, 0:n], x[1][:, k0 + k, 0:n]
                        first, last = k0 + k == 0, k0 + k == k_all - 1
                        nc.tensor.matmul(bank[b][:, 0:n], wh, xh, start=first, stop=False)
                        nc.tensor.matmul(bank[b][:, 0:n], wh, xl, start=False, stop=False)
                        ins = nc.tensor.matmul(bank[b][:, 0:n], wl, xh, start=False, stop=last)
                ins.then_inc(w_used, 1)

            def token_products(s, cols, x, tiles, b0):
                for t in range(tiles):
                    out_ = bank[b0 + t // 2][:, UC * (t % 2):UC * (t % 2) + cols]
                    for k in range(KT):
                        xh, xl = x[0][:, k, t * P:(t + 1) * P], x[1][:, k, t * P:(t + 1) * P]
                        wh, wl = w_hi[s][:, k * cols:(k + 1) * cols], w_lo[s][:, k * cols:(k + 1) * cols]
                        nc.tensor.matmul(out_, xh, wh, start=k == 0, stop=False)
                        nc.tensor.matmul(out_, xh, wl, start=False, stop=False)
                        ins = nc.tensor.matmul(out_, xl, wh, start=False, stop=k == KT - 1)
                ins.then_inc(w_used, 1)

            def sum_of_squares():
                nc.tensor.matmul(bank[4][:, :], ones, ssq[:, :], start=True, stop=True).then_inc(sumsq, 1)

            pe.wait_ge(const_in_place, 16)
            pe.wait_ge(rows_in_place, 16 * (len(ROWS) + 4))
            for j in range(KT):
                nc.tensor.transpose(bank[7][:, j * NROWS:(j + 1) * NROWS], rows[0:NROWS, j * P:(j + 1) * P], cid[0:NROWS, 0:NROWS])
            for b in range(2):
                ins = nc.tensor.transpose(bank[7][:, 448 + 32 * b:480 + 32 * b], pe_rows[0:32, b, :], cid[0:32, 0:32])
            ins.then_inc(vec_turned, 1)
            for n in range(16):
                if n == 7:
                    pe.wait_ge(vec_ready, 1)
                if n >= 8:
                    pe.wait_ge(start_lo, n - 7)
                pe.wait_ge(tok_scaled, MT if n < 8 else 6)
                j = n % 8
                for t in range(MT if n < 8 else TT):
                    src = mem_tok if n < 8 else x_tok
                    ins = nc.tensor.transpose(bank[j][:, t * P:(t + 1) * P], src[:, t, j * P:(j + 1) * P], ident)
                ins.then_inc(tok_turned, 1)

            def unit(u):
                w, c, n, kind = UNITS[u]
                s, b0 = u % 2, 2 * (u % 2)
                pe.wait_ge(w_lo_ready, u + 1)
                if u < 2:
                    pe.wait_ge(start_lo, 12)
                else:
                    pe.wait_ge(evac_act, u - 1)
                    pe.wait_ge(evac_dve, max(1, DVE_EVACS[u - 1]))
                if u == 4:
                    pe.wait_ge(start_lo, 16)
                if kind == "mem_k":
                    products(s, KT, n, (m_hi, m_lo), (b0, b0 + 1), MEM)
                elif kind == "mem_v":
                    token_products(s, n, (m_hi, m_lo), MT, b0)
                elif kind in FEATURE_MAJOR:
                    products(s, KT, n, (h_hi, h_lo), (b0, b0 + 1))
                else:
                    token_products(s, n, (h_hi, h_lo), TT, b0)

            def mem_scores(h):
                pe.wait_ge(evac_act, 6)
                pe.wait_ge(evac_dve, DVE_EVACS[6])
                if h > 0:
                    pe.wait_ge(mem_y, h)
                for qb in range(TT):
                    ins = nc.tensor.matmul(bank[4 + qb // 2][:, 256 * (qb % 2):256 * (qb % 2) + 256],
                                           q_mem[:, h, qb * P:(qb + 1) * P], k_mem[:, h, :], start=True, stop=True)
                ins.then_inc(mem_s, 1)

            def mem_turn(h):
                pe.wait_ge(mem_p, h + 1)
                for m in range(MT):
                    for qb in range(TT):
                        ins = nc.tensor.transpose(bank[6 + m][:, qb * P:(qb + 1) * P], p_mem[:, qb, m * P:(m + 1) * P], ident)
                ins.then_inc(mem_t, 1)

            def mem_out(h):
                pe.wait_ge(mem_ta, h + 1)
                pe.wait_ge(mem_td, h + 1)
                for m in range(MT):
                    ins = nc.tensor.matmul(bank[4][:, :], v_mem[:, m, h * P:(h + 1) * P], pt_mem[:, m, :], start=m == 0, stop=m == MT - 1)
                ins.then_inc(mem_o, 1)

            def cmp_hidden(b):
                pe.wait_ge(w1_landed, 32 * (b + 1))
                pe.wait_ge(cmp_ab, b + 1)
                if b == 0:
                    pe.wait_ge(mem_y, 4)
                else:
                    pe.wait_ge(cmp_hs, 1)
                for l in range(32):
                    for par in range(2):
                        lo, hi = DH * par, DH * (par + 1)
                        src = (cmp_a if l < 16 else cmp_b)[lo:hi, :, :].rearrange("p t (n r) -> p t n r", r=16)
                        ins = nc.tensor.matmul(bank[4 + par][:, 0:2 * NC].rearrange("p (t n) -> p t n", n=NC), cmp_w1[lo:hi, l, :],
                                               src[:, :, l // 16:l // 16 + NC, l % 16], start=l == 0, stop=l == 31)
                ins.then_inc(cmp_h, 1)

            def cmp_out(b):
                pe.wait_ge(w2_landed, 48)
                pe.wait_ge(cmp_hs, b + 1)
                pe.wait_ge(mem_td, 4)
                if b == 0:
                    ins = nc.tensor.matmul(bank[6][:, 0:4 * NC], w2k[:, :, :].rearrange("p a d -> p (a d)"),
                                           hid_c[:, :, :, :].rearrange("p a t n -> p (a t n)"), start=True, stop=True)
                else:
                    pe.wait_ge(cmp_e, 1)
                    for par in range(2):
                        for t in range(2):
                            g = 2 * t + par
                            ins = nc.tensor.matmul(bank[6][0:NC, g * DH:(g + 1) * DH], hid_c[:, par, t, :], w2v[:, :],
                                                   start=True, stop=True)
                ins.then_inc(cmp_o, 1)

            def ml_gates(_):
                pe.wait_ge(evac_act, 14)
                pe.wait_ge(cmp_e, 2)
                for half in range(2):
                    for t in range(TT):
                        ins = nc.tensor.transpose(bank[6 + half][0:4, t * P:(t + 1) * P], if_tok[:, t, 4 * half:4 * half + 4], ident)
                ins.then_inc(if_turned, 1)

            def ml_rows(_):
                pe.wait_ge(g_rows, 1)
                for i, src in enumerate((row4[0], row4[2])):
                    for t in range(TT):
                        c = 16 * i + 4 * t
                        ins = nc.tensor.transpose(bank[7][:, c:c + 4], src[:, t * P:(t + 1) * P], cid[0:4, 0:4])
                ins.then_inc(g_turned, 1)

            def ml_scores(h):
                if h == 0:
                    pe.wait_ge(qk_ready, 8)
                    pe.wait_ge(cmp_e, 2)
                    pe.wait_ge(g_cols, 1)
                    pe.wait_ge(emt_ready, 1)
                    pe.wait_ge(ml_const, 64)
                else:
                    pe.wait_ge(m_h, h)
                nc.tensor.matmul(bank[4][:, :], sel4[:, h, :], row4[5][:, :], start=True, stop=True).then_inc(bc_ready, 1)
                for sb in range(TT):
                    n = TT * h + sb
                    if n >= 2:
                        pe.wait_ge(s_masked, n - 1)
                    nc.tensor.matmul(bank[5 + n % 2][:, 0:T - P * sb], qk_in[:, 4 + h, 3 + P * sb:3 + P * (sb + 1)],
                                     qk_in[:, h, 3 + P * sb:3 + T], start=True, stop=True).then_inc(sT_ready, 1)

            def ml_out(h):
                pe.wait_ge(s_masked, TT * (h + 1))
                pe.wait_ge(evac_act, NFIX)
                pe.wait_ge(evac_dve, DVE_EVACS[NFIX])
                for tb in range(TT):
                    for sb in range(tb + 1):
                        c = (P + 1) * (tb % 2)
                        ins = nc.tensor.matmul(bank[7 if tb < 2 else 4][:, c:c + P + 1], s_ml[:, sb, tb * P:(tb + 1) * P],
                                               v_ml[:, sb, h, :], start=sb == 0, stop=sb == tb)
                ins.then_inc(mo_ready, 1)

            def ml_turn(_):
                pe.wait_ge(m_y, 16)
                for h in range(4):
                    for t in range(TT):
                        ins = nc.tensor.transpose(bank[4 + h][:, t * P:(t + 1) * P], h_mlt[:, t, h * P:(h + 1) * P], ident)
                    ins.then_inc(m_turned, 1)

            steps = {"unit": unit, "mem_scores": mem_scores, "mem_turn": mem_turn, "mem_out": mem_out, "cmp_hidden": cmp_hidden,
                     "cmp_out": cmp_out, "ml_gates": ml_gates, "ml_rows": ml_rows, "ml_scores": ml_scores, "ml_out": ml_out,
                     "ml_turn": ml_turn}
            for what, n in SCHEDULE:
                steps[what](n)

            pe.wait_ge(m_lo_s, 4)
            with pe.Fori(0, GROUPS) as g:
                for s in range(2):
                    pe.wait_ge(w_lo_ready, g * 2 + (U_NSA + s + 1))
                    products(s, KT, P, (h_hi, h_lo), (s,))
                pe.wait_ge(q_act, g + 1)
                pe.wait_ge(q_dve, g + 1)
                def head_rows(hh):
                    return DH * (hh % 2), DH * (hh % 2 + 1)

                for qb in range(TT):
                    for hh in range(HPG):
                        lo, hi = head_rows(hh)
                        c = NC * (2 * qb + hh // 2)
                        ins = nc.tensor.matmul(bank[hh % 2][:, c:c + NC], qT[lo:hi, hh // 2, qb * P:(qb + 1) * P], kc_g[lo:hi, :],
                                               start=True, stop=True)
                ins.then_inc(c_s, 1)
                pe.wait_ge(kd_landed, g * 64 + 64)

                def scores(i):
                    br, qb, hh = STEPS[i]
                    lo, hi = head_rows(hh)
                    n = P * (qb + 1)
                    if i >= 3:
                        pe.wait_ge(s_m, g * NS + (i - 2))
                    nc.tensor.matmul(bank[2 + i % 3][:, 0:n], qT[lo:hi, hh // 2, qb * P:(qb + 1) * P], k_dup[br][lo:hi, 0:n],
                                     start=True, stop=True).then_inc(s_s, 1)

                def turn(i):
                    br, qb, hh = STEPS[i]
                    pe.wait_ge(s_e, g * NS + (i + 1))
                    if i >= 2:
                        pe.wait_ge(s_pa if i % 2 == 0 else s_pd, g * (NS // 2) + i // 2)
                    for kb in range(qb + 1):
                        ins = nc.tensor.transpose(bank[5 + i % 2][:, kb * P:(kb + 1) * P], prob[i % 4][:, kb * P:(kb + 1) * P], ident)
                    ins.then_inc(s_t, 1)

                def weigh(i):
                    br, qb, hh = STEPS[i]
                    pe.wait_ge(s_pa if i % 2 == 0 else s_pd, g * (NS // 2) + (i // 2 + 1))
                    if i % HPG == 0 and i >= 2 * HPG:
                        pe.wait_ge(s_or, g * (NS // HPG) + (i // HPG - 1))
                    c = DH * hh
                    for kb in range(qb + 1):
                        ins = nc.tensor.matmul(bank[OUT_BANK[i // HPG % 2]][:, c:c + DH], probT[i % 4][:, kb * P:(kb + 1) * P],
                                               v_sw[br][:, kb, bass.ds(g * DH, DH)], start=kb == 0, stop=kb == qb)
                    ins.then_inc(s_o, 1)

                for i in range(NS + 3):
                    if i < NS:
                        scores(i)
                    if 2 <= i < NS + 2:
                        turn(i - 2)
                    if i >= 3:
                        weigh(i - 3)
                pe.wait_ge(c_p, g + 1)
                for qb in range(TT):
                    for hh in range(HPG):
                        ins = nc.tensor.transpose(bank[CMP_BANK[qb]][0:NC, hh * P:(hh + 1) * P], p_c[:, qb, hh, :], ident)
                ins.then_inc(c_t, 1)
                pe.wait_ge(c_ta, g + 1)
                for qb in range(TT):
                    for hh in range(HPG):
                        c = 256 * (qb % 2) + DH * hh
                        ins = nc.tensor.matmul(bank[0 if qb < 2 else 5][:, c:c + DH], pT_c[:, HPG * qb + hh, :],
                                               vcmp[0:NC, bass.ds(g, 1), :].rearrange("p a d -> p (a d)"), start=True, stop=True)
                ins.then_inc(c_o, 1)
                pe.wait_ge(y_done, g + 1)
                for t in range(2):
                    for qb in range(TT):
                        ins = nc.tensor.transpose(bank[6 + t][:, qb * P:(qb + 1) * P], y_tok[:, qb, t * P:(t + 1) * P], ident)
                    ins.then_inc(y_turned, 1)
                pe.wait_ge(y_split, g * 2 + 2)

            def merge(c):
                for b in range(3):
                    n3 = c * 3 + b
                    u = c * 6 + (U_MERGE + 2 * b)
                    pe.wait_ge(w_lo_ready, u + 1)
                    if not isinstance(n3, int) or n3 > 0:
                        pe.wait_ge(mg_used, n3 * 2)
                    products(0, KT, UC, (h_hi, h_lo), (0, 1))
                    pe.wait_ge(w_lo_ready, u + 2)
                    products(1, KT if b == 0 else 4, UC, (ynsa, yml, ymem)[b], (2, 3))

            merge(0)
            with pe.Fori(1, 4) as c:
                merge(c)
            for n in range(4):
                pe.wait_ge(w_lo_ready, U_WOUT + n + 1)
                if n == 0:
                    pe.wait_ge(mg_split, 8)
                if n >= 2:
                    pe.wait_ge(o_ready, 2 * n - 2)
                products(n % 2, KT, UC, ym, (2 * (n % 2), 2 * (n % 2) + 1))
            pe.wait_ge(x_again, 16)
            for j in range(KT):
                if j == 3:
                    pe.wait_ge(o_ready, 8)
                    pe.wait_ge(sq_added, 9)
                    sum_of_squares()
                if j == 7:
                    pe.wait_ge(x_new, 1)
                b = (5, 6, 7, 0, 1, 2, 3)[j % 7]
                for t in range(TT):
                    ins = nc.tensor.transpose(bank[b][:, t * P:(t + 1) * P], x_tok2[:, t, j * P:(j + 1) * P], ident)
                ins.then_inc(x_turned, 1)

            SUM_AT = {event: 9 * event for event in range(2, 10)}

            for f in range(5):
                event = R_EVENT[f] if f < 4 else 9

                def up(i, first=False):
                    u = i * 2 + U_FFN[f]
                    n = i * 2 + 2 * UP_STEPS * f
                    pe.wait_ge(w_lo_ready, u + 1)
                    if not first:
                        pe.wait_ge(g_scaled, n)
                    ready = (lambda k: pe.wait_ge(h_ready, KT * H_EVENT[f] + k + 1)) if first else None
                    products(0, KT, UC, (h_hi, h_lo), (0, 1), ready=ready)
                    if first:
                        pe.wait_ge(sq_added, SUM_AT[event])
                        sum_of_squares()
                    pe.wait_ge(w_lo_ready, u + 2)
                    if not first:
                        pe.wait_ge(up_read, n)
                    products(1, KT, UC, (h_hi, h_lo), (2, 3))

                if f == 0:
                    pe.wait_ge(x_new, 8)
                if f == 2:
                    pe.wait_ge(x_new, 24)
                up(0, True)
                with pe.Fori(1, UP_STEPS) as i:
                    up(i)
                for c in range(4):
                    k0 = 0
                    for m, k in enumerate(DOWN_K):
                        u = U_FFN[f] + 2 * UP_STEPS + 3 * c + m
                        pe.wait_ge(w_lo_ready, u + 1)
                        if m == 0:
                            if c >= 2:
                                pe.wait_ge(o_ready, 8 + 8 * f + 2 * (c - 1))
                            else:
                                pe.wait_ge(rstd, R_EVENT[f])
                        ready = (lambda kk: pe.wait_ge(hid_ready, HT * f + k0 + kk + 1)) if c == 0 else None
                        products(u % 2, k, UC, hid, (4 + 2 * (c % 2), 5 + 2 * (c % 2)), k0=k0, k_all=HT, ready=ready)
                        k0 += k
                if f == 0:
                    pe.wait_ge(sq_added, SUM_AT[3])
                    sum_of_squares()
                if f == 1:
                    pe.wait_ge(sq_added, SUM_AT[5])
                    sum_of_squares()
                    pe.wait_ge(rstd, 5)
                    for n in range(2):
                        pe.wait_ge(w_lo_ready, U_POOL + n + 1)
                        if n == 0:
                            pe.wait_ge(o_ready, 24)
                        for q in range(4):
                            gi, t = q // 2, q % 2
                            pe.wait_ge(pooled, 4 * n + 2 * gi + 2)
                            for k in range(2):
                                c = (2 * gi + k) * UC + t * P
                                b = bank[4 - 4 * n + q][:, :]
                                j = 4 * n + 2 * gi + k
                                nc.tensor.matmul(b, w_hi[n][:, c:c + P], h_hi[:, j, :], start=k == 0, stop=False)
                                nc.tensor.matmul(b, w_hi[n][:, c:c + P], h_lo[:, j, :], start=False, stop=False)
                                ins = nc.tensor.matmul(b, w_lo[n][:, c:c + P], h_hi[:, j, :], start=False, stop=k == 1)
                        ins.then_inc(w_used, 1)
                if f == 3:
                    pe.wait_ge(sq_added, SUM_AT[8])
                    sum_of_squares()
                    for n in range(4):
                        u = U_PW1 + 2 * n
                        pe.wait_ge(w_lo_ready, u + 1)
                        if n > 0:
                            pe.wait_ge(glu_arg, 2 * n)
                        ready = (lambda k: pe.wait_ge(h_ready, KT * 4 + k + 1)) if n == 0 else None
                        products(0, KT, UC, (h_hi, h_lo), (0, 1), ready=ready)
                        pe.wait_ge(w_lo_ready, u + 2)
                        if n > 0:
                            pe.wait_ge(glu, 2 * n)
                        products(1, KT, UC, (h_hi, h_lo), (2, 3))
                    for j in range(KT):
                        pe.wait_ge(conv_y, j + 1)
                        ins = nc.tensor.matmul(bank[4][:, :], ones, hy[:, j, :], start=j == 0, stop=j == KT - 1)
                    ins.then_inc(mean_s, 1)
                    for j in range(KT):
                        pe.wait_ge(ln_sq, j + 1)
                        ins = nc.tensor.matmul(bank[5][:, :], ones, sq[j % 2][:, :], start=j == 0, stop=j == KT - 1)
                        ins.then_inc(ln_used, 1)
                    for n in range(4):
                        pe.wait_ge(w_lo_ready, U_PW2 + n + 1)
                        if n >= 2:
                            pe.wait_ge(x_new, 24 + 2 * (n - 1))
                        ready = (lambda k: pe.wait_ge(ln_h, k + 1)) if n == 0 else None
                        products(n % 2, KT, UC, (h_hi, h_lo), (4 + 2 * (n % 2), 5 + 2 * (n % 2)), ready=ready)
            pe.wait_ge(o_ready, 48)
            for t in range(TT):
                for j in range(KT):
                    ins = nc.tensor.transpose(bank[2 * t + j // 4][:, (j % 4) * P:(j % 4 + 1) * P], X[:, j, t * P:(t + 1) * P], ident)
            ins.then_inc(fin_turned, 1)

        @block.vector
        def _(dve):
            chain = Chain(dve_chain_s)
            v = nc.vector

            def link(ins):
                chain.link(dve, ins)

            def mark(ins, s, n):
                ins.then_inc(s, 1)
                dve.wait_ge(s, n)

            link(v.memset(stat[:, 0:1], EPS))
            v.memset(stat[:, 1:2], LN_EPS).then_inc(stat_set, 1)
            dve.wait_ge(tok_root, 1)
            link(v.reciprocal(rs_tok[:, 0:6], rs_tok[:, 0:6]))
            for t in range(6):
                src = mem_tok[:, t, :] if t < MT else x_tok[:, t - MT, :]
                v.tensor_scalar(src, src, rs_tok[:, t:t + 1], None, ALU.mult).then_inc(tok_scaled, 1)
            dve.wait_ge(vec_turned, 1)
            link(v.tensor_copy(vec[:, 0:KT * NROWS], bank[7][:, 0:KT * NROWS]))
            mark(v.tensor_copy(vec[:, 448:512], bank[7][:, 448:512]), vec_ready, 1)
            for n in range(16):
                dve.wait_ge(start_hi, n + 1)
                j = n % 8
                if n < 8:
                    ins = v.scalar_tensor_tensor(m_lo[:, j, :], bank[j][:, 0:MEM], col("g_mem", j), m_hi[:, j, :].bitcast(F32),
                                                 ALU.mult, ALU.subtract)
                else:
                    ins = v.scalar_tensor_tensor(h_lo[:, j, :], bank[j][:, :], col("g_pre_mix", j), h_hi[:, j, :].bitcast(F32),
                                                 ALU.mult, ALU.subtract)
                ins.then_inc(start_lo, 1)

            def unit(u):
                w, c, n, kind = UNITS[u]
                if kind in ACT_ONLY:
                    return
                b1 = bank[2 * (u % 2) + 1]
                v1 = b1[:, :].rearrange("p (t c) -> p t c", c=UC)
                dve.wait_ge(w_used, u + 1)
                if u == 14:
                    link(v.memset(qk_in[:, :, 0:3], 0.0))
                if u == 18:
                    link(v.memset(v_ml[:, :, :, P:P + 1], 1.0))
                if kind == "mem_k":
                    ins = v.tensor_copy(k_mem[:, 2 * u + 1, :], b1[:, 0:MEM])
                elif kind == "q_mem":
                    ins = v.tensor_copy(q_mem[:, 2 * (u - 4) + 1, :], b1[:, :])
                elif kind in ("kc", "vc"):
                    ins = v.tensor_copy(kv_c[u - 6][:, 1, :], b1[:, :])
                elif kind in ("ks", "kw"):
                    ins = v.tensor_copy(k_stage[u - 8][:, 1, :], b1[:, :])
                elif kind in ("vs", "vw"):
                    ins = v.tensor_copy(v_sw[u - 10][:, 2:4, :], v1)
                elif kind == "qk":
                    ins = v.tensor_copy(qk_in[:, 2 * (u - 14) + 1, 3:3 + T], b1[:, :])
                else:
                    h0 = 2 * (u - 18)
                    link(v.tensor_copy(v_ml[:, 2, h0:h0 + 2, 0:P], v1[:, 0, :].rearrange("p (h d) -> p h d", d=P)))
                    ins = v.tensor_copy(v_ml[:, 3, h0:h0 + 2, 0:P], v1[:, 1, :].rearrange("p (h d) -> p h d", d=P))
                mark(ins, evac_dve, DVE_EVACS[u + 1])
                if kind == "qk":
                    dve.wait_ge(evac_act, u + 1)
                    for j in range(2 * (u - 14), 2 * (u - 14) + 2):
                        acc = conv_acc[j % 2][:, :]
                        if j >= 2:
                            dve.wait_ge(qk_ready, j - 1)
                        link(v.tensor_scalar(acc, qk_in[:, j, 0:T], col("ml_conv_w", j, 0), col("ml_conv_b", j), ALU.mult, ALU.add))
                        for k in range(1, 4):
                            ins = v.scalar_tensor_tensor(acc, qk_in[:, j, k:k + T], col("ml_conv_w", j, k), acc, ALU.mult, ALU.add)
                            if k < 3:
                                link(ins)
                        ins.then_inc(conv_done, 1)

            def mem_scores(h):
                dve.wait_ge(mem_s, h + 1)
                for b in range(2):
                    link(v.reduce_max(stat[:, 32 + 2 * b:34 + 2 * b], bank[4 + b][:, :].rearrange("p (q m) -> p q m", m=MEM), AX_X))
                v.tensor_scalar(stat[:, 32:36], stat[:, 32:36], -(P ** -0.5), None, ALU.mult).then_inc(mem_m, 1)
                dve.wait_ge(mem_e, h + 1)
                link(v.reciprocal(stat[:, 36:40], stat[:, 36:40]))
                for qb in range(TT):
                    ins = v.tensor_scalar(p_mem[:, qb, :], p_mem[:, qb, :], stat[:, 36 + qb:37 + qb], None, ALU.mult)
                mark(ins, mem_p, h + 1)

            def mem_turn(h):
                dve.wait_ge(mem_t, h + 1)
                v.tensor_copy(pt_mem[:, 1, :], bank[7][:, :]).then_inc(mem_td, 1)

            def mem_out(h):
                dve.wait_ge(mem_yh, h + 1)
                v.tensor_tensor(ymem[1][:, h, :], bank[4][:, :], ymem[0][:, h, :].bitcast(F32), ALU.subtract).then_inc(mem_y, 1)

            def cmp_hidden(b):
                dve.wait_ge(evac_act, 7 + b)
                if b == 1:
                    dve.wait_ge(cmp_h, 1)
                src = kv_c[b][:, :, :].rearrange("p t (n r) -> p (t n) r", r=16)
                for half, dst in enumerate((cmp_a, cmp_b)):
                    pos = pe_cols[b][:, 16 * half:16 * half + 16].unsqueeze(1).to_broadcast([P, 64, 16])
                    ins = v.tensor_tensor(dst[:, :, :].rearrange("p t (n r) -> p (t n) r", r=16), src, pos, ALU.add)
                ins.then_inc(cmp_ab, 1)

            def cmp_out(b):
                dve.wait_ge(cmp_o, b + 1)
                if b == 0:
                    ins = v.tensor_copy(kcmp[:, :, :].rearrange("p (t a) n -> p a t n", a=2),
                                        bank[6][:, 0:4 * NC].rearrange("p (a t n) -> p a t n", a=2, t=2))
                else:
                    ins = v.tensor_copy(vcmp[0:NC, :, :].rearrange("p g d -> p (g d)"), bank[6][0:NC, 0:GROUPS * DH])
                ins.then_inc(cmp_e, 1)

            def ml_rows(_):
                link(v.memset(ones4[:, :], 1.0))
                dve.wait_ge(if_rows, 1)
                link(v.tensor_scalar(row4[2][:, :], row4[1][:, :], -1.0, None, ALU.mult))
                v.tensor_tensor(row4[2][:, :], row4[1][:, :], row4[2][:, :], ALU.min).then_inc(f_min, 1)
                dve.wait_ge(f_log, 1)
                link(v.scalar_tensor_tensor(row4[1][:, :], row4[1][:, :], 0.0, row4[2][:, :], ALU.min, ALU.subtract))
                link(v.tensor_tensor_scan(row4[3][:, :], ones4[:, :], row4[1][:, :], 0.0, ALU.mult, ALU.add))
                link(v.tensor_tensor(row4[0][:, :], row4[0][:, :], row4[3][:, :], ALU.subtract))
                link(v.tensor_tensor_scan(row4[4][:, :], row4[0][:, :], row4[0][:, :], 0.0, ALU.max, ALU.max))
                link(v.tensor_scalar(row4[5][:, :], row4[4][:, :], -1.0, None, ALU.mult))
                mark(v.tensor_tensor(row4[2][:, :], row4[3][:, :], row4[4][:, :], ALU.add), g_rows, 1)
                dve.wait_ge(emt_ready, 1)
                mark(v.tensor_copy(g_col, bank[7][:, 0:16]), g_cols, 1)

            def ml_scores(h):
                dve.wait_ge(bc_ready, h + 1)
                if h == 0:
                    dve.wait_ge(k_stored, 32)
                else:
                    dve.wait_ge(mo_ready, h)

                def argument(sb):
                    n = TT * h + sb
                    v.tensor_scalar(d_ml[n % 2][:, 0:T - P * sb], bank[4][:, P * sb:T], g_col[:, 4 * sb + h:4 * sb + h + 1], 0.0,
                                    ALU.add, ALU.min).then_inc(d_arg, 1)

                argument(0)
                for sb in range(TT):
                    n = TT * h + sb
                    if sb + 1 < TT:
                        argument(sb + 1)
                    dve.wait_ge(d_exp, n + 1)
                    dve.wait_ge(sT_ready, n + 1)
                    link(v.scalar_tensor_tensor(s_ml[:, sb, P * sb:T], bank[5 + n % 2][:, 0:T - P * sb], P ** -0.5,
                                                d_ml[n % 2][:, 0:T - P * sb], ALU.mult, ALU.mult))
                    diag = s_ml[:, sb, P * sb:P * (sb + 1)]
                    mark(v.tensor_tensor(diag, diag, tri, ALU.mult), s_masked, n + 1)

            def ml_out(h):
                dve.wait_ge(mo_ready, h + 1)
                if h > 0:
                    dve.wait_ge(m_h, h)
                for b in range(2):
                    link(v.tensor_copy(den2[:, 2 * b:2 * b + 2], bank[7 - 3 * b][:, P:2 * P + 2:P + 1]))
                link(v.scalar_tensor_tensor(den, den2, -1.0, den2, ALU.mult, ALU.max))
                link(v.tensor_tensor(den, den, emt[:, h:16:4], ALU.max))
                mark(v.reciprocal(den, den), m_rec, h + 1)

            def ml_turn(_):
                for tb in range(TT):
                    link(v.tensor_tensor(o_ml[:, tb, :], o_ml[:, tb, :], head_g[:, :], ALU.mult))
                dve.wait_ge(m_root, 1)
                link(v.reciprocal(rr_ml, rr_ml))
                for h in range(4):
                    for tb in range(TT):
                        y = h_mlt[:, tb, P * h:P * (h + 1)]
                        v.scalar_tensor_tensor(y, y, rr_ml[:, 4 * tb + h:4 * tb + h + 1], o_ml[:, tb, P * h:P * (h + 1)],
                                               ALU.mult, ALU.mult).then_inc(m_y, 1)
                for h in range(4):
                    dve.wait_ge(m_hi_s, h + 1)
                    mark(v.tensor_tensor(yml[1][:, h, :], bank[4 + h][:, :], yml[0][:, h, :].bitcast(F32), ALU.subtract), m_lo_s, h + 1)

            steps = {"unit": unit, "mem_scores": mem_scores, "mem_turn": mem_turn, "mem_out": mem_out, "cmp_hidden": cmp_hidden,
                     "cmp_out": cmp_out, "ml_rows": ml_rows, "ml_scores": ml_scores, "ml_out": ml_out, "ml_turn": ml_turn}
            for what, n in SCHEDULE:
                if what in steps:
                    steps[what](n)

            dve.wait_ge(mask_in_place, 16)
            gate4 = gate[:, :, :].rearrange("p q (h b) -> p q h b", b=3)
            pc3 = p_c[:, :, :, :].rearrange("p q h n -> p (q h) n")
            with dve.Fori(0, GROUPS) as g:
                chain.enter(g, 0, NSA_PER)
                dve.wait_ge(w_used, g * 2 + (U_NSA + 2))
                link(v.tensor_scalar(kc_g, kcmp[:, bass.ds(g, 1), :].rearrange("p a n -> p (a n)"), 1.0, None, ALU.mult))
                v.tensor_scalar(qT[:, 1, :], bank[1][:, :], 1.0, None, ALU.mult).then_inc(q_dve, 1)
                dve.wait_ge(c_s, g + 1)
                for half in range(2):
                    link(v.tensor_tensor(p_c[:, :, half:HPG:2, :], bank[half][:, 0:8 * NC].rearrange("p (q h n) -> p q h n", h=2, n=NC),
                                         cneg.rearrange("p (q n) -> p q n", n=NC).unsqueeze(2).to_broadcast([P, TT, 2, NC]), ALU.add))
                link(v.reduce_max(cmax, pc3, AX_X))
                v.tensor_tensor(pc3, pc3, cmax.unsqueeze(2).to_broadcast([P, 16, NC]), ALU.subtract).then_inc(c_sh, 1)
                dve.wait_ge(c_e, g + 1)
                link(v.reduce_sum(csum, pc3, AX_X))
                v.tensor_tensor(p_c[:, :, :, :], p_c[:, :, :, :],
                                c01.rearrange("p (q n) -> p q n", n=NC).unsqueeze(2).to_broadcast([P, TT, HPG, NC]),
                                ALU.mult).then_inc(c_p, 1)
                link(v.reciprocal(crec, csum))
                link(v.tensor_tensor(cg_c.rearrange("p (q h) -> p q h", h=HPG), crec.rearrange("p (q h) -> p q h", h=HPG),
                                     gate4[:, :, bass.ds(g * HPG, HPG), 0], ALU.mult))

                def mask_step(i):
                    br, qb, hh = STEPS[i]
                    n = P * (qb + 1)
                    dve.wait_ge(s_s, g * NS + (i + 1))
                    if i >= 4:
                        dve.wait_ge(s_t, g * NS + (i - 3))
                    dve.sem_inc(s_open, 1)
                    v.tensor_tensor_reduce(prob[i % 4][:, 0:n], bank[2 + i % 3][:, 0:n], strip[:, T - n:T], -(DH ** -0.5), 1e38,
                                           ALU.add, ALU.min, nmax[:, i:i + 1]).then_inc(s_m, 1)

                def turn_step(i):
                    if i % 2 == 1:
                        br, qb, hh = STEPS[i]
                        n = P * (qb + 1)
                        dve.wait_ge(s_t, g * NS + (i + 1))
                        v.tensor_copy(probT[i % 4][:, 0:n], bank[5 + i % 2][:, 0:n]).then_inc(s_pd, 1)

                def out_step(k):
                    br, qb, _ = STEPS[HPG * k]
                    dve.wait_ge(s_o, g * NS + (HPG * k + HPG))
                    link(v.reciprocal(prec[:, HPG * k:HPG * (k + 1)], psum_row[:, HPG * k:HPG * (k + 1)]))
                    link(v.tensor_tensor(cg[:, HPG * k:HPG * (k + 1)], prec[:, HPG * k:HPG * (k + 1)],
                                         gate4[:, qb, bass.ds(g * HPG, HPG), br + 1], ALU.mult))
                    for hh in range(HPG):
                        y = y_tok[:, qb, DH * hh:DH * (hh + 1)]
                        o_ = bank[OUT_BANK[k % 2]][:, DH * hh:DH * (hh + 1)]
                        c = cg[:, HPG * k + hh:HPG * k + hh + 1]
                        if br == 0:
                            ins = v.tensor_scalar(y, o_, c, None, ALU.mult)
                        else:
                            ins = v.scalar_tensor_tensor(y, o_, c, y, ALU.mult, ALU.add)
                    ins.then_inc(s_or, 1)

                for i in range(NS + 5):
                    if i < NS:
                        mask_step(i)
                    if 2 <= i < NS + 2:
                        turn_step(i - 2)
                    if i >= 8 and i % HPG == 0:
                        out_step(i // HPG - 2)
                dve.wait_ge(s_or, g * (NS // HPG) + NS // HPG)
                dve.wait_ge(c_o, g + 1)
                for qb in range(TT):
                    for hh in range(HPG):
                        y = y_tok[:, qb, DH * hh:DH * (hh + 1)]
                        o_ = bank[0 if qb < 2 else 5][:, 256 * (qb % 2) + DH * hh:256 * (qb % 2) + DH * (hh + 1)]
                        ins = v.scalar_tensor_tensor(y, o_, cg_c[:, HPG * qb + hh:HPG * qb + hh + 1], y, ALU.mult, ALU.add)
                ins.then_inc(y_done, 1)
                for t in range(2):
                    dve.wait_ge(y_turned, g * 2 + (t + 1))
                    yh = ynsa[0][:, bass.ds(g * 2 + t, 1), :].rearrange("p a n -> p (a n)")
                    yl = ynsa[1][:, bass.ds(g * 2 + t, 1), :].rearrange("p a n -> p (a n)")
                    link(v.tensor_scalar(yh, bank[6 + t][:, :], 1.0, None, ALU.mult))
                    v.tensor_tensor(yl, bank[6 + t][:, :], yh.bitcast(F32), ALU.subtract).then_inc(y_split, 1)
            chain.leave(GROUPS)

            def merge(c):
                for b in range(3):
                    n3 = c * 3 + b
                    dve.wait_ge(w_used, n3 * 2 + (U_MERGE + 2))
                    for t in range(2):
                        dve.wait_ge(mg_gate, n3 * 2 + (t + 1))
                        if b == 0:
                            v.tensor_tensor(ma[t][:, :], mg[t][:, :], bank[2 + t][:, :], ALU.mult).then_inc(mg_used, 1)
                        else:
                            link(v.tensor_tensor(mb[t][:, :], mg[t][:, :], bank[2 + t][:, :], ALU.mult))
                            v.tensor_tensor(ma[t][:, :], ma[t][:, :], mb[t][:, :], ALU.add).then_inc(mg_used, 1)
                dve.wait_ge(mg_used, c * 6 + 6)
                for t in range(2):
                    yh = ym[0][:, bass.ds(c * 2 + t, 1), :].rearrange("p a n -> p (a n)")
                    yl = ym[1][:, bass.ds(c * 2 + t, 1), :].rearrange("p a n -> p (a n)")
                    link(v.tensor_scalar(yh, ma[t][:, :], 1.0, None, ALU.mult))
                    mark(v.tensor_tensor(yl, ma[t][:, :], yh.bitcast(F32), ALU.subtract), mg_split, c * 2 + (t + 1))

            merge(0)
            with dve.Fori(1, 4) as c:
                chain.enter(c, 1, 6)
                merge(c)
            chain.leave(3)

            def square(src, k):
                if k >= 2:
                    dve.wait_ge(sq_added, 9 * ((k - 2) // 8) + (k - 2) % 8 + 2)
                v.tensor_tensor(sq[k % 2][:, :], src, src, ALU.mult).then_inc(sq_ready, 1)

            def split(src, gain, j, s, n):
                link(v.tensor_scalar(h_hi[:, j, :], src, gain, None, ALU.mult))
                mark(v.scalar_tensor_tensor(h_lo[:, j, :], src, gain, h_hi[:, j, :].bitcast(F32), ALU.mult, ALU.subtract), s, n)

            def reciprocal_root(n):
                dve.wait_ge(root, n)
                mark(v.reciprocal(rb[:, :], rb[:, :]), rstd, n)

            def post_norm(name, x_first, r, sq_first, gain_row, event):
                reciprocal_root(r)
                for j in range(KT):
                    link(v.scalar_tensor_tensor(O[:, j, :], O[:, j, :], col(name, j), rb[:, :], ALU.mult, ALU.mult))
                    if x_first:
                        dve.wait_ge(x_turned, j + 1)
                        b = (5, 6, 7, 0, 1, 2, 3)[j % 7]
                        mark(v.tensor_tensor(X[:, j, :], O[:, j, :], bank[b][:, :], ALU.add), x_new, j + 1)
                    else:
                        mark(v.tensor_tensor(X[:, j, :], O[:, j, :], X[:, j, :], ALU.add), x_new, KT + j + 1)
                    square(X[:, j, :], sq_first + j)
                    split(X[:, j, :], gain_row(j), j, h_ready, KT * event + j + 1)

            for n in range(4):
                dve.wait_ge(w_used, U_WOUT + n + 1)
                for t in range(2):
                    j = 2 * n + t
                    mark(v.tensor_copy(O[:, j, :], bank[2 * (n % 2) + t][:, :]), o_ready, j + 1)
                    square(O[:, j, :], j)
            post_norm("g_post_mix", True, 1, 8, lambda j: col("g_pre_ffn", j), 0)

            for f in range(5):
                def up(i):
                    u = i * 2 + U_FFN[f]
                    n = i * 2 + 2 * UP_STEPS * f
                    dve.wait_ge(w_used, u + 1)
                    for t in range(2):
                        v.tensor_tensor(tg[t][:, :], bank[t][:, :], rb[:, :], ALU.mult).then_inc(g_scaled, 1)
                    for t in range(2):
                        dve.wait_ge(silu_done, n + (t + 1))
                        link(v.tensor_tensor(tg[t][:, :], tg[t][:, :], rb[:, :], ALU.mult))
                    dve.wait_ge(w_used, u + 2)
                    for t in range(2):
                        mark(v.tensor_tensor(tg[t][:, :], tg[t][:, :], bank[2 + t][:, :], ALU.mult), up_read, n + (t + 1))
                        hh = hid[0][:, bass.ds(i * 2 + t, 1), :].rearrange("p a n -> p (a n)")
                        hl = hid[1][:, bass.ds(i * 2 + t, 1), :].rearrange("p a n -> p (a n)")
                        link(v.tensor_scalar(hh, tg[t][:, :], 1.0, None, ALU.mult))
                        mark(v.tensor_tensor(hl, tg[t][:, :], hh.bitcast(F32), ALU.subtract), hid_ready, n + (t + 1))

                reciprocal_root(R_EVENT[f])
                up(0)
                with dve.Fori(1, UP_STEPS) as i:
                    chain.enter(i, 1, 4)
                    up(i)
                chain.leave(UP_STEPS - 1)
                kind, gain = NEXT[f]
                for c in range(4):
                    dve.wait_ge(w_used, U_FFN[f] + 2 * UP_STEPS + 3 * c + 3)
                    for t in range(2):
                        j = 2 * c + t
                        src = bank[4 + 2 * (c % 2) + t][:, :]
                        n = 8 + 8 * f + j + 1
                        if kind == "post":
                            mark(v.tensor_copy(O[:, j, :], src), o_ready, n)
                            square(O[:, j, :], SQ_BASE[f] + j)
                        else:
                            mark(v.scalar_tensor_tensor(X[:, j, :], src, 0.5, X[:, j, :], ALU.mult, ALU.add), o_ready, n)
                            if kind == "half":
                                square(X[:, j, :], SQ_BASE[f] + j)
                            if gain is not None:
                                split(X[:, j, :], col(gain[0], j, gain[1]), j, h_ready, KT * H_EVENT[f + 1] + j + 1)
                if f == 0:
                    post_norm("g_post_ffn", False, 3, 24, lambda j: col("norm_g_2", j, 0), 1)
                if f == 1:
                    link(v.memset(hp[:, :, 0:POOL_PAD], 0.0))
                    link(v.memset(hp[:, :, POOL_PAD + T:W_HP], 0.0))
                    reciprocal_root(5)
                    dve.wait_ge(inv_landed, 16)
                    for j in range(KT):
                        gi = j // 2
                        mid = hp[:, j, POOL_PAD:POOL_PAD + T]
                        link(v.scalar_tensor_tensor(mid, X[:, j, :], col("norm_g_2", j, 1), rb[:, :], ALU.mult, ALU.mult))
                        cur = hp[:, j, :]
                        for m in range(gi + 1):
                            n = W_HP - ((2 << m) - 1)
                            dst = pool_s[m % 2][:, :]
                            link(v.tensor_tensor(dst[:, 0:n], cur[:, 0:n], cur[:, (1 << m):(1 << m) + n], ALU.add))
                            cur = dst
                        c0 = POOL_PAD - (1 << gi)
                        tmp = tg[j % 2][:, :]
                        link(v.tensor_tensor(tmp, cur[:, c0:c0 + T], inv[:, gi, :], ALU.mult))
                        link(v.tensor_tensor(tmp, tmp, mid, ALU.subtract))
                        link(v.tensor_scalar(h_hi[:, j, :], tmp, 1.0, None, ALU.mult))
                        mark(v.tensor_tensor(h_lo[:, j, :], tmp, h_hi[:, j, :].bitcast(F32), ALU.subtract), pooled, j + 1)
                    for n in range(2):
                        dve.wait_ge(w_used, U_POOL + n + 1)
                        if n == 0:
                            dve.wait_ge(w_used, U_POOL + 2)
                        for q in range(4):
                            j = 4 * n + q
                            tmp = tg[j % 2][:, :]
                            link(v.tensor_scalar(tmp, bank[4 - 4 * n + q][:, :], col("pool_b_2", j), col("pool_scale_2", j),
                                                 ALU.add, ALU.mult))
                            mark(v.tensor_tensor(X[:, j, :], tmp, X[:, j, :], ALU.add), x_new, 16 + j + 1)
                            square(X[:, j, :], 40 + j)
                            split(X[:, j, :], col("norm_g_2", j, 2), j, h_ready, KT * 2 + j + 1)
                if f == 3:
                    link(v.memset(hc[:, :, 0:PAD], 0.0))
                    link(v.memset(hc[:, :, PAD + T:W_HC], 0.0))
                    reciprocal_root(8)
                    for j in range(KT):
                        tmp = tg[j % 2][:, :]
                        link(v.scalar_tensor_tensor(tmp, X[:, j, :], col("norm_g_2", j, 4), rb[:, :], ALU.mult, ALU.mult))
                        link(v.tensor_scalar(h_hi[:, j, :], tmp, 1.0, None, ALU.mult))
                        mark(v.tensor_tensor(h_lo[:, j, :], tmp, h_hi[:, j, :].bitcast(F32), ALU.subtract), h_ready, KT * 4 + j + 1)
                    for n in range(4):
                        dve.wait_ge(w_used, U_PW1 + 2 * n + 2)
                        for t in range(2):
                            j = 2 * n + t
                            dve.wait_ge(glu_arg, j + 1)
                            mark(v.scalar_tensor_tensor(hc[:, j, PAD:PAD + T], bank[2 + t][:, :], col("conv_b_pw1_2", j, 0),
                                                        tg[t][:, :], ALU.add, ALU.mult), glu, j + 1)
                        for k in range(TAPS):
                            for t in range(2):
                                j = 2 * n + t
                                w = col("conv_w_dw_2", j, k)
                                src = hc[:, j, k:k + T]
                                if k == 0:
                                    ins = v.tensor_scalar(cacc[t][:, :], src, w, col("conv_b_dw_2", j), ALU.mult, ALU.add)
                                else:
                                    dst = cacc[t][:, :] if k < TAPS - 1 else hy[:, j, :]
                                    ins = v.scalar_tensor_tensor(dst, src, w, cacc[t][:, :], ALU.mult, ALU.add)
                                if k < TAPS - 1:
                                    chain.step(ins)
                                    dve.wait_ge(chain.sem, chain.n - 1)
                                else:
                                    ins.then_inc(conv_y, 1)
                                    dve.wait_ge(chain.sem, chain.n)
                        dve.wait_ge(conv_y, 2 * n + 2)
                    dve.wait_ge(mean_s, 1)
                    link(v.tensor_scalar(mu[:, :], bank[4][:, :], 1.0 / D, None, ALU.mult))
                    for j in range(KT):
                        mark(v.tensor_tensor(hy[:, j, :], hy[:, j, :], mu[:, :], ALU.subtract), ln_x, j + 1)
                        if j >= 2:
                            dve.wait_ge(ln_used, j - 1)
                        v.tensor_tensor(sq[j % 2][:, :], hy[:, j, :], hy[:, j, :], ALU.mult).then_inc(ln_sq, 1)
                    reciprocal_root(9)
                    for j in range(KT):
                        v.scalar_tensor_tensor(hy[:, j, :], hy[:, j, :], col("conv_ln_g_2", j), rb[:, :], ALU.mult,
                                               ALU.mult).then_inc(ln_z, 1)
                    for j in range(KT):
                        dve.wait_ge(ln_act, j + 1)
                        link(v.tensor_scalar(h_hi[:, j, :], hy[:, j, :], 1.0, None, ALU.mult))
                        mark(v.tensor_tensor(h_lo[:, j, :], hy[:, j, :], h_hi[:, j, :].bitcast(F32), ALU.subtract), ln_h, j + 1)
                    for n in range(4):
                        dve.wait_ge(w_used, U_PW2 + n + 1)
                        for t in range(2):
                            j = 2 * n + t
                            mark(v.scalar_tensor_tensor(X[:, j, :], bank[4 + 2 * (n % 2) + t][:, :], col("conv_b_pw2_2", j),
                                                        X[:, j, :], ALU.add, ALU.add), x_new, 24 + j + 1)
                            square(X[:, j, :], 64 + j)
                    for j in range(KT):
                        split(X[:, j, :], col("norm_g_2", j, 5), j, h_ready, KT * 5 + j + 1)

            dve.wait_ge(fin_sq, 1)
            pairs = stat[:, 32:40].rearrange("p (t b) -> p t b", b=2)
            v.tensor_tensor(stat[:, 40:44], pairs[:, :, 0], pairs[:, :, 1], ALU.add).then_inc(fin_sum, 1)
            dve.wait_ge(fin_root, 1)
            link(v.reciprocal(stat[:, 44:48], stat[:, 44:48]))
            dve.wait_ge(fg_landed, 16)
            for t in range(TT):
                for b in range(2):
                    ins = v.scalar_tensor_tensor(o_tok[:, t, T * b:T * (b + 1)], bank[2 * t + b][:, :], stat[:, 44 + t:45 + t],
                                                 fg[:, T * b:T * (b + 1)], ALU.mult, ALU.mult)
                    if b == 0:
                        link(ins)
                ins.then_inc(fin_y, 1)


_SKIP = ("x", "mem")


def kernel(**inputs):
    import concourse.bacc as _bacc
    from concourse.bass_utils import run_bass_kernel_spmd as _run

    nc = _bacc.Bacc("TRN2", target_bir_lowering=False, num_devices=1)
    arrays, aps = {}, {}
    table, inv_count = constants()
    for name, value in list(inputs.items()) + [("const_table", table), ("const_inv_count", inv_count)]:
        a = np.ascontiguousarray(value)
        arrays[f"in_{name}_dram"] = a
        aps[name] = nc.dram_tensor(f"in_{name}_dram", a.shape, mybir.dt.from_np(a.dtype), kind="ExternalInput").ap()
    out = nc.dram_tensor("out_0_dram", (1, T, D), F32, kind="ExternalOutput").ap()
    build(nc, aps, aps["const_table"], aps["const_inv_count"], out)
    r = _run(nc, [arrays], core_ids=[0])
    return r.results[0]["out_0_dram"]
```

```python
from contextlib import ExitStack

import numpy as np

import concourse.bass as bass
from concourse import mybir

F32 = mybir.dt.float32
F32R = mybir.dt.float32r
ALU = mybir.AluOpType
ACT = mybir.ActivationFunctionType
AX_X = mybir.AxisListType.X

P = 128
T = 512
D = 1024
KT = D // P
TT = T // P
MEM = 256
MT = MEM // P
UC = 256
UNIT = KT * UC
FF = 2816
HT = FF // P
UP_STEPS = FF // UC
DOWN_K = (8, 8, 6)
GROUPS, HPG, DH = 4, 4, 64
NC = (T - 32) // 16 + 1
EPS = 1e-6
LN_EPS = 1e-5
TAPS = 31
PAD = TAPS // 2
POOL_PAD = 8
NEG = -1e30

C_KV, C_GATE, C_QK, C_V, C_IF, C_O, C_QMEM, C_MERGE = 1024, 2560, 2608, 3632, 4144, 4152, 4664, 5176

ROWS = [("g_pre_mix", 1), ("g_post_mix", 1), ("g_pre_ffn", 1), ("g_post_ffn", 1), ("g_mem", 1),
        ("norm_g_2", 6), ("pool_b_2", 1), ("pool_scale_2", 1), ("conv_b_pw1_2", 2), ("conv_b_dw_2", 1),
        ("conv_ln_g_2", 1), ("conv_ln_b_2", 1), ("conv_b_pw2_2", 1), ("ml_conv_w", 4), ("ml_conv_b", 1),
        ("conv_w_dw_2", TAPS)]
ROW, NROWS = {}, 0
for _name, _count in ROWS:
    ROW[_name] = NROWS
    NROWS += _count

UNITS = [("mem", 0, UC, "mem_k"), ("mem", 256, UC, "mem_k"), ("mem", 512, UC, "mem_v"), ("mem", 768, UC, "mem_v"),
         ("in", C_QMEM, UC, "q_mem"), ("in", C_QMEM + UC, UC, "q_mem"),
         ("in", C_KV, UC, "kc"), ("in", C_KV + 256, UC, "vc"), ("in", C_KV + 512, UC, "ks"), ("in", C_KV + 1024, UC, "kw"),
         ("in", C_KV + 768, UC, "vs"), ("in", C_KV + 1280, UC, "vw"), ("gates", 0, P, "gate"), ("gates", P, P, "if"),
         ("in", C_QK, UC, "qk"), ("in", C_QK + 256, UC, "qk"), ("in", C_QK + 512, UC, "qk"), ("in", C_QK + 768, UC, "qk"),
         ("in", C_V, UC, "v"), ("in", C_V + UC, UC, "v"), ("in", C_O, UC, "o"), ("in", C_O + UC, UC, "o")]
NFIX = len(UNITS)
FEATURE_MAJOR = ("mem_k", "q_mem", "kc", "vc", "ks", "kw", "qk")
ACT_ONLY = ("mem_v", "gate", "if", "o")
DVE_EVACS = [0]
for _u in UNITS:
    DVE_EVACS.append(DVE_EVACS[-1] + (_u[3] not in ACT_ONLY))

SCHEDULE = [("unit", u) for u in range(6)]
for _h in range(4):
    SCHEDULE += [("mem_scores", _h), ("unit", 6 + 2 * _h), ("mem_turn", _h), ("unit", 7 + 2 * _h), ("mem_out", _h)]
    if _h in (1, 2):
        SCHEDULE += [("cmp_place", _h - 1)]
SCHEDULE += [("gate_turn", 0), ("cmp_hidden", 0), ("cmp_out", 0), ("unit", 14), ("cmp_hidden", 1), ("cmp_out", 1),
             ("ml_const", 0), ("ml_rows", 0), ("unit", 15), ("unit", 16), ("unit", 17), ("ml_cols", 0), ("unit", 18),
             ("ml_scores", 0), ("ml_out", 0), ("unit", 19), ("ml_scores", 1), ("ml_out", 1),
             ("unit", 20), ("ml_gain", 0), ("ml_norm", 0), ("unit", 21), ("ml_scores", 2), ("ml_out", 2), ("ml_scores", 3),
             ("ml_gain", 1), ("ml_out", 3), ("ml_norm", 1), ("ml_turn", 0)]

U_NSA = NFIX
U_MERGE = U_NSA + 4 * GROUPS
U_WOUT = U_MERGE + 2 * 4
PER_FFN = 2 * UP_STEPS + 12
U_FFN = [0] * 5
U_FFN[0] = U_WOUT + 4
U_FFN[1] = U_FFN[0] + PER_FFN
U_POOL = U_FFN[1] + PER_FFN
U_FFN[2] = U_POOL + 2
U_FFN[3] = U_FFN[2] + PER_FFN
U_PW1 = U_FFN[3] + PER_FFN
U_PW2 = U_PW1 + 8
U_FFN[4] = U_PW2 + 4
N_UNITS = U_FFN[4] + PER_FFN

STEPS = [(br, qb, hh) for br in range(2) for qb in range(TT) for hh in range(HPG)]
NS = len(STEPS)
S_BANK = (2, 3)
OUT_BANK = (7, 1)
CMP_BANK = (2, 3, 5, 6)
CMP_OUT_BANK = (3, 5)

GATE_BANK = (4, 0)
GATE_TILES = 6
GATE_PRE, GATE_STEP = 8, 3
GATE_EVAC = {8: 0, 16: 1, 24: 2, 32: 3}

TURN_ORDER = (4, 5, 6, 0, 1, 2, 3, 7)
TURN_BANK = (0, 1, 2, 3, 5, 6, 7, 4)

PE_TAPS = (7, 8, 8, 12)
HI_POST_MIX, HI_POST_FFN, HI_POOLED, HI_POOL_OUT, HI_CONV_IN, HI_LN, HI_CONV_OUT = (8 * _i for _i in range(7))

K_ID, K_ONE, K_STRIP, K_TRI, K_CNEG, K_C01, K_SEL = 0, 128, 256, 768, 896, 1020, 1144
K_END = 1656


NSA_PER = 25


class Chain:

    def __init__(self, sem):
        self.sem, self.n, self.made = sem, 0, 0

    def link(self, eng, ins):
        self.step(ins)
        eng.wait_ge(self.sem, self.n)

    def step(self, ins):
        ins.then_inc(self.sem, 1)
        self.n = self.n + 1
        self.made += 1

    def enter(self, i, first, per):
        self.base, self.per, self.made = self.n, per, 0
        self.n = (i - first) * per + self.base

    def leave(self, turns):
        assert self.made == self.per, (self.made, self.per)
        self.n = self.base + turns * self.per


def constants():
    c = np.zeros((P, K_END), np.float32)
    p = np.arange(P)
    c[:, K_ID:K_ID + P] = np.eye(P)
    c[:, K_ONE:K_ONE + P] = 1
    c[:, K_STRIP + 384:K_STRIP + 512] = np.where(p[None, :] <= p[:, None], 0, NEG)
    c[:, K_TRI:K_TRI + P] = p[:, None] <= p[None, :]
    for qb in range(TT):
        seen = (16 * np.arange(NC) + 31)[None, :] <= (p + P * qb)[:, None]
        c[:, K_CNEG + NC * qb:K_CNEG + NC * (qb + 1)] = np.where(seen, 0, NEG)
        c[:, K_C01 + NC * qb:K_C01 + NC * (qb + 1)] = seen
    for h in range(4):
        c[h, K_SEL + P * h:K_SEL + P * (h + 1)] = 1
    t = np.arange(T)
    inv = np.zeros((4, T), np.float32)
    for g in range(4):
        w = 2 << g
        count = np.clip(t - w // 2 + w, 0, T) - np.clip(t - w // 2, 0, T)
        inv[g] = np.float32(1) / count.astype(np.float32)
    return c, inv


def layout(inputs):
    arrays = dict(inputs)
    w_in = np.asarray(arrays["w_in"])[0]
    gates = np.zeros((D, 2 * P), w_in.dtype)
    gates[:, 0:48] = w_in[:, C_GATE:C_GATE + 48]
    for i in range(2):
        gates[:, P + 32 * i:P + 32 * i + 4] = w_in[:, C_IF + 4 * i:C_IF + 4 * i + 4]
    arrays["w_gates"] = gates
    arrays["vector_rows"] = np.concatenate([np.asarray(arrays[name]).reshape(-1, D) for name, _ in ROWS])
    arrays["cmp_pe_rows"] = np.stack([np.concatenate([np.asarray(arrays[name])[0, 16 * half:16 * half + 16] for half in range(2)], 1)
                                      for name in ("cmp_pe_k", "cmp_pe_v")], 1)
    arrays["w_proj_ml_mem"] = np.concatenate([np.asarray(arrays.pop("w_proj_ml"))[0], np.asarray(arrays.pop("w_proj_mem"))[0]])
    return arrays


def build(nc, A, const_in, invcount_in, out):
    with ExitStack() as ctx:
        def sem(name):
            return ctx.enter_context(nc.semaphore(name))

        base = (nc.sbuf_base + 63) // 64 * 64
        limit = nc.sbuf_usable_end

        def at(name, shape, off, dt=F32):
            n = 4
            for s in shape[1:]:
                n *= s
            assert off + n <= limit, (name, off, n, limit)
            return nc.alloc_sbuf_tensor_at(name, shape, dt, offset=off)

        KB = 1024
        cid = at("identity_ones", [P, 256], base)
        vec = at("vectors", [P, 512], base + 1 * KB)
        stat = at("stat", [P, 128], base + 3 * KB)
        H0 = base + 3 * KB + 512
        h_hi = at("h_hi", [P, KT, T], H0, F32R)
        h_lo = at("h_lo", [P, KT, T], H0 + 16 * KB, F32R)
        W0 = H0 + 32 * KB
        raw = [at(f"w_raw{s}", [P, UNIT], W0 + 8 * KB * s) for s in range(2)]
        w_hi = [at(f"w_hi{s}", [P, UNIT], W0 + 8 * KB * (2 + s), F32R) for s in range(2)]
        w_lo = [at(f"w_lo{s}", [P, UNIT], W0 + 8 * KB * (4 + s), F32R) for s in range(2)]
        AR = W0 + 48 * KB

        ident = cid[:, 0:P]
        ones = cid[:, P:2 * P]

        def col(name, j, r=0):
            k = j * NROWS + ROW[name] + r
            return vec[:, k:k + 1]

        pe_cols = [vec[:, 448:464], vec[:, 464:480]]
        eps = stat[:, 0:1]
        ln_eps = stat[:, 1:2]
        ss = stat[:, 8:16]
        rs_tok = stat[:, 16:24]

        ymem = [at("ymem_hi", [P, 4, T], AR + 32 * KB, F32R), at("ymem_lo", [P, 4, T], AR + 40 * KB, F32R)]
        yml = [at("yml_hi", [P, 4, T], AR + 48 * KB, F32R), at("yml_lo", [P, 4, T], AR + 56 * KB, F32R)]
        ynsa = [at("ynsa_hi", [P, 8, T], AR, F32R), at("ynsa_lo", [P, 8, T], AR + 16 * KB, F32R)]
        PE0 = AR + 64 * KB
        v_sw = [at("v_sel", [P, TT, UC], PE0), at("v_win", [P, TT, UC], PE0 + 4 * KB)]
        gate = at("nsa_gate", [P, TT, 48], PE0 + 8 * KB)
        kcmp = at("k_cmp", [P, GROUPS, NC], PE0 + 8 * KB + 768)
        vcmp = at("v_cmp", [P, GROUPS, DH], PE0 + 9 * KB + 512)
        cms = at("const_masks", [P, 1144 - 256], PE0 + 10 * KB + 512)
        WK = PE0 + 14 * KB + 32
        strip = cms[:, 0:512]
        tri = cms[:, 512:640]
        cneg = cms[:, 640:640 + TT * NC]
        c01 = cms[:, 764:764 + TT * NC]

        x_tok = at("x_tok", [P, TT, D], AR)
        mem_tok = at("mem_tok", [P, MT, D], AR + 16 * KB)
        rows = at("vector_rows", [P, D], AR + 24 * KB)
        pe_rows = at("pe_rows", [16, 2, P], AR + 28 * KB)
        junk = at("junk", [P, D], AR + 30 * KB)
        m_hi = at("m_hi", [P, KT, MEM], WK, F32R)
        m_lo = at("m_lo", [P, KT, MEM], WK + 8 * KB, F32R)
        KM = WK + 17 * KB
        k_mem = at("k_mem", [P, 4, MEM], KM)
        v_mem = at("v_mem", [P, MT, T], KM + 4 * KB)
        q_mem = at("q_mem", [P, 4, T], KM + 8 * KB)
        p_mem = at("p_mem", [P, TT, MEM], AR + 48 * KB)
        pt_mem = at("pt_mem", [P, MT, T], AR + 52 * KB)
        kv_c = [at("k_c", [P, GROUPS, T], AR), at("v_c", [P, GROUPS, T], AR + 8 * KB)]
        cmp_w1 = [at("cmp_w1_k", [P, 16, P], AR + 16 * KB), at("cmp_w1_v", [P, 16, P], AR + 24 * KB)]
        gate_T = at("nsa_gate_turned", [48, T], AR + 56 * KB)
        hid_c = at("cmp_hidden", [P, GROUPS, NC], WK + 45 * KB)
        w2k = at("cmp_w2k", [P, 2, DH], WK + 45 * KB + 512)
        w2v = at("cmp_w2v", [P, DH], WK + 46 * KB)
        k_stage = [at("k_sel_stage", [P, 2, T], WK + 33 * KB), at("k_win_stage", [P, 2, T], WK + 37 * KB)]
        qk_in = at("qk_in", [P, 8, T + 3], WK)
        v_ml = at("v_ml", [P, TT, 4, P + 1], WK + 16 * KB + 128)
        o_ml = at("o_ml", [P, TT, T], WK + 25 * KB)
        if_row = [at(f"if_row{i}", [4, T], WK + (41 + 2 * i) * KB) for i in range(2)]
        conv_acc = [at(f"conv_acc{i}", [P, T], AR + (58 + 2 * i) * KB) for i in range(2)]
        d_ml = [at(f"decay{i}", [P, T], WK + (41 + 2 * i) * KB - 512) for i in range(2)]
        head_g = at("head_g", [P, T], AR + 56 * KB)
        s_ml = at("s_ml", [P, TT, T], AR)
        h_mlt = at("h_ml", [P, TT, T], AR + 8 * KB)
        row4 = [at(f"gate_row{i}", [4, T], AR + (16 + 2 * i) * KB) for i in range(6)]
        sel4 = at("head_selector", [4, 4, P], AR + 28 * KB)
        gate_b = at("gate_bias", [36, 2], AR + 62 * KB)
        ones4 = at("ones_row", [4, T], AR + 30 * KB)
        g_col = stat[:, 32:48]
        emt = stat[:, 48:64]
        den = stat[:, 64:68]
        den2 = stat[:, 68:72]
        ss_ml = stat[:, 72:88]
        rr_ml = stat[:, 88:104]
        junk2 = at("ml_junk", [P, P], WK + 45 * KB)
        qT = at("q_group", [P, 2, T], WK)
        k_dup = [at("k_sel_group", [P, T], WK + 4 * KB), at("k_win_group", [P, T], WK + 6 * KB)]
        y_tok = at("y_tok", [P, TT, HPG * DH], WK + 8 * KB)
        prob = [at(f"prob{i}", [P, T], WK + (12 + 2 * i) * KB) for i in range(4)]
        probT = [at(f"probT{i}", [P, T], WK + (20 + 2 * i) * KB) for i in range(4)]
        p_c = at("p_cmp", [P, TT, HPG, NC], WK + 28 * KB)
        pT_c = at("pT_cmp", [NC, TT * HPG, P], WK + 30 * KB)
        y_br = at("y_branch", [P, HPG, DH], WK + 38 * KB)
        nst = at("nsa_stat", [P, 256], WK + 39 * KB)
        cmax = nst[:, 0:16]
        csum = nst[:, 16:32]
        crec = nst[:, 32:48]
        cg_c = nst[:, 48:64]
        nmax = nst[:, 64:96]
        psum_row = nst[:, 96:128]
        kc_g = nst[:, 192:192 + NC]
        prec = nst[:, 128:160]
        cg = nst[:, 160:192]
        gt_stage = [at(f"gate_stage{i}", [P, T], WK + (40 + 2 * i) * KB) for i in range(2)]
        ym = [at("merged_hi", [P, 8, T], WK, F32R), at("merged_lo", [P, 8, T], WK + 16 * KB, F32R)]
        mg = [at(f"merge_gate{b}", [P, 2, T], PE0 + 4 * KB * b) for b in range(3)]
        ma = [at(f"merge_acc{t}", [P, T], WK + (36 + 2 * t) * KB) for t in range(2)]
        X = at("x", [P, KT, T], AR)
        x_tok2 = at("x_tok_again", [P, TT, D], AR + 16 * KB)
        O = at("o", [P, KT, T], H0)
        hid = [at("hid_hi", [P, HT, T], AR + 16 * KB, F32R), at("hid_lo", [P, HT, T], AR + 60 * KB, F32R)]
        TL = AR + 104 * KB
        rb = at("rstd", [P, T], TL)
        tg = [at(f"gate_tmp{t}", [P, T], TL + (2 + 2 * t) * KB) for t in range(2)]
        sq = [at(f"square{t}", [P, T], TL + (6 + 2 * t) * KB + 64) for t in range(2)]
        ssq = at("sum_squares", [P, T], TL + 10 * KB + 64)
        W_HP = T + 2 * POOL_PAD
        hp = at("pool_h", [P, KT, W_HP], AR + 16 * KB)
        pool_s = [at(f"pool_sum{i}", [P, W_HP], AR + 33 * KB + 2176 * i) for i in range(2)]
        pool_w = [at(f"pool_window{i}", [P, W_HP], AR + 33 * KB + 2176 * (2 + i)) for i in range(2)]
        inv = at("inv_count", [P, 4, T], AR + 44 * KB)
        W_HC = T + 2 * PAD
        hc = at("conv_h", [P, KT, W_HC], AR + 16 * KB)
        hy = at("conv_y", [P, KT, T], AR + 34 * KB)
        cacc = [at(f"conv_sum{i}", [P, T], AR + (50 + 2 * i) * KB) for i in range(2)]
        mu = at("mean", [P, T], AR + 62 * KB)
        diag_w = at("tap_diagonals", [P, 2 * sum(PE_TAPS), P], AR + 64 * KB)
        fg = at("final_gain", [P, D], AR + 16 * KB)
        junk3 = at("final_junk", [P, T], AR + 36 * KB)
        o_tok = at("out_tok", [P, TT, D], AR + 20 * KB)

        bank = [ctx.enter_context(nc.psum_tensor(f"bank{i}", [P, T], F32)) for i in range(8)]
        k_scratch = nc.dram_tensor("k_scratch", [2, 2 * P, T], F32, kind="Internal").ap()

        g_scratch = nc.dram_tensor("gate_scratch", [GATE_TILES * GROUPS, P, T], F32, kind="Internal").ap()

        const_in_place = sem("const_in_place")
        mask_in_place = sem("mask_in_place")
        mem_in_place = sem("mem_in_place")
        x_in_place = sem("x_in_place")
        rows_in_place = sem("rows_in_place")
        w_landed = [sem("w_landed0"), sem("w_landed1")]
        w_hi_ready = sem("w_hi_ready")
        w_lo_ready = sem("w_lo_ready")
        w_used = sem("w_used")
        act_chain_s = sem("act_chain")
        dve_chain_s = sem("dve_chain")
        pool_chain_s = sem("pool_chain")
        pe_done = sem("pe_done")
        stat_set = sem("stat_set")
        tok_root = sem("tok_root")
        tok_scaled = sem("tok_scaled")
        vec_turned = sem("vec_turned")
        vec_ready = sem("vec_ready")
        tok_turned = sem("tok_turned")
        start_hi = sem("start_hi")
        start_lo = sem("start_lo")
        evac_act = sem("evac_act")
        evac_dve = sem("evac_dve")
        mem_s = sem("mem_scores_ready")
        mem_m = sem("mem_max_ready")
        mem_e = sem("mem_exp_done")
        mem_p = sem("mem_prob_ready")
        mem_t = sem("mem_prob_turned")
        mem_ta = sem("mem_probT_act")
        mem_td = sem("mem_probT_dve")
        mem_o = sem("mem_out_ready")
        mem_yh = sem("mem_y_hi")
        mem_y = sem("mem_y_ready")
        w1_landed = sem("w1_landed")
        w2_landed = sem("w2_landed")
        cmp_ab = sem("cmp_ab_ready")
        cmp_h = sem("cmp_hidden_summed")
        cmp_hs = sem("cmp_hidden_ready")
        cmp_o = sem("cmp_out_ready")
        cmp_e = sem("cmp_kv_ready")
        k_stored = sem("k_stored")
        ml_const = sem("ml_const")
        gate_turned = sem("gate_turned")
        gate_ready = sem("gate_ready")
        f_min = sem("f_min")
        f_log = sem("f_log")
        g_rows = sem("g_rows")
        g_turned = sem("g_turned")
        g_cols = sem("g_cols")
        emt_ready = sem("emt_ready")
        conv_done = sem("ml_conv_done")
        qk_ready = sem("qk_ready")
        bc_ready = sem("ml_bcast_ready")
        sT_ready = sem("ml_scores_ready")
        d_arg = sem("decay_arg")
        d_exp = sem("decay_exp")
        s_used = sem("ml_scores_used")
        s_masked = sem("ml_scores_masked")
        mo_ready = sem("ml_out_ready")
        m_rec = sem("ml_den_ready")
        m_h = sem("ml_h_ready")
        m_root = sem("ml_root_ready")
        m_y = sem("ml_y_ready")
        m_turned = sem("ml_y_turned")
        m_hi_s = sem("ml_y_hi")
        m_lo_s = sem("ml_y_lo")
        kd_landed = sem("k_group_landed")
        q_act = sem("q_tile0_ready")
        q_dve = sem("q_tile1_ready")
        c_s = sem("c_scores_ready")
        c_sh = sem("c_shifted")
        c_e = sem("c_exp_done")
        c_p = sem("c_prob_ready")
        c_t = sem("c_prob_turned")
        c_ta = sem("c_probT_ready")
        c_o = sem("c_out_ready")
        s_s = sem("scores_ready")
        s_m = sem("scores_masked")
        s_open = sem("scores_open")
        s_e = sem("prob_ready")
        s_t = sem("prob_turned")
        s_pa = sem("probT_act")
        s_pd = sem("probT_dve")
        s_o = sem("attn_out_ready")
        s_or = sem("attn_out_read")
        y_done = sem("y_group_done")
        y_turned = sem("y_group_turned")
        y_split = sem("y_group_split")
        gt_half = sem("gate_unit_half_made")
        gt_copied = sem("gate_tile_copied")
        gt_stored = [sem("gate_tile_stored0"), sem("gate_tile_stored1")]
        mg_landed = sem("merge_gates_landed")
        mg_gate = sem("merge_gate_ready")
        mg_used = sem("merge_gate_used")
        mg_split = sem("merged_ready")
        x_again = sem("x_tok_again_landed")
        x_turned = sem("x_turned")
        o_ready = sem("tile_evacuated")
        sq_ready = sem("square_ready")
        sq_added = sem("square_added")
        sumsq = sem("sum_squares_ready")
        root = sem("root_ready")
        rstd = sem("rstd_ready")
        x_new = sem("x_updated")
        ln_used = sem("ln_square_used")
        h_ready = sem("h_ready")
        g_scaled = sem("gate_scaled")
        silu_done = sem("silu_done")
        up_read = sem("up_read")
        hid_ready = sem("hidden_ready")
        inv_landed = sem("inv_count_landed")
        pooled = sem("pooled_ready")
        glu_arg = sem("glu_sigmoid_ready")
        glu = sem("glu_ready")
        h_hi_s = sem("h_high_ready")
        pool_win = sem("pool_window_summed")
        pool_mean = sem("pool_window_mean")
        pool_diff = sem("pool_difference")
        conv_in = sem("conv_input_ready")
        diag_s = sem("tap_diagonals_ready")
        taps_made = sem("pe_taps_made")
        conv_y = sem("conv_y_ready")
        mean_s = sem("mean_sum_ready")
        ln_x = sem("ln_centred")
        ln_sq = sem("ln_square_ready")
        ln_z = sem("ln_affine_ready")
        ln_act = sem("ln_silu_done")
        ln_h = sem("ln_h_ready")
        fin_turned = sem("final_turned")
        fin_sq = sem("final_squares")
        fin_sum = sem("final_sum")
        fin_root = sem("final_root")
        fin_y = sem("final_ready")
        fg_landed = sem("final_gain_landed")
        stored = sem("out_stored")

        w_in = A["w_in"][0]
        w_mem = A["w_mem_kv"][0]
        tiles_of = lambda w: w.rearrange("(k p) c -> p k c", p=P)
        w_in_t = tiles_of(w_in)
        src_fixed = {"mem": tiles_of(w_mem), "in": w_in_t, "gates": tiles_of(A["w_gates"])}
        proj_t = [tiles_of(A["w_proj_nsa"][0]), tiles_of(A["w_proj_ml_mem"])]
        wout_t = tiles_of(A["w_out"][0])
        ffn_in = [tiles_of(A["w_ffn_in"][0])] + [tiles_of(A["ffn_w_in_2"][i, j]) for i in range(2) for j in range(2)]
        ffn_dn = [tiles_of(A["w_ffn_down"][0])] + [tiles_of(A["ffn_w_out_2"][i, j]) for i in range(2) for j in range(2)]
        pool_t = A["pool_w_2"][0].rearrange("g (k p) c -> p (g k) c", p=P)
        pw1_t = tiles_of(A["conv_w_pw1_2"][0])
        pw2_t = tiles_of(A["conv_w_pw2_2"][0])
        x_rows = A["x"][0].rearrange("(t p) d -> p t d", p=P)

        NEXT = [("post", ("norm_g_2", 0)), ("half", None), ("half", ("norm_g_2", 3)), ("half", None), ("last", None)]
        H_EVENT = [0, 1, 2, 3, 5]
        R_EVENT = [2, 4, 6, 7, 10]
        X_BASE = [8, 16, 32, 40, 56]
        O_BASE = [8, 16, 24, 32, 40]
        SQ_BASE = [16, 32, 48, 56, None]

        block = ctx.enter_context(nc.Block())

        @block.sync
        def _(sp):
            def load(u2, s, src, k, n):
                if not isinstance(u2, int) or u2 > 0:
                    sp.wait_ge(w_landed[s], 16)
                    sp.wait_ge(w_lo_ready, u2 * 2 + (s - 1))
                sp.dma_start(raw[s][:, 0:k * n].rearrange("p (k c) -> p k c", c=n), src).then_inc(w_landed[s], 16)

            sp.dma_start(cid[:, :], const_in[:, 0:256]).then_inc(const_in_place, 16)
            for m in range(MT):
                sp.dma_start(mem_tok[:, m, :], A["mem"][0][m * P:(m + 1) * P, :]).then_inc(mem_in_place, 16)
            for t in range(TT):
                sp.dma_start(x_tok[:, t, :], x_rows[:, t, :]).then_inc(x_in_place, 16)
            for u, (w, c, n, kind) in enumerate(UNITS):
                load(u // 2, u % 2, src_fixed[w][:, :, c:c + n], KT, n)
                if u == 4:
                    sp.wait_ge(tok_turned, 16)
                    for b, name in enumerate(("cmp_w1_k", "cmp_w1_v")):
                        for half in range(2):
                            sp.dma_start(cmp_w1[b][DH * half:DH * (half + 1), :, :],
                                         A[name][0][16 * half:16 * half + 16].rearrange("l d h -> d l h")).then_inc(w1_landed, 16)
                if u == 12:
                    sp.wait_ge(evac_act, 10)
                    sp.wait_ge(evac_dve, DVE_EVACS[10])
                    for b in range(2):
                        sp.dma_start(k_scratch[b].rearrange("(t p) n -> p t n", p=P), k_stage[b][:, :, :]).then_inc(k_stored, 16)
            sp.wait_ge(k_stored, 32)
            with sp.Fori(0, GROUPS) as g:
                def gate_load(b):
                    load(g * 2 + (U_NSA // 2 + (b + 1) // 2), (b + 1) % 2, w_in_t[:, :, bass.ds(g * UC + (C_MERGE + b * D), UC)], KT, UC)

                load(g * 2 + U_NSA // 2, 0, w_in_t[:, :, bass.ds(g * UC, UC)], KT, UC)
                gate_load(0)
                gate_load(1)
                sp.wait_ge(k_stored, 32)
                sp.wait_ge(w_used, g * 4 + (U_NSA + 1))
                for b in range(2):
                    for half in range(2):
                        sp.dma_start(k_dup[b][DH * half:DH * (half + 1), :],
                                     k_scratch[b, bass.ds(g * DH, DH), :]).then_inc(kd_landed, 16)
                gate_load(2)

            def merge_loads(c):
                for s in range(2):
                    load(c + U_MERGE // 2, s, proj_t[s][:, :, bass.ds(c * UC, UC)], KT, UC)
                for s in range(2):
                    sp.wait_ge(gt_stored[s], 16 + 16 * GATE_TILES * GROUPS // 2)
                if isinstance(c, int):
                    sp.wait_ge(y_done, GROUPS)
                else:
                    sp.wait_ge(mg_used, c * 6)
                for b in range(3):
                    sp.dma_start(mg[b][:, :, :], g_scratch[bass.ds(c * GATE_TILES + 2 * b, 2), :, :].rearrange("t p n -> p t n")
                                 ).then_inc(mg_landed, 16)

            merge_loads(0)
            with sp.Fori(1, 4) as c:
                merge_loads(c)
            for n in range(4):
                load((U_WOUT + n) // 2, n % 2, wout_t[:, :, n * UC:(n + 1) * UC], KT, UC)
                if n == 1:
                    sp.wait_ge(w_used, U_WOUT)
                    sp.dma_start(x_tok2[:, :, :], x_rows).then_inc(x_again, 16)
            for f in range(5):
                with sp.Fori(0, UP_STEPS) as i:
                    load(i + U_FFN[f] // 2, 0, ffn_in[f][:, :, bass.ds(i * UC, UC)], KT, UC)
                    load(i + U_FFN[f] // 2, 1, ffn_in[f][:, :, bass.ds(i * UC + FF, UC)], KT, UC)
                u = U_FFN[f] + 2 * UP_STEPS
                for c in range(4):
                    k0 = 0
                    for k in DOWN_K:
                        load(u // 2, u % 2, ffn_dn[f][:, k0:k0 + k, c * UC:(c + 1) * UC], k, UC)
                        k0 += k
                        u += 1
                if f == 1:
                    for n in range(2):
                        load((U_POOL + n) // 2, n, pool_t[:, 4 * n:4 * n + 4, :], 4, UC)
                    sp.wait_ge(w_used, U_POOL)
                    sp.dma_start(inv[:, :, :], invcount_in.rearrange("(o g) t -> o g t", o=1).to_broadcast([P, 4, T])
                                 ).then_inc(inv_landed, 16)
                if f == 3:
                    for n in range(4):
                        load(U_PW1 // 2 + n, 0, pw1_t[:, :, D + n * UC:D + (n + 1) * UC], KT, UC)
                        load(U_PW1 // 2 + n, 1, pw1_t[:, :, n * UC:(n + 1) * UC], KT, UC)
                    for n in range(4):
                        load((U_PW2 + n) // 2, n % 2, pw2_t[:, :, n * UC:(n + 1) * UC], KT, UC)
            sp.wait_ge(w_used, N_UNITS)
            sp.dma_start(fg[:, :], A["final_g_2"].rearrange("(o d) -> o d", o=1).to_broadcast([P, D])).then_inc(fg_landed, 16)
            for t in range(TT):
                sp.wait_ge(fin_y, t + 1)
                sp.dma_start(out[0].rearrange("(t p) d -> p t d", p=P)[:, t, :], o_tok[:, t, :]).then_inc(stored, 16)
            sp.wait_ge(stored, 16 * TT)

        @block.scalar
        def _(act):
            chain = Chain(act_chain_s)

            def high(u2, s):
                act.wait_ge(w_landed[s], u2 * 16 + 16)
                if not isinstance(u2, int) or u2 > 0:
                    act.wait_ge(w_used, u2 * 2 + (s - 1))
                nc.scalar.activation(w_hi[s][:, :], raw[s][:, :], ACT.Copy).then_inc(w_hi_ready, 1)

            def high_next(u):
                if u + 1 < N_UNITS:
                    high((u + 1) // 2, (u + 1) % 2)

            def root_of_sum(n):
                act.wait_ge(sumsq, n)
                nc.scalar.activation(rb[:, :], bank[4][:, :], ACT.Sqrt, bias=eps, scale=1.0 / D).then_inc(root, 1)

            def square(src, k):
                if k >= 2:
                    act.wait_ge(sq_added, 9 * ((k - 2) // 8) + (k - 2) % 8 + 2)
                nc.scalar.activation(sq[k % 2][:, :], src, ACT.Square).then_inc(sq_ready, 1)

            def hi_part(src, j, gain=1.0):
                nc.scalar.activation(h_hi[:, j, :], src, ACT.Copy, scale=gain).then_inc(h_hi_s, 1)

            def post_norm(x_base, sq_first, gain_row):
                for j in range(KT):
                    act.wait_ge(x_new, x_base + j + 1)
                    hi_part(X[:, j, :], j, gain_row(j))
                    square(X[:, j, :], sq_first + j)

            act.dma_start(rows[0:NROWS, :], A["vector_rows"]).then_inc(rows_in_place, 16)
            act.dma_start(pe_rows[:, :, :], A["cmp_pe_rows"]).then_inc(rows_in_place, 16)
            act.wait_ge(stat_set, 1)
            act.wait_ge(mem_in_place, 16 * MT)
            for t in range(6):
                if t == MT:
                    nc.scalar.activation(rs_tok[:, 0:MT], ss[:, 0:MT], ACT.Sqrt, bias=eps, scale=1.0 / D).then_inc(tok_root, 1)
                    act.wait_ge(x_in_place, 16 * TT)
                src = mem_tok[:, t, :] if t < MT else x_tok[:, t - MT, :]
                chain.link(act, nc.scalar.activation(junk[:, :], src, ACT.Square, accum_out=ss[:, t:t + 1]))
            nc.scalar.activation(rs_tok[:, MT:6], ss[:, MT:6], ACT.Sqrt, bias=eps, scale=1.0 / D).then_inc(tok_root, 1)
            high(0, 0)
            act.wait_ge(vec_ready, 1)
            for n in range(16):
                if n == 8:
                    high(0, 1)
                act.wait_ge(tok_turned, n + 1)
                if n < 8:
                    nc.scalar.activation(m_hi[:, n, :], bank[n][:, 0:MEM], ACT.Copy, scale=col("g_mem", n)).then_inc(start_hi, 1)
                else:
                    j = n - 8
                    nc.scalar.activation(h_hi[:, j, :], bank[j][:, :], ACT.Copy, scale=col("g_pre_mix", j)).then_inc(start_hi, 1)

            def load_small():
                act.dma_start(cms[:, :], const_in[:, K_STRIP:K_SEL]).then_inc(mask_in_place, 16)
                for half in range(2):
                    act.dma_start(w2k[:, half, :], A["cmp_w2_k"][0]).then_inc(w2_landed, 16)
                act.dma_start(w2v[:, :], A["cmp_w2_v"][0]).then_inc(w2_landed, 16)
                for half in range(2):
                    act.dma_start(gate_b[32 * half:32 * half + 4, half:half + 1],
                                  A["ml_gate_b"][0][4 * half:4 * half + 4].rearrange("(a b) -> a b", b=1)).then_inc(ml_const, 16)

            def evacuate(u):
                w, c, n, kind = UNITS[u]
                b0, b1 = bank[2 * (u % 2)], bank[2 * (u % 2) + 1]
                act.wait_ge(w_used, u + 1)
                v0 = b0[:, :].rearrange("p (t c) -> p t c", c=UC)
                v1 = b1[:, :].rearrange("p (t c) -> p t c", c=UC)
                cp = ACT.Copy
                if kind == "mem_k":
                    ins = nc.scalar.activation(k_mem[:, 2 * u, :], b0[:, 0:MEM], cp)
                elif kind == "mem_v":
                    ins = nc.scalar.activation(v_mem[:, :, c - 512:c - 512 + UC], v0, cp)
                elif kind == "q_mem":
                    ins = nc.scalar.activation(q_mem[:, 2 * (u - 4), :], b0[:, :], cp)
                elif kind in ("kc", "vc"):
                    for g in range(2):
                        rows_ = b0[DH * g:DH * (g + 1), :]
                        nc.scalar.activation(kv_c[u - 6][0:DH, g, :], rows_, cp)
                        ins = nc.scalar.activation(kv_c[u - 6][DH:P, g, 0:T - 16], rows_[:, 16:T], cp)
                elif kind in ("ks", "kw"):
                    ins = nc.scalar.activation(k_stage[u - 8][:, 0, :], b0[:, :], cp)
                elif kind in ("vs", "vw"):
                    ins = nc.scalar.activation(v_sw[u - 10][:, 0:2, :], v0, cp)
                elif kind == "gate":
                    ins = nc.scalar.activation(gate_T[:, :], b0[0:48, :], ACT.Sigmoid)
                elif kind == "if":
                    act.wait_ge(ml_const, 32)
                    for i in range(2):
                        ins = nc.scalar.activation(if_row[i][:, :], b0[32 * i:32 * i + 4, :], ACT.Identity,
                                                   bias=gate_b[32 * i:32 * i + 4, i:i + 1])
                elif kind == "qk":
                    ins = nc.scalar.activation(qk_in[:, 2 * (u - 14), 3:3 + T], b0[:, :], cp)
                elif kind == "v":
                    h0 = 2 * (u - 18)
                    for t in range(2):
                        ins = nc.scalar.activation(v_ml[:, t, h0:h0 + 2, 0:P], v0[:, t, :].rearrange("p (h d) -> p h d", d=P), cp)
                else:
                    c0 = UC * (u - 20)
                    nc.scalar.activation(o_ml[:, 0:2, c0:c0 + UC], v0, ACT.Sigmoid)
                    ins = nc.scalar.activation(o_ml[:, 2:4, c0:c0 + UC], v1, ACT.Sigmoid)
                ins.then_inc(evac_act, 1)
                if kind == "qk":
                    for j in range(2 * (u - 14), 2 * (u - 14) + 2):
                        act.wait_ge(conv_done, j + 1)
                        nc.scalar.activation(qk_in[:, j, 3:3 + T], conv_acc[j % 2][:, :], ACT.Silu).then_inc(qk_ready, 1)

            def mem_scores(h):
                act.wait_ge(mem_m, h + 1)
                for qb in range(TT):
                    src = bank[4 + qb // 2][:, 256 * (qb % 2):256 * (qb % 2) + 256]
                    ins = nc.scalar.activation(p_mem[:, qb, :], src, ACT.Exp, bias=stat[:, 32 + qb:33 + qb], scale=P ** -0.5,
                                               accum_out=stat[:, 36 + qb:37 + qb])
                ins.then_inc(mem_e, 1)

            def mem_turn(h):
                act.wait_ge(mem_t, h + 1)
                nc.scalar.activation(pt_mem[:, 0, :], bank[6][:, :], ACT.Copy).then_inc(mem_ta, 1)

            def mem_out(h):
                act.wait_ge(mem_o, h + 1)
                nc.scalar.activation(ymem[0][:, h, :], bank[4][:, :], ACT.Copy).then_inc(mem_yh, 1)

            def cmp_hidden(b):
                act.wait_ge(cmp_h, b + 1)
                nc.scalar.activation(hid_c[:, :, :], bank[5][:, 0:4 * NC].rearrange("p (g n) -> p g n", n=NC), ACT.Silu).then_inc(cmp_hs, 1)

            def gate_turn(_):
                act.wait_ge(gate_turned, 1)
                nc.scalar.activation(gate[:, :, :], bank[6][:, 0:48 * TT].rearrange("p (t c) -> p t c", c=48), ACT.Copy).then_inc(gate_ready, 1)

            def load_ml_const(_):
                act.dma_start(sel4[:, :, :], const_in[0:4, K_SEL:K_END].rearrange("p (h c) -> p h c", c=P)).then_inc(ml_const, 16)
                act.dma_start(head_g[:, :], A["ml_head_g"].to_broadcast([P, T])).then_inc(ml_const, 16)

            def ml_rows(_):
                act.wait_ge(f_min, 1)
                chain.link(act, nc.scalar.activation(row4[2][:, :], row4[2][:, :], ACT.Exp))
                nc.scalar.activation(row4[2][:, :], row4[2][:, :], ACT.Ln, bias=1.0).then_inc(f_log, 1)

            def ml_cols(_):
                act.wait_ge(g_turned, 1)
                nc.scalar.activation(emt, bank[7][:, 16:32], ACT.Exp, scale=-1.0).then_inc(emt_ready, 1)

            def ml_scores(h):
                for sb in range(TT):
                    n = TT * h + sb
                    act.wait_ge(d_arg, n + 1)
                    d = d_ml[n % 2][:, 0:T - P * sb]
                    nc.scalar.activation(d, d, ACT.Exp).then_inc(d_exp, 1)

            def ml_out(h):
                act.wait_ge(m_rec, h + 1)
                for tb in range(TT):
                    src = bank[7 if tb < 2 else 4][:, (P + 1) * (tb % 2):(P + 1) * (tb % 2) + P]
                    chain.link(act, nc.scalar.activation(h_mlt[:, tb, P * h:P * (h + 1)], src, ACT.Copy, scale=den[:, tb:tb + 1]))
                for tb in range(TT):
                    ins = nc.scalar.activation(junk2[:, :], h_mlt[:, tb, P * h:P * (h + 1)], ACT.Square,
                                               accum_out=ss_ml[:, 4 * tb + h:4 * tb + h + 1])
                    chain.link(act, ins)
                act.sem_inc(m_h, 1)

            def ml_norm(half):
                heads = slice(2 * half, 2 * half + 2)
                nc.scalar.activation(rr_ml.rearrange("p (t h) -> p t h", h=4)[:, :, heads],
                                     ss_ml.rearrange("p (t h) -> p t h", h=4)[:, :, heads],
                                     ACT.Sqrt, bias=eps, scale=1.0 / P).then_inc(m_root, 1)

            def ml_turn(_):
                for h in range(4):
                    act.wait_ge(m_turned, h + 1)
                    nc.scalar.activation(yml[0][:, h, :], bank[h][:, :], ACT.Copy).then_inc(m_hi_s, 1)

            steps = {"mem_scores": mem_scores, "mem_turn": mem_turn, "mem_out": mem_out, "cmp_hidden": cmp_hidden,
                     "gate_turn": gate_turn,
                     "ml_norm": ml_norm, "ml_const": load_ml_const, "ml_rows": ml_rows, "ml_cols": ml_cols, "ml_scores": ml_scores, "ml_out": ml_out,
                     "ml_turn": ml_turn}
            for what, n in SCHEDULE:
                if what == "unit":
                    if n == 0:
                        load_small()
                    else:
                        high_next(n)
                    evacuate(n)
                elif what in steps:
                    steps[what](n)

            act.sem_inc(gt_copied, 2)
            for s in range(2):
                act.sem_inc(gt_stored[s], 16)
            with act.Fori(0, GROUPS) as g:
                high(g * 2 + U_NSA // 2, 1)
                act.wait_ge(w_used, g * 4 + (U_NSA + 1))
                nc.scalar.activation(qT[:, 0, :], bank[0][:, :], ACT.Copy).then_inc(q_act, 1)
                act.wait_ge(c_sh, g + 1)
                nc.scalar.activation(p_c[:, :, :, :], p_c[:, :, :, :], ACT.Exp, scale=DH ** -0.5).then_inc(c_e, 1)

                def exp_step(i):
                    br, qb, hh = STEPS[i]
                    n = P * (qb + 1)
                    act.wait_ge(s_m, g * NS + (i + 1))
                    nc.scalar.activation(prob[i % 4][:, 0:n], prob[i % 4][:, 0:n], ACT.Exp, bias=nmax[:, i:i + 1], scale=-1.0,
                                         accum_out=psum_row[:, i:i + 1]).then_inc(s_e, 1)

                def turn_step(i):
                    if i % 2 == 0:
                        br, qb, hh = STEPS[i]
                        n = P * (qb + 1)
                        act.wait_ge(s_t, g * NS + (i + 1))
                        nc.scalar.activation(probT[i % 4][:, 0:n], bank[5 + i % 2][:, 0:n], ACT.Copy).then_inc(s_pa, 1)

                def gate_evac(m):
                    if m % 2 == 0:
                        act.wait_ge(gt_half, g * 3 + (m // 2 + 1))
                    else:
                        act.wait_ge(w_used, g * 4 + (U_NSA + m // 2 + 2))
                    act.wait_ge(gt_stored[m % 2], g * 48 + 16 * (m // 2 + 1))
                    nc.scalar.activation(gt_stage[m % 2][:, :], bank[GATE_BANK[m % 2]][:, :], ACT.Copy).then_inc(gt_copied, 1)
                    act.wait_ge(gt_copied, g * GATE_TILES + (m + 3))
                    act.dma_start(g_scratch[bass.ds(g * GATE_TILES + m, 1), :, :].rearrange("a p n -> p (a n)"),
                                  gt_stage[m % 2][:, :]).then_inc(gt_stored[m % 2], 16)

                for i in range(NS + 2):
                    if i < NS:
                        exp_step(i)
                    if i >= 2:
                        turn_step(i - 2)
                    if i == 2:
                        high(g * 2 + (U_NSA // 2 + 1), 0)
                    if i in GATE_EVAC:
                        gate_evac(GATE_EVAC[i])
                        if GATE_EVAC[i] == 1:
                            high(g * 2 + (U_NSA // 2 + 1), 1)
                        if GATE_EVAC[i] == 3:
                            high(g * 2 + (U_NSA // 2 + 2), 0)
                act.wait_ge(c_t, g + 1)
                for qb in range(TT):
                    ins = nc.scalar.activation(pT_c[:, HPG * qb:HPG * (qb + 1), :],
                                               bank[CMP_BANK[qb]][0:NC, :].rearrange("p (h q) -> p h q", q=P), ACT.Copy)
                ins.then_inc(c_ta, 1)
                gate_evac(4)
                gate_evac(5)

            def merge(c):
                high(c + U_MERGE // 2, 1)
                act.wait_ge(mg_landed, c * 48 + 48)
                for b in range(3):
                    nc.scalar.activation(mg[b][:, :, :], mg[b][:, :, :], ACT.Sigmoid).then_inc(mg_gate, 1)
                high(c + (U_MERGE // 2 + 1), 0)

            merge(0)
            with act.Fori(1, 4) as c:
                merge(c)
            for n in range(4):
                high_next(U_WOUT + n)
            root_of_sum(1)
            high(U_FFN[0] // 2, 1)
            post_norm(0, 8, lambda j: col("g_pre_ffn", j))

            for f in range(5):
                def up(i, first=False):
                    u2 = i + U_FFN[f] // 2
                    n = i * 2 + 2 * UP_STEPS * f
                    if not first or f == 3:
                        high(u2, 1)
                    if first:
                        root_of_sum(R_EVENT[f] if f < 4 else 9)
                    for t in range(2):
                        act.wait_ge(g_scaled, n + (t + 1))
                        nc.scalar.activation(tg[t][:, :], tg[t][:, :], ACT.Silu).then_inc(silu_done, 1)
                    high(u2 + 1, 0)

                up(0, True)
                with act.Fori(1, UP_STEPS) as i:
                    up(i)
                for n in range(12):
                    high_next(U_FFN[f] + 2 * UP_STEPS + n)
                if f == 0:
                    root_of_sum(3)
                    high(U_FFN[1] // 2, 1)
                    post_norm(KT, 24, lambda j: col("norm_g_2", j, 0))
                if f == 1:
                    root_of_sum(5)
                    high_next(U_POOL)
                    for j in range(KT):
                        act.wait_ge(pool_diff, j + 1)
                        hi_part(tg[j % 2][:, :], j)
                    high_next(U_POOL + 1)
                    for j in range(4):
                        act.wait_ge(x_new, 16 + j + 1)
                        square(X[:, j, :], 40 + j)
                    act.wait_ge(w_used, U_POOL + 2)
                    for j in range(KT):
                        if j < 4:
                            hi_part(X[:, j, :], j, col("norm_g_2", j, 2))
                            act.wait_ge(x_new, 20 + j + 1)
                            square(X[:, 4 + j, :], 44 + j)
                        else:
                            hi_part(X[:, j, :], j, col("norm_g_2", j, 2))
                    high(U_FFN[2] // 2, 1)
                if f == 3:
                    root_of_sum(8)
                    for j in range(KT):
                        act.wait_ge(conv_in, j + 1)
                        hi_part(tg[j % 2][:, :], j)
                    made = 0
                    for n in range(4):
                        u = U_PW1 + 2 * n
                        high_next(u)
                        for t in range(2):
                            act.wait_ge(w_used, u + 1)
                            if n > 0:
                                act.wait_ge(glu, 2 * n)
                            nc.scalar.activation(tg[t][:, :], bank[t][:, :], ACT.Sigmoid,
                                                 bias=col("conv_b_pw1_2", 2 * n + t, 1)).then_inc(glu_arg, 1)
                        high_next(u + 1)
                        for t in range(2):
                            for k in range(TAPS - PE_TAPS[n], TAPS):
                                ins = nc.scalar.activation(diag_w[:, made, :], ident, ACT.Copy, scale=col("conv_w_dw_2", 2 * n + t, k))
                                made += 1
                        ins.then_inc(diag_s, 1)
                    for j in range(KT):
                        act.wait_ge(ln_x, j + 1)
                        if j >= 2:
                            act.wait_ge(ln_used, j - 1)
                        nc.scalar.activation(sq[j % 2][:, :], hy[:, j, :], ACT.Square).then_inc(ln_sq, 1)
                    act.wait_ge(ln_used, KT)
                    nc.scalar.activation(rb[:, :], bank[1][:, :], ACT.Sqrt, bias=ln_eps, scale=1.0 / D).then_inc(root, 1)
                    for j in range(KT):
                        act.wait_ge(ln_z, j + 1)
                        nc.scalar.activation(hy[:, j, :], hy[:, j, :], ACT.Silu, bias=col("conv_ln_b_2", j)).then_inc(ln_act, 1)
                        act.wait_ge(ln_act, j + 1)
                        hi_part(hy[:, j, :], j)
                    for n in range(4):
                        high_next(U_PW2 + n)
                        for t in range(2):
                            j = 2 * n + t
                            act.wait_ge(x_new, 24 + j + 1)
                            square(X[:, j, :], 64 + j)
                    act.wait_ge(w_used, U_PW2 + 4)
                    for j in range(KT):
                        hi_part(X[:, j, :], j, col("norm_g_2", j, 5))
                    high(U_FFN[4] // 2, 1)

            act.wait_ge(fin_turned, 1)
            for t in range(TT):
                for b in range(2):
                    chain.link(act, nc.scalar.activation(junk3[:, :], bank[2 * t + b][:, :], ACT.Square,
                                                         accum_out=stat[:, 32 + 2 * t + b:33 + 2 * t + b]))
            act.sem_inc(fin_sq, 1)
            act.wait_ge(fin_sum, 1)
            nc.scalar.activation(stat[:, 44:48], stat[:, 40:44], ACT.Sqrt, bias=eps, scale=1.0 / D).then_inc(fin_root, 1)

        @block.gpsimd
        def _(pool):
            def low_part(u, s):
                pool.wait_ge(w_hi_ready, u + 1)
                nc.gpsimd.tensor_tensor(w_lo[s][:, :], raw[s][:, :], w_hi[s][:, :].bitcast(F32), ALU.subtract).then_inc(w_lo_ready, 1)

            def low_next(u):
                if u + 1 < N_UNITS:
                    low_part(u + 1, (u + 1) % 2)

            def clear():
                nc.gpsimd.memset(ssq[:, :], 0.0).then_inc(sq_added, 1)
                tally[0] += 1
                pool.wait_ge(sq_added, tally[0])

            def add_square(k):
                pool.wait_ge(sq_ready, k + 1)
                nc.gpsimd.tensor_tensor(ssq[:, :], ssq[:, :], sq[k % 2][:, :], ALU.add).then_inc(sq_added, 1)
                tally[0] += 1
                pool.wait_ge(sq_added, tally[0])

            def clear_after(n):
                pool.wait_ge(sumsq, n)
                clear()

            tally = [0]
            low_part(0, 0)
            for u in range(NFIX):
                low_next(u)
            with pool.Fori(0, GROUPS) as g:
                for n in range(4):
                    low_part(g * 4 + (U_NSA + 1 + n), (n + 1) % 2)
            with pool.Fori(0, 4) as i:
                low_part(i * 2 + (U_MERGE + 1), 1)
                low_part(i * 2 + (U_MERGE + 2), 0)
            pool.wait_ge(mg_split, 8)
            clear()
            for n in range(4):
                low_next(U_WOUT + n)
                for t in range(2):
                    add_square(2 * n + t)
            clear_after(1)
            for j in range(KT):
                add_square(8 + j)
            for f in range(5):
                low_part(U_FFN[f] + 1, 1)
                clear_after(R_EVENT[f] if f < 4 else 9)
                low_part(U_FFN[f] + 2, 0)
                with pool.Fori(1, UP_STEPS) as i:
                    low_part(i * 2 + (U_FFN[f] + 1), 1)
                    low_part(i * 2 + (U_FFN[f] + 2), 0)
                for c in range(4):
                    for n in range(3):
                        low_next(U_FFN[f] + 2 * UP_STEPS + 3 * c + n)
                    if f < 4:
                        for t in range(2):
                            add_square(SQ_BASE[f] + 2 * c + t)
                if f == 0:
                    clear_after(3)
                    for j in range(KT):
                        add_square(24 + j)
                if f == 1:
                    clear_after(5)
                    low_next(U_POOL)
                    pool.wait_ge(inv_landed, 16)
                    for j in range(KT):
                        c0 = POOL_PAD - (1 << (j // 2))
                        pool.wait_ge(pool_win, j + 1)
                        if j >= 2:
                            pool.wait_ge(pooled, j - 1)
                        nc.gpsimd.tensor_tensor(tg[j % 2][:, :], pool_w[j % 2][:, c0:c0 + T], inv[:, j // 2, :], ALU.mult
                                                ).then_inc(pool_mean, 1)
                    low_next(U_POOL + 1)
                    for j in range(KT):
                        add_square(40 + j)
                if f == 3:
                    clear_after(8)
                    for n in range(8):
                        low_next(U_PW1 + n)
                    for n in range(4):
                        low_next(U_PW2 + n)
                        for t in range(2):
                            add_square(64 + 2 * n + t)

        @block.tensor
        def _(pe):
            def products(s, kt, cols, x, banks, n=T, k0=0, k_all=None, ready=None, w0=0, used=True):
                k_all = kt if k_all is None else k_all
                for k in range(kt):
                    if ready is not None:
                        ready(k)
                    for t, b in enumerate(banks):
                        c = (w0 + k) * cols + t * P
                        wh, wl = w_hi[s][:, c:c + P], w_lo[s][:, c:c + P]
                        xh, xl = x[0][:, k0 + k, 0:n], x[1][:, k0 + k, 0:n]
                        first, last = k0 + k == 0, k0 + k == k_all - 1
                        nc.tensor.matmul(bank[b][:, 0:n], wh, xh, start=first, stop=False)
                        nc.tensor.matmul(bank[b][:, 0:n], wh, xl, start=False, stop=False)
                        ins = nc.tensor.matmul(bank[b][:, 0:n], wl, xh, start=False, stop=last)
                if used:
                    ins.then_inc(w_used, 1)

            def token_products(s, cols, x, tiles, b0):
                for t in range(tiles):
                    out_ = bank[b0 + t // 2][:, UC * (t % 2):UC * (t % 2) + cols]
                    for k in range(KT):
                        xh, xl = x[0][:, k, t * P:(t + 1) * P], x[1][:, k, t * P:(t + 1) * P]
                        wh, wl = w_hi[s][:, k * cols:(k + 1) * cols], w_lo[s][:, k * cols:(k + 1) * cols]
                        nc.tensor.matmul(out_, xh, wh, start=k == 0, stop=False)
                        nc.tensor.matmul(out_, xh, wl, start=False, stop=False)
                        ins = nc.tensor.matmul(out_, xl, wh, start=False, stop=k == KT - 1)
                ins.then_inc(w_used, 1)

            def sum_of_squares():
                nc.tensor.matmul(bank[4][:, :], ones, ssq[:, :], start=True, stop=True).then_inc(sumsq, 1)

            pe.wait_ge(const_in_place, 16)
            pe.wait_ge(rows_in_place, 32)
            for j in range(KT):
                nc.tensor.transpose(bank[7][:, j * NROWS:(j + 1) * NROWS], rows[0:NROWS, j * P:(j + 1) * P], cid[0:NROWS, 0:NROWS])
            for b in range(2):
                ins = nc.tensor.transpose(bank[7][:, 448 + 16 * b:464 + 16 * b], pe_rows[:, b, :], cid[0:16, 0:16])
            ins.then_inc(vec_turned, 1)
            for n in range(16):
                if n == 7:
                    pe.wait_ge(vec_ready, 1)
                if n >= 8:
                    pe.wait_ge(start_lo, n - 7)
                pe.wait_ge(tok_scaled, MT if n < 8 else 6)
                j = n % 8
                for t in range(MT if n < 8 else TT):
                    src = mem_tok if n < 8 else x_tok
                    ins = nc.tensor.transpose(bank[j][:, t * P:(t + 1) * P], src[:, t, j * P:(j + 1) * P], ident)
                ins.then_inc(tok_turned, 1)

            def unit(u):
                w, c, n, kind = UNITS[u]
                s, b0 = u % 2, 2 * (u % 2)
                pe.wait_ge(w_lo_ready, u + 1)
                if u < 2:
                    pe.wait_ge(start_lo, 12)
                else:
                    pe.wait_ge(evac_act, u - 1)
                    pe.wait_ge(evac_dve, max(1, DVE_EVACS[u - 1]))
                if u == 4:
                    pe.wait_ge(start_lo, 16)
                if kind == "mem_k":
                    products(s, KT, n, (m_hi, m_lo), (b0, b0 + 1), MEM)
                elif kind == "mem_v":
                    token_products(s, n, (m_hi, m_lo), MT, b0)
                elif kind in ("gate", "if"):
                    products(s, KT, n, (h_hi, h_lo), (b0,))
                elif kind in FEATURE_MAJOR:
                    products(s, KT, n, (h_hi, h_lo), (b0, b0 + 1))
                else:
                    token_products(s, n, (h_hi, h_lo), TT, b0)

            def mem_scores(h):
                pe.wait_ge(evac_act, 6)
                pe.wait_ge(evac_dve, DVE_EVACS[6])
                if h > 0:
                    pe.wait_ge(mem_y, h)
                for qb in range(TT):
                    ins = nc.tensor.matmul(bank[4 + qb // 2][:, 256 * (qb % 2):256 * (qb % 2) + 256],
                                           q_mem[:, h, qb * P:(qb + 1) * P], k_mem[:, h, :], start=True, stop=True)
                ins.then_inc(mem_s, 1)

            def mem_turn(h):
                pe.wait_ge(mem_p, h + 1)
                for m in range(MT):
                    for qb in range(TT):
                        ins = nc.tensor.transpose(bank[6 + m][:, qb * P:(qb + 1) * P], p_mem[:, qb, m * P:(m + 1) * P], ident)
                ins.then_inc(mem_t, 1)

            def mem_out(h):
                pe.wait_ge(mem_ta, h + 1)
                pe.wait_ge(mem_td, h + 1)
                for m in range(MT):
                    ins = nc.tensor.matmul(bank[4][:, :], v_mem[:, m, h * P:(h + 1) * P], pt_mem[:, m, :], start=m == 0, stop=m == MT - 1)
                ins.then_inc(mem_o, 1)

            def cmp_hidden(b):
                pe.wait_ge(w1_landed, 64)
                pe.wait_ge(cmp_ab, b + 1)
                if b == 0:
                    pe.wait_ge(mem_y, 4)
                else:
                    pe.wait_ge(cmp_hs, 1)
                src = kv_c[b][:, :, :].rearrange("p g (n r) -> p g n r", r=16)
                for r in range(16):
                    ins = nc.tensor.matmul(bank[5][:, 0:4 * NC].rearrange("p (g n) -> p g n", n=NC), cmp_w1[b][:, r, :],
                                           src[:, :, 0:NC, r], start=r == 0, stop=r == 15)
                ins.then_inc(cmp_h, 1)

            def gate_turn(_):
                pe.wait_ge(evac_act, 13)
                pe.wait_ge(mem_ta, 4)
                for t in range(TT):
                    ins = nc.tensor.transpose(bank[6][:, 48 * t:48 * (t + 1)], gate_T[:, t * P:(t + 1) * P], cid[0:48, 0:48])
                ins.then_inc(gate_turned, 1)

            def cmp_out(b):
                pe.wait_ge(w2_landed, 48)
                pe.wait_ge(cmp_hs, b + 1)
                if b == 0:
                    pe.wait_ge(gate_ready, 1)
                    ins = nc.tensor.matmul(bank[6][:, 0:4 * NC], w2k[:, :, :].rearrange("p a d -> p (a d)"),
                                           hid_c[:, :, :].rearrange("p g n -> p (g n)"), start=True, stop=True)
                else:
                    pe.wait_ge(cmp_e, 1)
                    for g in range(GROUPS):
                        ins = nc.tensor.matmul(bank[6][0:NC, g * DH:(g + 1) * DH], hid_c[:, g, :], w2v[:, :], start=True, stop=True)
                ins.then_inc(cmp_o, 1)

            def ml_cols(_):
                pe.wait_ge(mem_td, 4)
                pe.wait_ge(g_rows, 1)
                for i, src in enumerate((row4[0], row4[2])):
                    for t in range(TT):
                        c = 16 * i + 4 * t
                        ins = nc.tensor.transpose(bank[7][:, c:c + 4], src[:, t * P:(t + 1) * P], cid[0:4, 0:4])
                ins.then_inc(g_turned, 1)

            def ml_scores(h):
                if h == 0:
                    pe.wait_ge(qk_ready, 8)
                    pe.wait_ge(cmp_e, 2)
                    pe.wait_ge(g_cols, 1)
                    pe.wait_ge(emt_ready, 1)
                    pe.wait_ge(ml_const, 64)
                else:
                    pe.wait_ge(m_h, h)
                nc.tensor.matmul(bank[4][:, :], sel4[:, h, :], row4[5][:, :], start=True, stop=True).then_inc(bc_ready, 1)
                for sb in range(TT):
                    n = TT * h + sb
                    if n >= 2:
                        pe.wait_ge(s_masked, n - 1)
                    nc.tensor.matmul(bank[5 + n % 2][:, 0:T - P * sb], qk_in[:, 4 + h, 3 + P * sb:3 + P * (sb + 1)],
                                     qk_in[:, h, 3 + P * sb:3 + T], start=True, stop=True).then_inc(sT_ready, 1)

            def ml_out(h):
                pe.wait_ge(s_masked, TT * (h + 1))
                u = 19 if h < 2 else 20
                pe.wait_ge(evac_act, u)
                pe.wait_ge(evac_dve, DVE_EVACS[u])
                for tb in range(TT):
                    for sb in range(tb + 1):
                        c = (P + 1) * (tb % 2)
                        ins = nc.tensor.matmul(bank[7 if tb < 2 else 4][:, c:c + P + 1], s_ml[:, sb, tb * P:(tb + 1) * P],
                                               v_ml[:, sb, h, :], start=sb == 0, stop=sb == tb)
                ins.then_inc(mo_ready, 1)

            def ml_turn(_):
                pe.wait_ge(evac_act, NFIX)
                for h in range(4):
                    pe.wait_ge(m_y, 8 if h < 2 else 16)
                    for t in range(TT):
                        ins = nc.tensor.transpose(bank[h][:, t * P:(t + 1) * P], h_mlt[:, t, h * P:(h + 1) * P], ident)
                    ins.then_inc(m_turned, 1)

            steps = {"unit": unit, "mem_scores": mem_scores, "mem_turn": mem_turn, "mem_out": mem_out, "cmp_hidden": cmp_hidden,
                     "cmp_out": cmp_out, "gate_turn": gate_turn, "ml_cols": ml_cols, "ml_scores": ml_scores, "ml_out": ml_out,
                     "ml_turn": ml_turn}
            for what, n in SCHEDULE:
                if what in steps:
                    steps[what](n)

            pe.wait_ge(m_lo_s, 4)
            with pe.Fori(0, GROUPS) as g:
                def gate_products(m, first, last):
                    b, t = m // 2, m % 2
                    s, out_ = (b + 1) % 2, bank[GATE_BANK[t]][:, :]
                    if first == 0:
                        pe.wait_ge(gt_copied, g * GATE_TILES + (m + 1))
                        if t == 0:
                            pe.wait_ge(w_lo_ready, g * 4 + (U_NSA + 2 + b))
                    for n in range(first, last):
                        k, part = n // 3, n % 3
                        c = k * UC + t * P
                        ins = nc.tensor.matmul(out_, (w_lo if part == 2 else w_hi)[s][:, c:c + P],
                                               (h_lo if part == 1 else h_hi)[:, k, :], start=n == 0, stop=n == 3 * KT - 1)
                    if last == 3 * KT:
                        ins.then_inc(gt_half if t == 0 else w_used, 1)

                made = [0]

                def gates(count):
                    while count > 0 and made[0] < GATE_TILES * 3 * KT:
                        m, first = made[0] // (3 * KT), made[0] % (3 * KT)
                        last = min(3 * KT, first + count)
                        gate_products(m, first, last)
                        made[0] += last - first
                        count -= last - first

                pe.wait_ge(w_lo_ready, g * 4 + (U_NSA + 1))
                pe.wait_ge(gt_copied, g * GATE_TILES + 2)
                products(0, KT, UC, (h_hi, h_lo), (0, 1))
                gates(GATE_PRE)
                pe.wait_ge(q_act, g + 1)
                pe.wait_ge(q_dve, g + 1)
                def head_rows(hh):
                    return DH * (hh % 2), DH * (hh % 2 + 1)

                for qb in range(TT):
                    for hh in range(HPG):
                        lo, hi = head_rows(hh)
                        c = NC * (2 * qb + hh // 2)
                        ins = nc.tensor.matmul(bank[hh % 2][:, c:c + NC], qT[lo:hi, hh // 2, qb * P:(qb + 1) * P], kc_g[lo:hi, :],
                                               start=True, stop=True)
                ins.then_inc(c_s, 1)
                pe.wait_ge(kd_landed, g * 64 + 64)
                pe.wait_ge(y_split, g * 2 + 2)

                def scores(i):
                    br, qb, hh = STEPS[i]
                    lo, hi = head_rows(hh)
                    n = P * (qb + 1)
                    if i >= len(S_BANK):
                        pe.wait_ge(s_m, g * NS + (i + 1 - len(S_BANK)))
                    nc.tensor.matmul(bank[S_BANK[i % len(S_BANK)]][:, 0:n], qT[lo:hi, hh // 2, qb * P:(qb + 1) * P], k_dup[br][lo:hi, 0:n],
                                     start=True, stop=True).then_inc(s_s, 1)

                def turn(i):
                    br, qb, hh = STEPS[i]
                    pe.wait_ge(s_e, g * NS + (i + 1))
                    if i >= 2:
                        pe.wait_ge(s_pa if i % 2 == 0 else s_pd, g * (NS // 2) + i // 2)
                    for kb in range(qb + 1):
                        ins = nc.tensor.transpose(bank[5 + i % 2][:, kb * P:(kb + 1) * P], prob[i % 4][:, kb * P:(kb + 1) * P], ident)
                    ins.then_inc(s_t, 1)

                def weigh(i):
                    br, qb, hh = STEPS[i]
                    pe.wait_ge(s_pa if i % 2 == 0 else s_pd, g * (NS // 2) + (i // 2 + 1))
                    if i % HPG == 0 and i >= 2 * HPG:
                        pe.wait_ge(s_or, g * (NS // HPG) + (i // HPG - 1))
                    c = DH * hh
                    for kb in range(qb + 1):
                        ins = nc.tensor.matmul(bank[OUT_BANK[i // HPG % 2]][:, c:c + DH], probT[i % 4][:, kb * P:(kb + 1) * P],
                                               v_sw[br][:, kb, bass.ds(g * DH, DH)], start=kb == 0, stop=kb == qb)
                    ins.then_inc(s_o, 1)

                for i in range(NS + 3):
                    if i < NS:
                        scores(i)
                    if 2 <= i < NS + 2:
                        turn(i - 2)
                    if i >= 3:
                        weigh(i - 3)
                    gates(GATE_STEP)
                pe.wait_ge(c_p, g + 1)
                for qb in range(TT):
                    for hh in range(HPG):
                        ins = nc.tensor.transpose(bank[CMP_BANK[qb]][0:NC, hh * P:(hh + 1) * P], p_c[:, qb, hh, :], ident)
                ins.then_inc(c_t, 1)
                gates(12)
                pe.wait_ge(c_ta, g + 1)
                for qb in range(TT):
                    for hh in range(HPG):
                        c = 256 * (qb % 2) + DH * hh
                        ins = nc.tensor.matmul(bank[CMP_OUT_BANK[qb // 2]][:, c:c + DH], pT_c[:, HPG * qb + hh, :],
                                               vcmp[0:NC, bass.ds(g, 1), :].rearrange("p a d -> p (a d)"), start=True, stop=True)
                ins.then_inc(c_o, 1)
                gates(12)
                pe.wait_ge(y_done, g + 1)
                for t in range(2):
                    for qb in range(TT):
                        ins = nc.tensor.transpose(bank[6 + t][:, qb * P:(qb + 1) * P], y_tok[:, qb, t * P:(t + 1) * P], ident)
                    ins.then_inc(y_turned, 1)
                gates(GATE_TILES * 3 * KT)

            def merge(c):
                for s in range(2):
                    pe.wait_ge(w_lo_ready, c * 2 + (U_MERGE + 1 + s))
                    if not isinstance(c, int):
                        pe.wait_ge(mg_used, c * 6 - (4 if s == 0 else 0))
                    elif s == 1:
                        pe.wait_ge(gt_copied, GATE_TILES * GROUPS + 2)
                    if s == 0:
                        if isinstance(c, int):
                            pe.wait_ge(gt_copied, GATE_TILES * GROUPS + 2)
                        products(0, KT, UC, ynsa, (0, 1))
                    else:
                        products(1, 4, UC, yml, (2, 3), k_all=4, used=False)
                        products(1, 4, UC, ymem, (4, 5), k_all=4, w0=4)

            pe.wait_ge(y_split, 2 * GROUPS + 2)
            merge(0)
            with pe.Fori(1, 4) as c:
                merge(c)
            for n in range(4):
                pe.wait_ge(w_lo_ready, U_WOUT + n + 1)
                if n == 0:
                    pe.wait_ge(mg_used, 6 * 3 + 2)
                if n == 1:
                    pe.wait_ge(mg_split, 8)
                if n >= 2:
                    pe.wait_ge(o_ready, 2 * n - 2)
                ready = (lambda k: pe.wait_ge(mg_split, k + 1)) if n == 0 else None
                products(n % 2, KT, UC, ym, (2 * (n % 2), 2 * (n % 2) + 1), ready=ready)
            pe.wait_ge(x_again, 16)
            for i, j in enumerate(TURN_ORDER):
                if j == 0:
                    pe.wait_ge(o_ready, 6)
                if j == 2:
                    pe.wait_ge(o_ready, 8)
                    pe.wait_ge(sq_added, 9)
                    sum_of_squares()
                if j == 7:
                    pe.wait_ge(root, 1)
                b = TURN_BANK[j]
                for t in range(TT):
                    ins = nc.tensor.transpose(bank[b][:, t * P:(t + 1) * P], x_tok2[:, t, j * P:(j + 1) * P], ident)
                ins.then_inc(x_turned, 1)

            SUM_AT = {event: 9 * event for event in range(2, 10)}

            for f in range(5):
                event = R_EVENT[f] if f < 4 else 9

                def up(i, first=False):
                    u = i * 2 + U_FFN[f]
                    n = i * 2 + 2 * UP_STEPS * f
                    pe.wait_ge(w_lo_ready, u + 1)
                    if not first:
                        pe.wait_ge(g_scaled, n)
                    ready = (lambda k: pe.wait_ge(h_ready, KT * H_EVENT[f] + k + 1)) if first else None
                    products(0, KT, UC, (h_hi, h_lo), (0, 1), ready=ready)
                    if first:
                        if f == 0:
                            pe.wait_ge(x_new, 8)
                        pe.wait_ge(sq_added, SUM_AT[event])
                        sum_of_squares()
                    pe.wait_ge(w_lo_ready, u + 2)
                    if not first:
                        pe.wait_ge(up_read, n)
                    products(1, KT, UC, (h_hi, h_lo), (2, 3))

                if f == 0:
                    pe.wait_ge(x_new, 2)
                if f == 2:
                    pe.wait_ge(x_new, 20)
                up(0, True)
                with pe.Fori(1, UP_STEPS) as i:
                    up(i)
                for c in range(4):
                    k0 = 0
                    for m, k in enumerate(DOWN_K):
                        u = U_FFN[f] + 2 * UP_STEPS + 3 * c + m
                        pe.wait_ge(w_lo_ready, u + 1)
                        if m == 0:
                            if c >= 2:
                                pe.wait_ge(o_ready, 8 + 8 * f + 2 * (c - 1))
                            else:
                                pe.wait_ge(rstd, R_EVENT[f])
                        ready = (lambda kk: pe.wait_ge(hid_ready, HT * f + k0 + kk + 1)) if c == 0 else None
                        products(u % 2, k, UC, hid, (4 + 2 * (c % 2), 5 + 2 * (c % 2)), k0=k0, k_all=HT, ready=ready)
                        k0 += k
                if f == 0:
                    pe.wait_ge(sq_added, SUM_AT[3])
                    sum_of_squares()
                if f == 1:
                    pe.wait_ge(sq_added, SUM_AT[5])
                    sum_of_squares()
                    pe.wait_ge(rstd, 5)
                    for n in range(2):
                        pe.wait_ge(w_lo_ready, U_POOL + n + 1)
                        if n == 0:
                            pe.wait_ge(o_ready, 24)
                        for q in range(4):
                            gi, t = q // 2, q % 2
                            pe.wait_ge(pooled, 4 * n + 2 * gi + 2)
                            for k in range(2):
                                c = (2 * gi + k) * UC + t * P
                                b = bank[4 * n + q][:, :]
                                j = 4 * n + 2 * gi + k
                                nc.tensor.matmul(b, w_hi[n][:, c:c + P], h_hi[:, j, :], start=k == 0, stop=False)
                                nc.tensor.matmul(b, w_hi[n][:, c:c + P], h_lo[:, j, :], start=False, stop=False)
                                ins = nc.tensor.matmul(b, w_lo[n][:, c:c + P], h_hi[:, j, :], start=False, stop=k == 1)
                        ins.then_inc(w_used, 1)
                if f == 3:
                    pe.wait_ge(sq_added, SUM_AT[8])
                    sum_of_squares()
                    pe.wait_ge(o_ready, 40)

                    def taps(n):
                        pe.wait_ge(diag_s, n + 1)
                        pe.wait_ge(glu, 2 * n + 2)
                        if n >= 2:
                            pe.wait_ge(conv_y, 2 * n - 2)
                        d = 2 * sum(PE_TAPS[:n])
                        for t in range(2):
                            for k in range(TAPS - PE_TAPS[n], TAPS):
                                ins = nc.tensor.matmul(bank[4 + 2 * (n % 2) + t][:, :], diag_w[:, d, :], hc[:, 2 * n + t, k:k + T],
                                                       start=k == TAPS - PE_TAPS[n], stop=k == TAPS - 1)
                                d += 1
                            ins.then_inc(taps_made, 1)

                    for n in range(4):
                        u = U_PW1 + 2 * n
                        pe.wait_ge(w_lo_ready, u + 1)
                        if n > 0:
                            pe.wait_ge(glu_arg, 2 * n)
                        ready = (lambda k: pe.wait_ge(h_ready, KT * 4 + k + 1)) if n == 0 else None
                        products(0, KT, UC, (h_hi, h_lo), (0, 1), ready=ready)
                        pe.wait_ge(w_lo_ready, u + 2)
                        if n > 0:
                            pe.wait_ge(glu, 2 * n)
                        products(1, KT, UC, (h_hi, h_lo), (2, 3))
                        if n >= 1:
                            taps(n - 1)
                    taps(3)
                    pe.wait_ge(glu, 8)
                    for j in range(KT):
                        pe.wait_ge(conv_y, j + 1)
                        ins = nc.tensor.matmul(bank[0][:, :], ones, hy[:, j, :], start=j == 0, stop=j == KT - 1)
                    ins.then_inc(mean_s, 1)
                    for j in range(KT):
                        pe.wait_ge(ln_sq, j + 1)
                        ins = nc.tensor.matmul(bank[1][:, :], ones, sq[j % 2][:, :], start=j == 0, stop=j == KT - 1)
                        ins.then_inc(ln_used, 1)
                    for n in range(4):
                        pe.wait_ge(w_lo_ready, U_PW2 + n + 1)
                        if n >= 2:
                            pe.wait_ge(x_new, 24 + 2 * (n - 1))
                        ready = (lambda k: pe.wait_ge(ln_h, k + 1)) if n == 0 else None
                        products(n % 2, KT, UC, (h_hi, h_lo), (4 + 2 * (n % 2), 5 + 2 * (n % 2)), ready=ready)
            pe.wait_ge(o_ready, 48)
            for t in range(TT):
                for j in range(KT):
                    ins = nc.tensor.transpose(bank[2 * t + j // 4][:, (j % 4) * P:(j % 4 + 1) * P], X[:, j, t * P:(t + 1) * P], ident)
            ins.then_inc(fin_turned, 1)

        @block.vector
        def _(dve):
            chain = Chain(dve_chain_s)
            v = nc.vector

            def link(ins):
                chain.link(dve, ins)

            def mark(ins, s, n):
                ins.then_inc(s, 1)
                dve.wait_ge(s, n)

            link(v.memset(stat[:, 0:1], EPS))
            v.memset(stat[:, 1:2], LN_EPS).then_inc(stat_set, 1)
            dve.wait_ge(tok_root, 1)
            link(v.reciprocal(rs_tok[:, 0:MT], rs_tok[:, 0:MT]))
            for t in range(6):
                if t == MT:
                    dve.wait_ge(vec_turned, 1)
                    link(v.tensor_copy(vec[:, 0:KT * NROWS], bank[7][:, 0:KT * NROWS]))
                    mark(v.tensor_copy(vec[:, 448:480], bank[7][:, 448:480]), vec_ready, 1)
                    dve.wait_ge(tok_root, 2)
                    link(v.reciprocal(rs_tok[:, MT:6], rs_tok[:, MT:6]))
                src = mem_tok[:, t, :] if t < MT else x_tok[:, t - MT, :]
                v.tensor_scalar(src, src, rs_tok[:, t:t + 1], None, ALU.mult).then_inc(tok_scaled, 1)
            for n in range(16):
                dve.wait_ge(start_hi, n + 1)
                j = n % 8
                if n < 8:
                    ins = v.scalar_tensor_tensor(m_lo[:, j, :], bank[j][:, 0:MEM], col("g_mem", j), m_hi[:, j, :].bitcast(F32),
                                                 ALU.mult, ALU.subtract)
                else:
                    ins = v.scalar_tensor_tensor(h_lo[:, j, :], bank[j][:, :], col("g_pre_mix", j), h_hi[:, j, :].bitcast(F32),
                                                 ALU.mult, ALU.subtract)
                ins.then_inc(start_lo, 1)

            def unit(u):
                w, c, n, kind = UNITS[u]
                if kind in ACT_ONLY:
                    return
                b1 = bank[2 * (u % 2) + 1]
                v1 = b1[:, :].rearrange("p (t c) -> p t c", c=UC)
                dve.wait_ge(w_used, u + 1)
                if u == 14:
                    link(v.memset(qk_in[:, :, 0:3], 0.0))
                if u == 18:
                    link(v.memset(v_ml[:, :, :, P:P + 1], 1.0))
                if kind == "mem_k":
                    ins = v.tensor_copy(k_mem[:, 2 * u + 1, :], b1[:, 0:MEM])
                elif kind == "q_mem":
                    ins = v.tensor_copy(q_mem[:, 2 * (u - 4) + 1, :], b1[:, :])
                elif kind in ("kc", "vc"):
                    for g in range(2):
                        rows_ = b1[DH * g:DH * (g + 1), :]
                        link(v.tensor_copy(kv_c[u - 6][0:DH, 2 + g, :], rows_))
                        ins = v.tensor_copy(kv_c[u - 6][DH:P, 2 + g, 0:T - 16], rows_[:, 16:T])
                elif kind in ("ks", "kw"):
                    ins = v.tensor_copy(k_stage[u - 8][:, 1, :], b1[:, :])
                elif kind in ("vs", "vw"):
                    ins = v.tensor_copy(v_sw[u - 10][:, 2:4, :], v1)
                elif kind == "qk":
                    ins = v.tensor_copy(qk_in[:, 2 * (u - 14) + 1, 3:3 + T], b1[:, :])
                else:
                    h0 = 2 * (u - 18)
                    link(v.tensor_copy(v_ml[:, 2, h0:h0 + 2, 0:P], v1[:, 0, :].rearrange("p (h d) -> p h d", d=P)))
                    ins = v.tensor_copy(v_ml[:, 3, h0:h0 + 2, 0:P], v1[:, 1, :].rearrange("p (h d) -> p h d", d=P))
                mark(ins, evac_dve, DVE_EVACS[u + 1])
                if kind == "qk":
                    dve.wait_ge(evac_act, u + 1)
                    for j in range(2 * (u - 14), 2 * (u - 14) + 2):
                        acc = conv_acc[j % 2][:, :]
                        if j >= 2:
                            dve.wait_ge(qk_ready, j - 1)
                        link(v.tensor_scalar(acc, qk_in[:, j, 0:T], col("ml_conv_w", j, 0), col("ml_conv_b", j), ALU.mult, ALU.add))
                        for k in range(1, 4):
                            ins = v.scalar_tensor_tensor(acc, qk_in[:, j, k:k + T], col("ml_conv_w", j, k), acc, ALU.mult, ALU.add)
                            if k < 3:
                                link(ins)
                        ins.then_inc(conv_done, 1)

            def mem_scores(h):
                dve.wait_ge(mem_s, h + 1)
                for b in range(2):
                    link(v.reduce_max(stat[:, 32 + 2 * b:34 + 2 * b], bank[4 + b][:, :].rearrange("p (q m) -> p q m", m=MEM), AX_X))
                v.tensor_scalar(stat[:, 32:36], stat[:, 32:36], -(P ** -0.5), None, ALU.mult).then_inc(mem_m, 1)
                dve.wait_ge(mem_e, h + 1)
                link(v.reciprocal(stat[:, 36:40], stat[:, 36:40]))
                for qb in range(TT):
                    ins = v.tensor_scalar(p_mem[:, qb, :], p_mem[:, qb, :], stat[:, 36 + qb:37 + qb], None, ALU.mult)
                mark(ins, mem_p, h + 1)

            def mem_turn(h):
                dve.wait_ge(mem_t, h + 1)
                v.tensor_copy(pt_mem[:, 1, :], bank[7][:, :]).then_inc(mem_td, 1)

            def mem_out(h):
                dve.wait_ge(mem_yh, h + 1)
                v.tensor_tensor(ymem[1][:, h, :], bank[4][:, :], ymem[0][:, h, :].bitcast(F32), ALU.subtract).then_inc(mem_y, 1)

            def cmp_place(b):
                dve.wait_ge(evac_act, 7 + b)
                blocks = kv_c[b][:, :, 0:T - 16].rearrange("p g (n r) -> p g n r", r=16)
                pos = pe_cols[b].unsqueeze(1).unsqueeze(1).to_broadcast([P, GROUPS, NC, 16])
                v.tensor_tensor(blocks, blocks, pos, ALU.add).then_inc(cmp_ab, 1)

            def cmp_out(b):
                dve.wait_ge(cmp_o, b + 1)
                if b == 0:
                    ins = v.tensor_copy(kcmp[:, :, :].rearrange("p g n -> p (g n)"), bank[6][:, 0:4 * NC])
                else:
                    ins = v.tensor_copy(vcmp[0:NC, :, :].rearrange("p g d -> p (g d)"), bank[6][0:NC, 0:GROUPS * DH])
                ins.then_inc(cmp_e, 1)

            def ml_rows(_):
                link(v.memset(ones4[:, :], 1.0))
                dve.wait_ge(evac_act, 14)
                link(v.tensor_scalar(row4[2][:, :], if_row[1][:, :], -1.0, None, ALU.mult))
                v.tensor_tensor(row4[2][:, :], if_row[1][:, :], row4[2][:, :], ALU.min).then_inc(f_min, 1)
                dve.wait_ge(f_log, 1)
                link(v.scalar_tensor_tensor(row4[1][:, :], if_row[1][:, :], 0.0, row4[2][:, :], ALU.min, ALU.subtract))
                link(v.tensor_tensor_scan(row4[3][:, :], ones4[:, :], row4[1][:, :], 0.0, ALU.mult, ALU.add))
                link(v.tensor_tensor(row4[0][:, :], if_row[0][:, :], row4[3][:, :], ALU.subtract))
                link(v.tensor_tensor_scan(row4[4][:, :], row4[0][:, :], row4[0][:, :], 0.0, ALU.max, ALU.max))
                link(v.tensor_scalar(row4[5][:, :], row4[4][:, :], -1.0, None, ALU.mult))
                mark(v.tensor_tensor(row4[2][:, :], row4[3][:, :], row4[4][:, :], ALU.add), g_rows, 1)

            def ml_cols(_):
                dve.wait_ge(emt_ready, 1)
                mark(v.tensor_copy(g_col, bank[7][:, 0:16]), g_cols, 1)

            def ml_scores(h):
                dve.wait_ge(bc_ready, h + 1)
                if h == 0:
                    dve.wait_ge(k_stored, 32)
                else:
                    dve.wait_ge(mo_ready, h)

                def argument(sb):
                    n = TT * h + sb
                    v.tensor_scalar(d_ml[n % 2][:, 0:T - P * sb], bank[4][:, P * sb:T], g_col[:, 4 * sb + h:4 * sb + h + 1], 0.0,
                                    ALU.add, ALU.min).then_inc(d_arg, 1)

                argument(0)
                for sb in range(TT):
                    n = TT * h + sb
                    if sb + 1 < TT:
                        argument(sb + 1)
                    dve.wait_ge(d_exp, n + 1)
                    dve.wait_ge(sT_ready, n + 1)
                    link(v.scalar_tensor_tensor(s_ml[:, sb, P * sb:T], bank[5 + n % 2][:, 0:T - P * sb], P ** -0.5,
                                                d_ml[n % 2][:, 0:T - P * sb], ALU.mult, ALU.mult))
                    diag = s_ml[:, sb, P * sb:P * (sb + 1)]
                    mark(v.tensor_tensor(diag, diag, tri, ALU.mult), s_masked, n + 1)

            def ml_out(h):
                dve.wait_ge(mo_ready, h + 1)
                if h > 0:
                    dve.wait_ge(m_h, h)
                for b in range(2):
                    link(v.tensor_copy(den2[:, 2 * b:2 * b + 2], bank[7 - 3 * b][:, P:2 * P + 2:P + 1]))
                link(v.scalar_tensor_tensor(den, den2, -1.0, den2, ALU.mult, ALU.max))
                link(v.tensor_tensor(den, den, emt[:, h:16:4], ALU.max))
                mark(v.reciprocal(den, den), m_rec, h + 1)

            def ml_gain(half):
                dve.wait_ge(evac_act, 21 + half)
                c = slice(2 * P * half, 2 * P * (half + 1))
                link(v.tensor_tensor(o_ml[:, :, c], o_ml[:, :, c], head_g[:, c].unsqueeze(1).to_broadcast([P, TT, 2 * P]), ALU.mult))

            def ml_norm(half):
                rr = rr_ml.rearrange("p (t h) -> p t h", h=4)[:, :, 2 * half:2 * half + 2]
                dve.wait_ge(m_root, half + 1)
                link(v.reciprocal(rr, rr))
                for h in (2 * half, 2 * half + 1):
                    for tb in range(TT):
                        y = h_mlt[:, tb, P * h:P * (h + 1)]
                        v.scalar_tensor_tensor(y, y, rr_ml[:, 4 * tb + h:4 * tb + h + 1], o_ml[:, tb, P * h:P * (h + 1)],
                                               ALU.mult, ALU.mult).then_inc(m_y, 1)

            def ml_turn(_):
                for h in range(4):
                    dve.wait_ge(m_hi_s, h + 1)
                    mark(v.tensor_tensor(yml[1][:, h, :], bank[h][:, :], yml[0][:, h, :].bitcast(F32), ALU.subtract), m_lo_s, h + 1)

            steps = {"unit": unit, "mem_scores": mem_scores, "mem_turn": mem_turn, "mem_out": mem_out, "cmp_place": cmp_place,
                     "cmp_out": cmp_out, "ml_rows": ml_rows, "ml_cols": ml_cols, "ml_scores": ml_scores, "ml_out": ml_out,
                     "ml_norm": ml_norm, "ml_gain": ml_gain,
                     "ml_turn": ml_turn}
            for what, n in SCHEDULE:
                if what in steps:
                    steps[what](n)

            dve.wait_ge(mask_in_place, 16)
            dve.sem_inc(y_split, 2)
            gate4 = gate[:, :, :].rearrange("p q (h b) -> p q h b", b=3)
            pc3 = p_c[:, :, :, :].rearrange("p q h n -> p (q h) n")
            with dve.Fori(0, GROUPS) as g:
                chain.enter(g, 0, NSA_PER)
                dve.wait_ge(w_used, g * 4 + (U_NSA + 1))
                link(v.tensor_scalar(kc_g, kcmp[:, bass.ds(g, 1), :].rearrange("p a n -> p (a n)"), 1.0, None, ALU.mult))
                v.tensor_scalar(qT[:, 1, :], bank[1][:, :], 1.0, None, ALU.mult).then_inc(q_dve, 1)
                dve.wait_ge(c_s, g + 1)
                for half in range(2):
                    link(v.tensor_tensor(p_c[:, :, half:HPG:2, :], bank[half][:, 0:8 * NC].rearrange("p (q h n) -> p q h n", h=2, n=NC),
                                         cneg.rearrange("p (q n) -> p q n", n=NC).unsqueeze(2).to_broadcast([P, TT, 2, NC]), ALU.add))
                link(v.reduce_max(cmax, pc3, AX_X))
                v.tensor_tensor(pc3, pc3, cmax.unsqueeze(2).to_broadcast([P, 16, NC]), ALU.subtract).then_inc(c_sh, 1)
                dve.wait_ge(c_e, g + 1)
                link(v.reduce_sum(csum, pc3, AX_X))
                v.tensor_tensor(p_c[:, :, :, :], p_c[:, :, :, :],
                                c01.rearrange("p (q n) -> p q n", n=NC).unsqueeze(2).to_broadcast([P, TT, HPG, NC]),
                                ALU.mult).then_inc(c_p, 1)
                link(v.reciprocal(crec, csum))
                link(v.tensor_tensor(cg_c.rearrange("p (q h) -> p q h", h=HPG), crec.rearrange("p (q h) -> p q h", h=HPG),
                                     gate4[:, :, bass.ds(g * HPG, HPG), 0], ALU.mult))

                def mask_step(i):
                    br, qb, hh = STEPS[i]
                    n = P * (qb + 1)
                    dve.wait_ge(s_s, g * NS + (i + 1))
                    if i >= 4:
                        dve.wait_ge(s_t, g * NS + (i - 3))
                    dve.sem_inc(s_open, 1)
                    v.tensor_tensor_reduce(prob[i % 4][:, 0:n], bank[S_BANK[i % len(S_BANK)]][:, 0:n], strip[:, T - n:T], -(DH ** -0.5), 1e38,
                                           ALU.add, ALU.min, nmax[:, i:i + 1]).then_inc(s_m, 1)

                def turn_step(i):
                    if i % 2 == 1:
                        br, qb, hh = STEPS[i]
                        n = P * (qb + 1)
                        dve.wait_ge(s_t, g * NS + (i + 1))
                        v.tensor_copy(probT[i % 4][:, 0:n], bank[5 + i % 2][:, 0:n]).then_inc(s_pd, 1)

                def out_step(k):
                    br, qb, _ = STEPS[HPG * k]
                    dve.wait_ge(s_o, g * NS + (HPG * k + HPG))
                    link(v.reciprocal(prec[:, HPG * k:HPG * (k + 1)], psum_row[:, HPG * k:HPG * (k + 1)]))
                    link(v.tensor_tensor(cg[:, HPG * k:HPG * (k + 1)], prec[:, HPG * k:HPG * (k + 1)],
                                         gate4[:, qb, bass.ds(g * HPG, HPG), br + 1], ALU.mult))
                    for hh in range(HPG):
                        y = y_tok[:, qb, DH * hh:DH * (hh + 1)]
                        o_ = bank[OUT_BANK[k % 2]][:, DH * hh:DH * (hh + 1)]
                        c = cg[:, HPG * k + hh:HPG * k + hh + 1]
                        if br == 0:
                            ins = v.tensor_scalar(y, o_, c, None, ALU.mult)
                        else:
                            ins = v.scalar_tensor_tensor(y, o_, c, y, ALU.mult, ALU.add)
                    ins.then_inc(s_or, 1)

                for i in range(NS + 5):
                    if i < NS:
                        mask_step(i)
                    if 2 <= i < NS + 2:
                        turn_step(i - 2)
                    if i >= 8 and i % HPG == 0:
                        out_step(i // HPG - 2)
                dve.wait_ge(s_or, g * (NS // HPG) + NS // HPG)
                dve.wait_ge(c_o, g + 1)
                for qb in range(TT):
                    for hh in range(HPG):
                        y = y_tok[:, qb, DH * hh:DH * (hh + 1)]
                        o_ = bank[CMP_OUT_BANK[qb // 2]][:, 256 * (qb % 2) + DH * hh:256 * (qb % 2) + DH * (hh + 1)]
                        ins = v.scalar_tensor_tensor(y, o_, cg_c[:, HPG * qb + hh:HPG * qb + hh + 1], y, ALU.mult, ALU.add)
                ins.then_inc(y_done, 1)
                for t in range(2):
                    dve.wait_ge(y_turned, g * 2 + (t + 1))
                    yh = ynsa[0][:, bass.ds(g * 2 + t, 1), :].rearrange("p a n -> p (a n)")
                    yl = ynsa[1][:, bass.ds(g * 2 + t, 1), :].rearrange("p a n -> p (a n)")
                    link(v.tensor_scalar(yh, bank[6 + t][:, :], 1.0, None, ALU.mult))
                    v.tensor_tensor(yl, bank[6 + t][:, :], yh.bitcast(F32), ALU.subtract).then_inc(y_split, 1)
            chain.leave(GROUPS)

            def merge(c):
                for b in range(3):
                    dve.wait_ge(w_used, c * 2 + (U_MERGE + 1 + (b > 0)))
                    dve.wait_ge(mg_gate, c * 3 + (b + 1))
                    for t in range(2):
                        if b == 0:
                            v.tensor_tensor(ma[t][:, :], mg[0][:, t, :], bank[t][:, :], ALU.mult).then_inc(mg_used, 1)
                        else:
                            link(v.tensor_tensor(mg[b][:, t, :], mg[b][:, t, :], bank[2 * b + t][:, :], ALU.mult))
                            v.tensor_tensor(ma[t][:, :], ma[t][:, :], mg[b][:, t, :], ALU.add).then_inc(mg_used, 1)
                dve.wait_ge(mg_used, c * 6 + 6)
                for t in range(2):
                    yh = ym[0][:, bass.ds(c * 2 + t, 1), :].rearrange("p a n -> p (a n)")
                    yl = ym[1][:, bass.ds(c * 2 + t, 1), :].rearrange("p a n -> p (a n)")
                    link(v.tensor_scalar(yh, ma[t][:, :], 1.0, None, ALU.mult))
                    mark(v.tensor_tensor(yl, ma[t][:, :], yh.bitcast(F32), ALU.subtract), mg_split, c * 2 + (t + 1))

            merge(0)
            with dve.Fori(1, 4) as c:
                chain.enter(c, 1, 6)
                merge(c)
            chain.leave(3)

            def square(src, k):
                if k >= 2:
                    dve.wait_ge(sq_added, 9 * ((k - 2) // 8) + (k - 2) % 8 + 2)
                v.tensor_tensor(sq[k % 2][:, :], src, src, ALU.mult).then_inc(sq_ready, 1)

            def low_of(src, gain, j, hi_first, s, n):
                dve.wait_ge(h_hi_s, hi_first + j + 1)
                mark(v.scalar_tensor_tensor(h_lo[:, j, :], src, gain, h_hi[:, j, :].bitcast(F32), ALU.mult, ALU.subtract), s, n)

            def split(src, gain, j, s, n):
                link(v.tensor_scalar(h_hi[:, j, :], src, gain, None, ALU.mult))
                mark(v.scalar_tensor_tensor(h_lo[:, j, :], src, gain, h_hi[:, j, :].bitcast(F32), ALU.mult, ALU.subtract), s, n)

            def reciprocal_root(n):
                dve.wait_ge(root, n)
                mark(v.reciprocal(rb[:, :], rb[:, :]), rstd, n)

            def post_norm(name, x_first, r, hi_first, gain_row, event):
                reciprocal_root(r)
                for j in range(KT + 1):
                    if j < KT:
                        link(v.scalar_tensor_tensor(O[:, j, :], O[:, j, :], col(name, j), rb[:, :], ALU.mult, ALU.mult))
                        if x_first:
                            dve.wait_ge(x_turned, TURN_ORDER.index(j) + 1)
                            b = TURN_BANK[j]
                            mark(v.tensor_tensor(X[:, j, :], O[:, j, :], bank[b][:, :], ALU.add), x_new, j + 1)
                        else:
                            mark(v.tensor_tensor(X[:, j, :], O[:, j, :], X[:, j, :], ALU.add), x_new, KT + j + 1)
                    if j >= 1:
                        low_of(X[:, j - 1, :], gain_row(j - 1), j - 1, hi_first, h_ready, KT * event + j)

            for n in range(4):
                dve.wait_ge(w_used, U_WOUT + n + 1)
                for t in range(2):
                    j = 2 * n + t
                    mark(v.tensor_copy(O[:, j, :], bank[2 * (n % 2) + t][:, :]), o_ready, j + 1)
                    square(O[:, j, :], j)
            post_norm("g_post_mix", True, 1, HI_POST_MIX, lambda j: col("g_pre_ffn", j), 0)

            for f in range(5):
                def up(i):
                    u = i * 2 + U_FFN[f]
                    n = i * 2 + 2 * UP_STEPS * f
                    dve.wait_ge(w_used, u + 1)
                    for t in range(2):
                        v.tensor_tensor(tg[t][:, :], bank[t][:, :], rb[:, :], ALU.mult).then_inc(g_scaled, 1)
                    for t in range(2):
                        dve.wait_ge(silu_done, n + (t + 1))
                        link(v.tensor_tensor(tg[t][:, :], tg[t][:, :], rb[:, :], ALU.mult))
                    dve.wait_ge(w_used, u + 2)
                    for t in range(2):
                        mark(v.tensor_tensor(tg[t][:, :], tg[t][:, :], bank[2 + t][:, :], ALU.mult), up_read, n + (t + 1))
                        hh = hid[0][:, bass.ds(i * 2 + t, 1), :].rearrange("p a n -> p (a n)")
                        hl = hid[1][:, bass.ds(i * 2 + t, 1), :].rearrange("p a n -> p (a n)")
                        link(v.tensor_scalar(hh, tg[t][:, :], 1.0, None, ALU.mult))
                        mark(v.tensor_tensor(hl, tg[t][:, :], hh.bitcast(F32), ALU.subtract), hid_ready, n + (t + 1))

                reciprocal_root(R_EVENT[f])
                up(0)
                with dve.Fori(1, UP_STEPS) as i:
                    chain.enter(i, 1, 4)
                    up(i)
                chain.leave(UP_STEPS - 1)
                kind, gain = NEXT[f]
                for c in range(4):
                    dve.wait_ge(w_used, U_FFN[f] + 2 * UP_STEPS + 3 * c + 3)
                    for t in range(2):
                        j = 2 * c + t
                        src = bank[4 + 2 * (c % 2) + t][:, :]
                        n = 8 + 8 * f + j + 1
                        if kind == "post":
                            mark(v.tensor_copy(O[:, j, :], src), o_ready, n)
                            square(O[:, j, :], SQ_BASE[f] + j)
                        else:
                            mark(v.scalar_tensor_tensor(X[:, j, :], src, 0.5, X[:, j, :], ALU.mult, ALU.add), o_ready, n)
                            if kind == "half":
                                square(X[:, j, :], SQ_BASE[f] + j)
                            if gain is not None:
                                split(X[:, j, :], col(gain[0], j, gain[1]), j, h_ready, KT * H_EVENT[f + 1] + j + 1)
                if f == 0:
                    post_norm("g_post_ffn", False, 3, HI_POST_FFN, lambda j: col("norm_g_2", j, 0), 1)
                if f == 1:
                    link(v.memset(hp[:, :, 0:POOL_PAD], 0.0))
                    link(v.memset(hp[:, :, POOL_PAD + T:W_HP], 0.0))
                    reciprocal_root(5)
                    for j in range(KT + 2):
                        if j < KT:
                            gi = j // 2
                            mid = hp[:, j, POOL_PAD:POOL_PAD + T]
                            link(v.scalar_tensor_tensor(mid, X[:, j, :], col("norm_g_2", j, 1), rb[:, :], ALU.mult, ALU.mult))
                            cur = hp[:, j, :]
                            for m in range(gi + 1):
                                n = W_HP - ((2 << m) - 1)
                                dst = (pool_w[j % 2] if m == gi else pool_s[m % 2])[:, :]
                                ins = v.tensor_tensor(dst[:, 0:n], cur[:, 0:n], cur[:, (1 << m):(1 << m) + n], ALU.add)
                                if m < gi:
                                    link(ins)
                                cur = dst
                            mark(ins, pool_win, j + 1)
                        if 1 <= j < KT + 1:
                            tmp = tg[(j - 1) % 2][:, :]
                            dve.wait_ge(pool_mean, j)
                            mark(v.tensor_tensor(tmp, tmp, hp[:, j - 1, POOL_PAD:POOL_PAD + T], ALU.subtract), pool_diff, j)
                        if j >= 2:
                            low_of(tg[j % 2][:, :], 1.0, j - 2, HI_POOLED, pooled, j - 1)
                    for n in range(2):
                        dve.wait_ge(w_used, U_POOL + n + 1)
                        for q in range(4):
                            j = 4 * n + q
                            tmp = tg[j % 2][:, :]
                            link(v.tensor_scalar(tmp, bank[4 * n + q][:, :], col("pool_b_2", j), col("pool_scale_2", j),
                                                 ALU.add, ALU.mult))
                            mark(v.tensor_tensor(X[:, j, :], tmp, X[:, j, :], ALU.add), x_new, 16 + j + 1)
                            if n == 1:
                                low_of(X[:, q, :], col("norm_g_2", q, 2), q, HI_POOL_OUT, h_ready, KT * 2 + q + 1)
                    for j in range(4, KT):
                        low_of(X[:, j, :], col("norm_g_2", j, 2), j, HI_POOL_OUT, h_ready, KT * 2 + j + 1)
                if f == 3:
                    link(v.memset(hc[:, :, 0:PAD], 0.0))
                    link(v.memset(hc[:, :, PAD + T:W_HC], 0.0))
                    reciprocal_root(8)
                    for j in range(KT + 1):
                        if j < KT:
                            mark(v.scalar_tensor_tensor(tg[j % 2][:, :], X[:, j, :], col("norm_g_2", j, 4), rb[:, :], ALU.mult,
                                                        ALU.mult), conv_in, j + 1)
                        if j >= 1:
                            low_of(tg[(j - 1) % 2][:, :], 1.0, j - 1, HI_CONV_IN, h_ready, KT * 4 + j)
                    for n in range(4):
                        dve.wait_ge(w_used, U_PW1 + 2 * n + 2)
                        for t in range(2):
                            j = 2 * n + t
                            dve.wait_ge(glu_arg, j + 1)
                            mark(v.scalar_tensor_tensor(hc[:, j, PAD:PAD + T], bank[2 + t][:, :], col("conv_b_pw1_2", j, 0),
                                                        tg[t][:, :], ALU.add, ALU.mult), glu, j + 1)
                        for k in range(TAPS - PE_TAPS[n]):
                            for t in range(2):
                                j = 2 * n + t
                                w = col("conv_w_dw_2", j, k)
                                src = hc[:, j, k:k + T]
                                if k == 0:
                                    ins = v.tensor_scalar(cacc[t][:, :], src, w, None, ALU.mult)
                                else:
                                    ins = v.scalar_tensor_tensor(cacc[t][:, :], src, w, cacc[t][:, :], ALU.mult, ALU.add)
                                chain.step(ins)
                                dve.wait_ge(chain.sem, chain.n - 1)
                        dve.wait_ge(chain.sem, chain.n)
                        for t in range(2):
                            j = 2 * n + t
                            dve.wait_ge(taps_made, j + 1)
                            v.scalar_tensor_tensor(hy[:, j, :], bank[4 + 2 * (n % 2) + t][:, :], col("conv_b_dw_2", j), cacc[t][:, :],
                                                   ALU.add, ALU.add).then_inc(conv_y, 1)
                        dve.wait_ge(conv_y, 2 * n + 2)
                    dve.wait_ge(mean_s, 1)
                    link(v.tensor_scalar(mu[:, :], bank[0][:, :], 1.0 / D, None, ALU.mult))
                    for j in range(KT):
                        mark(v.tensor_tensor(hy[:, j, :], hy[:, j, :], mu[:, :], ALU.subtract), ln_x, j + 1)
                    reciprocal_root(9)
                    for j in range(KT + 2):
                        if j < KT:
                            if j == 0:
                                dve.wait_ge(ln_sq, KT)
                            v.scalar_tensor_tensor(hy[:, j, :], hy[:, j, :], col("conv_ln_g_2", j), rb[:, :], ALU.mult,
                                                   ALU.mult).then_inc(ln_z, 1)
                        if j >= 2:
                            low_of(hy[:, j - 2, :], 1.0, j - 2, HI_LN, ln_h, j - 1)
                    for n in range(4):
                        dve.wait_ge(w_used, U_PW2 + n + 1)
                        for t in range(2):
                            j = 2 * n + t
                            mark(v.scalar_tensor_tensor(X[:, j, :], bank[4 + 2 * (n % 2) + t][:, :], col("conv_b_pw2_2", j),
                                                        X[:, j, :], ALU.add, ALU.add), x_new, 24 + j + 1)
                    for j in range(KT):
                        low_of(X[:, j, :], col("norm_g_2", j, 5), j, HI_CONV_OUT, h_ready, KT * 5 + j + 1)

            dve.wait_ge(fin_sq, 1)
            pairs = stat[:, 32:40].rearrange("p (t b) -> p t b", b=2)
            v.tensor_tensor(stat[:, 40:44], pairs[:, :, 0], pairs[:, :, 1], ALU.add).then_inc(fin_sum, 1)
            dve.wait_ge(fin_root, 1)
            link(v.reciprocal(stat[:, 44:48], stat[:, 44:48]))
            dve.wait_ge(fg_landed, 16)
            for t in range(TT):
                for b in range(2):
                    ins = v.scalar_tensor_tensor(o_tok[:, t, T * b:T * (b + 1)], bank[2 * t + b][:, :], stat[:, 44 + t:45 + t],
                                                 fg[:, T * b:T * (b + 1)], ALU.mult, ALU.mult)
                    if b == 0:
                        link(ins)
                ins.then_inc(fin_y, 1)


_SKIP = ("x", "mem")


def kernel(**inputs):
    import concourse.bacc as _bacc
    from concourse.bass_utils import run_bass_kernel_spmd as _run

    nc = _bacc.Bacc("TRN2", target_bir_lowering=False, num_devices=1)
    arrays, aps = {}, {}
    table, inv_count = constants()
    for name, value in list(layout(inputs).items()) + [("const_table", table), ("const_inv_count", inv_count)]:
        a = np.ascontiguousarray(value)
        arrays[f"in_{name}_dram"] = a
        aps[name] = nc.dram_tensor(f"in_{name}_dram", a.shape, mybir.dt.from_np(a.dtype), kind="ExternalInput").ap()
    out = nc.dram_tensor("out_0_dram", (1, T, D), F32, kind="ExternalOutput").ap()
    build(nc, aps, aps["const_table"], aps["const_inv_count"], out)
    r = _run(nc, [arrays], core_ids=[0])
    return r.results[0]["out_0_dram"]
```
